# Optimizing a Trainium2 kernel written in Bass

```python
import jax, jax.numpy as jnp
from jax import lax
import numpy as np

D_MODEL = 1024
BATCH = 1
SEQ = 1024
DEPTH = 1

N_HEADS = 8
HEAD_DIM = 64
N_KV_HEADS = 2
GROUP = N_HEADS // N_KV_HEADS
ATTN_WIDTH = N_HEADS * HEAD_DIM
KV_WIDTH = 2 * N_KV_HEADS * HEAD_DIM
N_NSA_BRANCHES = 3
CMP_BLOCK = 32
CMP_STRIDE = 16
CMP_HIDDEN = 64
SEL_BLOCK = 64
SEL_TOP_N = 16
WINDOW = 512
Q_BLOCK = 128
POOL_GROUPS = 4
POOL_GROUP_DIM = 128
POOL_WIDTH = POOL_GROUPS * POOL_GROUP_DIM
POOL_WINDOWS = (2, 4, 8, 16)
N_MIXERS = 2
D_FF = 4 * D_MODEL
IN_WIDTH = ATTN_WIDTH + N_NSA_BRANCHES * KV_WIDTH + N_NSA_BRANCHES * N_HEADS + POOL_WIDTH + N_MIXERS * D_MODEL
EPS = 1e-6
NEG = -1e30
FORCE = 1e6

kernel_name = "nsa_pool_gated_hybrid"

def rmsnorm(x, g):
    xf = x.astype(jnp.float32)
    y = xf * lax.rsqrt(jnp.mean(xf * xf, axis=-1, keepdims=True) + EPS)
    return (y * g.astype(jnp.float32)).astype(x.dtype)

def alibi_slopes():
    s = np.array([2.0 ** (-8.0 * (h + 1) / N_HEADS) for h in range(N_HEADS)], dtype=np.float32)
    return jnp.asarray(s.reshape(N_KV_HEADS, GROUP))

def compress_kv(kv, pe, w1, w2):
    S = kv.shape[1]
    n_cmp = (S - CMP_BLOCK) // CMP_STRIDE + 1
    idx = jnp.arange(n_cmp)[:, None] * CMP_STRIDE + jnp.arange(CMP_BLOCK)[None, :]
    blocks = kv[:, idx] + pe[None, None, :, None, :]
    h = jax.nn.gelu(jnp.einsum('bclgd,ldh->bcgh', blocks, w1))
    return jnp.einsum('bcgh,he->bcge', h, w2)

def nsa_attention(q, k_cmp, v_cmp, k_slc, v_slc, k_win, v_win, gates):
    B, S = q.shape[0], q.shape[1]
    nb = S // Q_BLOCK
    n_sel = S // SEL_BLOCK
    top_n = min(SEL_TOP_N, n_sel)
    n_cmp = k_cmp.shape[1]
    slopes = alibi_slopes()
    scale = HEAD_DIM ** -0.5

    cmp_start = jnp.arange(n_cmp) * CMP_STRIDE
    cmp_end = cmp_start + CMP_BLOCK - 1
    sel_start = jnp.arange(n_sel) * SEL_BLOCK
    sel_end = sel_start + SEL_BLOCK - 1
    overlap = ((cmp_start[:, None] <= sel_end[None, :]) &
               (cmp_end[:, None] >= sel_start[None, :])).astype(jnp.float32)

    k_blocks = k_slc.reshape(B, n_sel, SEL_BLOCK, N_KV_HEADS, HEAD_DIM).transpose(0, 3, 1, 2, 4)
    v_blocks = v_slc.reshape(B, n_sel, SEL_BLOCK, N_KV_HEADS, HEAD_DIM).transpose(0, 3, 1, 2, 4)
    k_pad = jnp.pad(k_win, ((0, 0), (WINDOW, 0), (0, 0), (0, 0)))
    v_pad = jnp.pad(v_win, ((0, 0), (WINDOW, 0), (0, 0), (0, 0)))
    bi = jnp.arange(B)[:, None, None, None]
    gi = jnp.arange(N_KV_HEADS)[None, :, None, None]
    j = jnp.arange(n_sel)

    q_blocks = q.reshape(B, nb, Q_BLOCK, N_KV_HEADS, GROUP, HEAD_DIM).transpose(1, 0, 2, 3, 4, 5)
    g_blocks = gates.reshape(B, nb, Q_BLOCK, N_KV_HEADS, GROUP, N_NSA_BRANCHES).transpose(1, 0, 2, 3, 4, 5)

    def one_block(args):
        i, q_blk, g_blk = args
        q0 = i * Q_BLOCK
        t = q0 + jnp.arange(Q_BLOCK)
        qs = q_blk * scale

        dist_c = (t[:, None] - cmp_end[None, :]).astype(jnp.float32)
        mask_c = dist_c >= 0
        s_c = jnp.einsum('bqgrd,bcgd->bgrqc', qs, k_cmp).astype(jnp.float32)
        s_c = s_c - slopes[None, :, :, None, None] * dist_c
        p_c = jax.nn.softmax(jnp.where(mask_c, s_c, NEG), axis=-1) * mask_c
        o_c = jnp.einsum('bgrqc,bcgd->bqgrd', p_c.astype(v_cmp.dtype), v_cmp)

        imp = jnp.einsum('bgrqc,cj->bgqj', p_c, overlap)
        cur = t // SEL_BLOCK
        future = j[None, :] > cur[:, None]
        forced = (j[None, :] == 0) | (j[None, :] == cur[:, None]) | (j[None, :] == cur[:, None] - 1)
        imp = jnp.where(future, NEG, jnp.where(forced, FORCE, imp))
        top_val, top_idx = lax.top_k(imp, top_n)
        valid = top_val > NEG / 2
        k_g = k_blocks[bi, gi, top_idx]
        v_g = v_blocks[bi, gi, top_idx]
        pos_s = top_idx[..., None] * SEL_BLOCK + jnp.arange(SEL_BLOCK)
        dist_s = (t[None, None, :, None, None] - pos_s).astype(jnp.float32)
        mask_s = valid[..., None] & (dist_s >= 0)
        s_s = jnp.einsum('bqgrd,bgqnld->bgrqnl', qs, k_g).astype(jnp.float32)
        s_s = s_s - slopes[None, :, :, None, None, None] * dist_s[:, :, None]
        s_s = jnp.where(mask_s[:, :, None], s_s, NEG).reshape(B, N_KV_HEADS, GROUP, Q_BLOCK, top_n * SEL_BLOCK)
        p_s = jax.nn.softmax(s_s, axis=-1).reshape(B, N_KV_HEADS, GROUP, Q_BLOCK, top_n, SEL_BLOCK)
        o_s = jnp.einsum('bgrqnl,bgqnld->bqgrd', p_s.astype(v_g.dtype), v_g)

        k_w = lax.dynamic_slice_in_dim(k_pad, q0, WINDOW + Q_BLOCK, axis=1)
        v_w = lax.dynamic_slice_in_dim(v_pad, q0, WINDOW + Q_BLOCK, axis=1)
        pos_w = q0 - WINDOW + jnp.arange(WINDOW + Q_BLOCK)
        dist_wi = t[:, None] - pos_w[None, :]
        mask_w = (dist_wi >= 0) & (dist_wi < WINDOW) & (pos_w >= 0)[None, :]
        s_w = jnp.einsum('bqgrd,bkgd->bgrqk', qs, k_w).astype(jnp.float32)
        s_w = s_w - slopes[None, :, :, None, None] * dist_wi.astype(jnp.float32)
        p_w = jax.nn.softmax(jnp.where(mask_w, s_w, NEG), axis=-1)
        o_w = jnp.einsum('bgrqk,bkgd->bqgrd', p_w.astype(v_w.dtype), v_w)

        o = g_blk[..., 0:1] * o_c + g_blk[..., 1:2] * o_s + g_blk[..., 2:3] * o_w
        return o.reshape(B, Q_BLOCK, ATTN_WIDTH)

    out = lax.map(one_block, (jnp.arange(nb), q_blocks, g_blocks))
    return out.transpose(1, 0, 2, 3).reshape(B, S, ATTN_WIDTH)

def pool_mixer(u, w_pool, pool_scale):
    B, S, _ = u.shape
    uf = u.astype(jnp.float32)
    c = jnp.pad(jnp.cumsum(uf, axis=1), ((0, 0), (1, 0), (0, 0)))
    t = jnp.arange(S)
    outs = []
    for gidx, w in enumerate(POOL_WINDOWS):
        sl = slice(gidx * POOL_GROUP_DIM, (gidx + 1) * POOL_GROUP_DIM)
        lo = jnp.maximum(t + 1 - w, 0)
        cnt = (t + 1 - lo).astype(jnp.float32)
        mean = (c[:, 1:, sl] - c[:, lo, sl]) / cnt[None, :, None]
        outs.append(mean - uf[..., sl])
    p = jnp.stack(outs, axis=2).astype(u.dtype)
    y = jnp.einsum('bsgc,gcd->bsgd', p, w_pool).reshape(B, S, POOL_WIDTH)
    return y * pool_scale

def setup_inputs(seed: int = 0) -> dict:
    key = jax.random.key(seed)
    ks = jax.random.split(key, 16)

    def nrm(k, shape, fan_in):
        return jax.random.normal(k, shape, jnp.float32) * (fan_in ** -0.5)

    def gain(k, shape):
        return 1.0 + 0.02 * jax.random.normal(k, shape, jnp.float32)

    return {
        "x": jax.random.normal(ks[0], (BATCH, SEQ, D_MODEL), jnp.float32),
        "norm1_g": gain(ks[1], (DEPTH, D_MODEL)),
        "w_in": nrm(ks[2], (DEPTH, D_MODEL, IN_WIDTH), D_MODEL),
        "cmp_pe": 0.02 * jax.random.normal(ks[3], (DEPTH, 2, CMP_BLOCK, HEAD_DIM), jnp.float32),
        "cmp_w1": nrm(ks[4], (DEPTH, 2, CMP_BLOCK, HEAD_DIM, CMP_HIDDEN), CMP_BLOCK * HEAD_DIM),
        "cmp_w2": nrm(ks[5], (DEPTH, 2, CMP_HIDDEN, HEAD_DIM), CMP_HIDDEN),
        "w_attn_proj": nrm(ks[6], (DEPTH, ATTN_WIDTH, D_MODEL), ATTN_WIDTH),
        "w_pool": nrm(ks[7], (DEPTH, POOL_GROUPS, POOL_GROUP_DIM, POOL_GROUP_DIM), POOL_GROUP_DIM),
        "pool_scale": gain(ks[8], (DEPTH, POOL_WIDTH)),
        "w_pool_proj": nrm(ks[9], (DEPTH, POOL_WIDTH, D_MODEL), POOL_WIDTH),
        "w_out": nrm(ks[10], (DEPTH, D_MODEL, D_MODEL), D_MODEL),
        "norm2_g": gain(ks[11], (DEPTH, D_MODEL)),
        "w_ff1": nrm(ks[12], (DEPTH, D_MODEL, D_FF), D_MODEL),
        "w_ff2": nrm(ks[13], (DEPTH, D_FF, D_MODEL), D_FF),
        "final_g": gain(ks[14], (D_MODEL,)),
    }

def reference(x, norm1_g, w_in, cmp_pe, cmp_w1, cmp_w2, w_attn_proj, w_pool, pool_scale,
              w_pool_proj, w_out, norm2_g, w_ff1, w_ff2, final_g):
    B, S, _ = x.shape
    hk = N_KV_HEADS * HEAD_DIM
    o_q = 0
    o_kv = o_q + ATTN_WIDTH
    o_gate = o_kv + N_NSA_BRANCHES * KV_WIDTH
    o_pool = o_gate + N_NSA_BRANCHES * N_HEADS
    o_merge = o_pool + POOL_WIDTH
    for l in range(DEPTH):
        h = rmsnorm(x, norm1_g[l])
        proj = h @ w_in[l]
        q = proj[..., o_q:o_kv].reshape(B, S, N_KV_HEADS, GROUP, HEAD_DIM)
        kvs = [proj[..., o_kv + bidx * KV_WIDTH: o_kv + (bidx + 1) * KV_WIDTH] for bidx in range(N_NSA_BRANCHES)]
        k_c = kvs[0][..., :hk].reshape(B, S, N_KV_HEADS, HEAD_DIM)
        v_c = kvs[0][..., hk:].reshape(B, S, N_KV_HEADS, HEAD_DIM)
        k_s = kvs[1][..., :hk].reshape(B, S, N_KV_HEADS, HEAD_DIM)
        v_s = kvs[1][..., hk:].reshape(B, S, N_KV_HEADS, HEAD_DIM)
        k_w = kvs[2][..., :hk].reshape(B, S, N_KV_HEADS, HEAD_DIM)
        v_w = kvs[2][..., hk:].reshape(B, S, N_KV_HEADS, HEAD_DIM)
        nsa_gates = jax.nn.sigmoid(proj[..., o_gate:o_pool]).reshape(B, S, N_KV_HEADS, GROUP, N_NSA_BRANCHES)
        u_pool = proj[..., o_pool:o_merge]
        merge = jax.nn.sigmoid(proj[..., o_merge:]).reshape(B, S, N_MIXERS, D_MODEL)

        k_cmp = compress_kv(k_c, cmp_pe[l, 0], cmp_w1[l, 0], cmp_w2[l, 0])
        v_cmp = compress_kv(v_c, cmp_pe[l, 1], cmp_w1[l, 1], cmp_w2[l, 1])
        a = nsa_attention(q, k_cmp, v_cmp, k_s, v_s, k_w, v_w, nsa_gates) @ w_attn_proj[l]
        b = pool_mixer(u_pool, w_pool[l], pool_scale[l]) @ w_pool_proj[l]
        x = x + (merge[..., 0, :] * a + merge[..., 1, :] * b) @ w_out[l]

        h = rmsnorm(x, norm2_g[l])
        x = x + jnp.square(jax.nn.relu(h @ w_ff1[l])) @ w_ff2[l]
    return rmsnorm(x, final_g)


_drawn_inputs = setup_inputs


def setup_inputs(seed=0):
    import zlib

    import numpy as np

    out = dict(_drawn_inputs(seed))
    spreads = {}
    factors = {'norm1_g': 4.742,
     'cmp_pe': 200.0,
     'pool_scale': 18.338,
     'norm2_g': 13.312,
     'final_g': 23.653}
    for name, (base, spread) in spreads.items():
        noise = np.random.default_rng([zlib.crc32(name.encode()), seed]).standard_normal(out[name].shape)
        drawn = base * np.exp(spread * noise) if base else spread * noise
        out[name] = __import__('jax').numpy.asarray(drawn.astype(out[name].dtype))
    for name, factor in factors.items():
        out[name] = (out[name] * factor).astype(out[name].dtype)
    return out
```

```python
import concourse.bass as bass
from concourse import mybir
from contextlib import ExitStack



def hybrid_trunk(nc, x, norm1_g, w_in, cmp_pe, cmp_w1, cmp_w2, w_attn_proj, w_pool, pool_scale,
                 w_pool_proj, w_out, norm2_g, w_ff1, w_ff2, final_g, out):
    f32 = mybir.dt.float32
    f32r = mybir.dt.float32r
    ALU = mybir.AluOpType
    ACT = mybir.ActivationFunctionType

    P = 128
    S, D = x.shape[1], x.shape[2]
    KT = D // P
    TT = S // P
    HALF = 512
    FF = w_ff1.shape[2]
    HEADS, HD, GROUPS = 8, 64, 2
    GR = HEADS // GROUPS
    WIN_TILES = 512 // P
    NCMP, CSTRIDE, CBLOCK = 63, 16, 32
    CP = 64
    NEG = -1e30
    EPS = 1e-6
    O_GATE = HEADS * HD + 3 * 2 * GROUPS * HD
    O_POOL = O_GATE + 3 * HEADS
    O_MERGE = O_POOL + 512
    NG = 3 * HEADS
    PAD = 16

    U_POOL, U_GATE, U_Q, U_KC, U_VC, U_KS, U_VS, U_KW, U_VW = 0, 4, 5, 9, 10, 11, 12, 13, 14
    N1 = 15
    N3 = N1
    N4 = N3 + 3 * KT
    N_Y, N_MISC = 8, 19
    GELU_C = 0.7978845608028654
    N5 = N4 + KT
    ROUNDS = FF // D

    w_in_u = w_in[0].rearrange("(k p) n -> p k n", p=P)
    w_ap_u = w_attn_proj[0].rearrange("(k p) n -> p k n", p=P)
    w_pp_u = w_pool_proj[0].rearrange("(k p) n -> p k n", p=P)
    w_out_u = w_out[0].rearrange("(k p) n -> p k n", p=P)
    w_ff1_u = w_ff1[0].rearrange("(k p) n -> p k n", p=P)
    w_ff2_u = w_ff2[0].rearrange("(k p) n -> p k n", p=P)

    ctx = ExitStack()
    with ctx:
        def sem(name):
            return ctx.enter_context(nc.semaphore(name))

        START = (nc.sbuf_base + 63) // 64 * 64
        END = nc.sbuf_usable_end
        cursor = [START]

        def size_of(shape):
            n = 4
            for d in shape[1:]:
                n *= d
            return (n + 31) // 32 * 32

        def place(name, shape, dt=f32):
            off = cursor[0]
            cursor[0] += size_of(shape)
            assert cursor[0] <= END, (name, cursor[0] - END)
            return nc.alloc_sbuf_tensor_at(name, shape, dt, offset=off)

        wraw = place("wraw", [P, 2, KT, P])
        whi = place("whi", [P, 2, KT, P], f32r)
        wlo = place("wlo", [P, 2, KT, P], f32r)
        ahi = place("ahi", [P, KT, S], f32r)
        alo = place("alo", [P, KT, S], f32r)
        ident = place("ident", [P, P])
        ones = place("ones", [P, P])
        grow = place("grow", [2 * KT + 4, P])
        gcol = place("gcol", [P, 2 * KT + 4])
        g1, g2, psc = gcol[:, 0:KT], gcol[:, KT:2 * KT], gcol[:, 2 * KT:]
        qscale = place("qscale", [P, N1])
        ssum = place("ssum", [P, TT])
        msq = place("msq", [P, TT])
        rms = place("rms", [P, TT])
        rstd = place("rstd", [P, TT])
        gate_t = place("gate_t", [P, TT * NG])
        gates = place("gates", [P, TT, HEADS, 3])
        cvalid = place("cvalid", [P, 1])
        mx = place("mx", [P, 2, GR, 3])
        nb = place("nb", [P, 2, GR, 3])
        esum = place("esum", [P, 2, GR, 3])
        rs = place("rs", [P, 2, GR, 3])
        ARENA = cursor[0]

        kS = place("kS", [P, GROUPS, S], f32r)
        kW = place("kW", [P, GROUPS, S], f32r)
        kC = place("kC", [P, GROUPS, CP], f32r)
        vS = place("vS", [P, TT, GROUPS, 2 * HD], f32r)
        vW = place("vW", [P, TT, GROUPS, 2 * HD], f32r)
        vC = place("vC", [CP, GROUPS, 2 * HD], f32r)
        T1 = place("T1", [P, S])
        TW = place("TW", [P, (WIN_TILES + 1) * P])
        TC = place("TC", [P, TT, CP])
        REGION = cursor[0]
        ORDER = [7, 0, 6, 1, 5, 2, 4, 3]
        ITER = [(g, i) for g in range(GROUPS) for i in ORDER]
        NIT = len(ITER)

        def n_slc(i):
            return (i + 1) * P

        def n_win(i):
            return min(i + 1, WIN_TILES + 1) * P

        def n_row(i):
            return n_slc(i) + n_win(i) + CP

        def blocks(i):
            return [("slc", kb) for kb in range(i + 1)] + \
                   [("win", kb) for kb in range(i + 1 - n_win(i) // P, i + 1)] + [("cmp", 0)]

        PB = [place("prob0", [P, GR, n_row(7)]), place("prob1", [P, GR, n_row(3)])]
        qraw = place("qraw", [P, 2, GR, P])
        qh = place("qh", [P, 2, GR, P], f32r)
        ql = place("ql", [P, 2, GR, P], f32r)
        pth = place("pth", [P, 2, GR * P], f32r)
        ptl = place("ptl", [P, 2, GR * P], f32r)
        otmp = place("otmp", [HD, GR * P])
        ostg = place("ostg", [HD, 2, GR * P])

        cursor[0] = REGION
        xt = place("xt", [P, TT, D])
        after_x = cursor[0]
        hraw = place("hraw", [P, 2, KT, P])
        sqj = place("sqj", [P, D])
        cursor[0] = REGION
        up = place("up", [P, 4, PAD + S])
        tA = place("tA", [P, PAD + S])
        tB = place("tB", [P, PAD + S])
        icnt = place("icnt", [P, 4, PAD])
        wp = place("wp", [P, 4, P])
        assert cursor[0] <= after_x
        cursor[0] = REGION
        ksd = place("ksd", [P, GROUPS, S])
        kwd = place("kwd", [P, GROUPS, S])
        cursor[0] = after_x
        stage = place("stage", [P, 2, S])
        ccd = place("ccd", [P, GROUPS, S])
        cw1 = place("cw1", [P, 2, CBLOCK // 2, HD])
        cw2 = place("cw2", [HD, 2, 2 * HD])
        pet = place("pet", [CBLOCK // 2, 2, 2 * HD])
        pe2 = place("pe2", [P, 2, CBLOCK // 2])
        cb = place("cb", [HD, 2])
        cu = place("cu", [HD, 2, P])
        cv = place("cv", [HD, P])
        cz = place("cz", [HD, P])
        chid = place("chid", [HD, 2, GROUPS, CP])
        kcs = place("kcs", [P, P])
        vsd = place("vsd", [P, S])
        vwd = place("vwd", [P, S])
        gtd = place("gtd", [NG, S])

        cursor[0] = ARENA
        cT = place("cT", [P, KT, S])
        C_END = cursor[0]
        yhi = place("yhi", [P, 4, S], f32r)
        ylo = place("ylo", [P, 4, S], f32r)
        ohi = place("ohi", [P, 4, S], f32r)
        olo = place("olo", [P, 4, S], f32r)
        m0 = place("m0", [P, S])
        m1 = place("m1", [P, S])
        mt = place("mt", [P, 2, HALF])
        cursor[0] = ARENA
        h2hi = place("h2hi", [P, KT, S], f32r)
        assert cursor[0] == C_END
        xT = place("xT", [P, KT, S])
        h2lo = place("h2lo", [P, KT, S], f32r)
        TAIL = cursor[0]
        xr = place("xr", [P, 2, D])
        sqt = place("sqt", [P, HALF])
        sqa = place("sqa", [P, S])
        cursor[0] = TAIL
        rel = place("rel", [P, 2, HALF])
        rsq = place("rsq", [P, 2, HALF])
        f2t = place("f2t", [P, 2, HALF])
        cursor[0] += size_of([P, HALF]) + size_of([P, S]) - size_of([P, 2, HALF])
        r2 = place("r2", [P, S])
        cursor[0] = ARENA
        gfb = place("gfb", [P, D])
        sqo = place("sqo", [P, D])
        ost = place("ost", [P, 2, D])

        psU = ctx.enter_context(nc.psum_tensor("psU", [P, 4, HALF], f32))
        psX = ctx.enter_context(nc.psum_tensor("psX", [P, 4, HALF], f32))
        psS0 = psU[:, 0:2, :].rearrange("p b n -> p (b n)")
        psS1 = psU[:, 2:4, :].rearrange("p b n -> p (b n)")

        proj = nc.dram_tensor("proj_scratch", [N1 * P, S], f32).ap()
        yscr = nc.dram_tensor("pool_scratch", [4 * P, S], f32).ap()
        oscr = nc.dram_tensor("attn_scratch", [HEADS * HD, S], f32).ap()

        x_in = [sem(f"x_in{t}") for t in range(TT)]
        const_in, gain_t, gain_ready = sem("const_in"), sem("gain_t"), sem("gain_ready")
        w_raw = [sem("w_raw0"), sem("w_raw1")]
        w_hi, w_lo = sem("w_hi"), sem("w_lo")
        u_done = sem("u_done")
        ev = [sem("ev0"), sem("ev1")]
        consts = sem("consts")
        chain_p, chain_v = sem("chain_p"), sem("chain_v")
        ss_ready, ms_ready, rms_ready, rstd_ready = sem("ss_ready"), sem("ms_ready"), sem("rms_ready"), sem("rstd_ready")
        xs_ready, xt_ready, hraw_ready, h_hi, h_lo = sem("xs_ready"), sem("xt_ready"), sem("hraw_ready"), sem("h_hi"), sem("h_lo")
        st_proj = [sem("st_proj0"), sem("st_proj1")]
        u_in, pool_w_in, pooled = sem("u_in"), sem("pool_w_in"), sem("pooled")
        st_y = [sem("st_y0"), sem("st_y1")]
        gate_in, vs_in, vw_in, ks_in, kw_in = sem("gate_in"), sem("vs_in"), sem("vw_in"), sem("ks_in"), sem("kw_in")
        cw_in, cc_in = sem("cw_in"), sem("cc_in")
        misc, misc_ev = sem("misc"), sem("misc_ev")
        k_hi, v_hi, gate_tanh = sem("k_hi"), sem("v_hi"), sem("gate_tanh")
        gelu_arg, gelu_tanh = sem("gelu_arg"), sem("gelu_tanh")
        k_ready = sem("k_ready")
        q_in = [sem("q_in0"), sem("q_in1")]
        q_hi, q_lo = sem("q_hi"), sem("q_lo")
        s_slc, s_win, m_slc, m_win = sem("s_slc"), sem("s_win"), sem("m_slc"), sem("m_win")
        nb_ready, exp_done, rs_ready, p_ready = sem("nb_ready"), sem("exp_done"), sem("rs_ready"), sem("p_ready")
        t_done, pt_hi, pt_lo, pv_done = sem("t_done"), sem("pt_hi"), sem("pt_lo"), sem("pv_done")
        o_half, o_ready = sem("o_half"), sem("o_ready")
        st_o = [sem("st_o0"), sem("st_o1")]
        yo_in, yo_hi, ab_free, z_ready = sem("yo_in"), sem("yo_hi"), sem("ab_free"), sem("z_ready")
        c_ready = sem("c_ready")
        xr_in = [sem("xr_in0"), sem("xr_in1")]
        xr_t, xT_a, xT_v, c_hi, c_lo = sem("xr_t"), sem("xT_a"), sem("xT_v"), sem("c_hi"), sem("c_lo")
        res = [sem("res0"), sem("res1")]
        relu = [sem("relu0"), sem("relu1")]
        h2_hi, h2_lo = sem("h2_hi"), sem("h2_lo")
        sq_sum, ms_done, r2_ready, mul_r2 = sem("sq_sum"), sem("ms_done"), sem("r2_ready"), sem("mul_r2")
        rsq_ready, hid_hi, hid_lo = sem("rsq_ready"), sem("hid_hi"), sem("hid_lo")
        gf_in, fin_t, fin_ss, fin_ms, fin_rms, fin_r, fin_o = (sem("gf_in"), sem("fin_t"), sem("fin_ss"),
                                                             sem("fin_ms"), sem("fin_rms"), sem("fin_r"), sem("fin_o"))
        st_out = [sem("st_out0"), sem("st_out1")]

        def raw_need(n):
            twice = [c for c in range(N3 + 2, N4, 3) if c <= n and c % 2 == n % 2]
            return 16 * (n // 2 + 1) + 16 * len(twice)

        def proj_col(n):
            return O_POOL + P * n if n < U_GATE else O_GATE if n == U_GATE else P * (n - U_Q)

        first_block = [0]
        for g, i in ITER:
            first_block.append(first_block[-1] + len(blocks(i)))

        def chunk(it, r):
            b = blocks(ITER[it][1])
            lo, hi = len(b) * r // GR, len(b) * (r + 1) // GR
            return [(first_block[it] + k, k, *b[k]) for k in range(lo, hi)]

        def prob_col(i, kind, kb):
            if kind == "slc":
                return kb * P
            if kind == "win":
                return n_slc(i) + (kb - (i + 1 - n_win(i) // P)) * P
            return n_slc(i) + n_win(i)

        block = ctx.enter_context(nc.Block())

        @block.sync
        def _(sp):
            def load(n, src, slot):
                sp.wait_ge(w_hi, n - 1)
                sp.wait_ge(w_lo, n - 1)
                sp.dma_start(wraw[:, slot], src).then_inc(w_raw[slot], 16)

            for lo, src in ((0, norm1_g), (KT, norm2_g), (2 * KT, pool_scale)):
                rows = src[0].rearrange("(k p) -> k p", p=P)
                sp.dma_start(grow[lo:lo + rows.shape[0]], rows).then_inc(const_in, 16)
            for t in range(4):
                sp.dma_start(xt[:, t, :], x[0, t * P:(t + 1) * P, :]).then_inc(x_in[t], 16)
            sp.dma_start(wraw[:, 0], w_in_u[:, :, bass.ds(proj_col(0), P)]).then_inc(w_raw[0], 16)
            for t in range(4, TT):
                sp.dma_start(xt[:, t, :], x[0, t * P:(t + 1) * P, :]).then_inc(x_in[t], 16)
            sp.dma_start(wraw[:, 1], w_in_u[:, :, bass.ds(proj_col(1), P)]).then_inc(w_raw[1], 16)
            for n in range(2, U_Q):
                load(n, w_in_u[:, :, bass.ds(proj_col(n), P)], n % 2)
            with sp.Fori(0, (N1 - U_Q) // 2) as j:
                for u in range(2):
                    load(U_Q + u + 2 * j, w_in_u[:, :, bass.ds(P * (2 * j) + P * u, P)], (U_Q + u) % 2)
            load(N3, w_in_u[:, :, bass.ds(O_MERGE, P)], N3 % 2)
            load(N3 + 1, w_in_u[:, :, bass.ds(O_MERGE + D, P)], (N3 + 1) % 2)

            def load_q(it):
                g, i = ITER[it]
                if it >= 2:
                    sp.wait_ge(q_lo, it - 1)
                src = proj[U_Q * P + g * GR * HD:U_Q * P + (g + 1) * GR * HD, i * P:(i + 1) * P]
                for side in range(2):
                    sp.dma_start(qraw[side * HD:(side + 1) * HD, it % 2], src.rearrange("(r d) t -> d r t", d=HD)) \
                        .then_inc(q_in[it % 2], 16)

            sp.wait_ge(k_ready, 2)
            sp.wait_ge(misc_ev, N_MISC)
            load_q(0)
            load_q(1)
            for it in range(NIT):
                if it >= 1:
                    g, i = ITER[it - 1]
                    sp.wait_ge(o_ready, it)
                    dst = oscr[g * GR * HD:(g + 1) * GR * HD, i * P:(i + 1) * P].rearrange("(r d) t -> d r t", d=HD)
                    sp.dma_start(dst, ostg[:, (it - 1) % 2].rearrange("d (r t) -> d r t", r=GR)).then_inc(st_o[(it - 1) % 2], 16)
                if it + 2 < NIT:
                    load_q(it + 2)
            g, i = ITER[NIT - 1]
            sp.wait_ge(o_ready, NIT)
            dst = oscr[g * GR * HD:(g + 1) * GR * HD, i * P:(i + 1) * P].rearrange("(r d) t -> d r t", d=HD)
            sp.dma_start(dst, ostg[:, (NIT - 1) % 2].rearrange("d (r t) -> d r t", r=GR)).then_inc(st_o[(NIT - 1) % 2], 16)

            for s in range(2):
                sp.wait_ge(st_o[s], 16 * NIT // 2)
                sp.wait_ge(st_y[s], 16 * 2)
            sp.dma_start(cT[:, 0:4, :], yscr.rearrange("(k p) t -> p k t", p=P)).then_inc(yo_in, 16)
            sp.dma_start(cT[:, 4:8, :], oscr.rearrange("(k p) t -> p k t", p=P)).then_inc(yo_in, 16)

            def load_ab(n, slot, m):
                sp.wait_ge(w_hi, n - 1)
                sp.wait_ge(w_lo, n - 1)
                sp.dma_start(wraw[:, slot, 0:4], w_ap_u[:, :, bass.ds(P * m, P)]).then_inc(w_raw[slot], 16)
                sp.dma_start(wraw[:, slot, 4:8], w_pp_u[:, :, bass.ds(P * m, P)]).then_inc(w_raw[slot], 16)

            with sp.Fori(0, KT // 2 - 1) as j:
                for mm in range(2):
                    n = N3 + 3 * mm
                    load_ab(n + 2 + 6 * j, (n + 2) % 2, 2 * j + mm)
                    load(n + 3 + 6 * j, w_in_u[:, :, bass.ds(P * (2 * j) + (P * (mm + 1) + O_MERGE), P)], (n + 3) % 2)
                    load(n + 4 + 6 * j, w_in_u[:, :, bass.ds(P * (2 * j) + (P * (mm + 1) + O_MERGE + D), P)], (n + 4) % 2)
            n = N3 + 3 * (KT - 2)
            load_ab(n + 2, (n + 2) % 2, KT - 2)
            load(n + 3, w_in_u[:, :, bass.ds(P * (KT - 1) + O_MERGE, P)], (n + 3) % 2)
            load(n + 4, w_in_u[:, :, bass.ds(P * (KT - 1) + O_MERGE + D, P)], (n + 4) % 2)
            load_ab(n + 5, (n + 5) % 2, KT - 1)

            load(N4, w_out_u[:, :, bass.ds(0, P)], N4 % 2)
            load(N4 + 1, w_out_u[:, :, bass.ds(P, P)], (N4 + 1) % 2)
            sp.wait_ge(u_done, 2 * N4)
            sp.wait_ge(c_ready, 2 * KT)
            for t in range(TT):
                if t >= 2:
                    sp.wait_ge(xr_t, t - 1)
                sp.dma_start(xr[:, t % 2], x[0, t * P:(t + 1) * P, :]).then_inc(xr_in[t % 2], 16)
            with sp.Fori(1, KT // 2) as j:
                for u in range(2):
                    load(N4 + u + 2 * j, w_out_u[:, :, bass.ds(P * (2 * j) + P * u, P)], (N4 + u) % 2)

            with sp.Fori(0, ROUNDS) as r:
                with sp.Fori(0, KT // 2) as j:
                    for u in range(2):
                        load(N5 + u + 2 * j + 2 * KT * r, w_ff1_u[:, :, bass.ds(D * r + P * 2 * j + P * u, P)], (N5 + u) % 2)
                with sp.Fori(0, KT // 2) as j:
                    for u in range(2):
                        load(N5 + KT + u + 2 * j + 2 * KT * r,
                             w_ff2_u[:, bass.ds(KT * r, KT), bass.ds(P * 2 * j + P * u, P)], (N5 + u) % 2)

            sp.wait_ge(u_done, 2 * (N5 + 2 * KT * ROUNDS))
            sp.dma_start(gfb[:], final_g.partition_broadcast(P)).then_inc(gf_in, 16)
            for t in range(TT):
                sp.wait_ge(fin_o, t + 1)
                sp.dma_start(out[0, t * P:(t + 1) * P, :], ost[:, t % 2]).then_inc(st_out[t % 2], 16)
            for s in range(2):
                sp.wait_ge(st_out[s], 16 * TT // 2)

        @block.gpsimd
        def _(pool):
            count = [0]

            def link(ins):
                count[0] += 1
                ins.then_inc(chain_p, 1)
                pool.wait_ge(chain_p, count[0])

            link(pool.memset(ident[:], 0.0))
            link(pool.affine_select(out=ident[:], in_=ident[:], compare_op=ALU.not_equal, fill=1.0, base=0,
                                    pattern=[[-1, P]], channel_multiplier=1))
            pool.memset(ones[:], 1.0)
            link(pool.memset(qscale[:], 1.0))
            for j in range(4):
                for side in range(2):
                    last = pool.memset(qscale[side * HD:(side + 1) * HD, U_Q + j:U_Q + j + 1],
                                       2.0 ** (2 * j + side + 1) * HD ** -0.5)
            last.then_inc(consts, 1)

            def h_low(t):
                pool.wait_ge(h_hi, t + 1)
                nc.gpsimd.tensor_tensor(alo[:, :, t * P:(t + 1) * P], hraw[:, t % 2],
                                        ahi[:, :, t * P:(t + 1) * P].bitcast(f32), ALU.subtract).then_inc(h_lo, 1)

            for t in range(TT):
                h_low(t)

            pool.iota(T1[:], pattern=[[1, S]], base=-(S - P), channel_multiplier=-1,
                      allow_small_or_imprecise_dtypes=True)
            pool.iota(TW[:], pattern=[[1, (WIN_TILES + 1) * P]], base=-WIN_TILES * P, channel_multiplier=-1,
                      allow_small_or_imprecise_dtypes=True)
            link(pool.iota(TC[:], pattern=[[-P, TT], [CSTRIDE, CP]], base=CBLOCK - 1, channel_multiplier=-1,
                           allow_small_or_imprecise_dtypes=True))
            pool.affine_select(out=T1[:], in_=T1[:], compare_op=ALU.is_ge, fill=NEG, base=S - P,
                               pattern=[[-1, S]], channel_multiplier=1)
            link(pool.affine_select(out=TW[:], in_=TW[:], compare_op=ALU.is_ge, fill=NEG, base=WIN_TILES * P,
                                    pattern=[[-1, (WIN_TILES + 1) * P]], channel_multiplier=1))
            link(pool.affine_select(out=TC[:], in_=TC[:], compare_op=ALU.is_ge, fill=NEG, base=-(CBLOCK - 1),
                                    pattern=[[P, TT], [-CSTRIDE, CP]], channel_multiplier=1))
            link(pool.affine_select(out=TW[:, 0:P], in_=TW[:, 0:P], compare_op=ALU.is_gt, fill=NEG, base=0,
                                    pattern=[[1, P]], channel_multiplier=-1))
            link(pool.memset(TC[:, :, NCMP:CP], NEG))
            link(pool.memset(cvalid[:], 1.0))
            link(pool.affine_select(out=cvalid[:], in_=cvalid[:], compare_op=ALU.is_ge, fill=0.0, base=-(CBLOCK - 1),
                                    pattern=[[0, 1]], channel_multiplier=1))
            pool.memset(up[:, :, 0:PAD], 0.0)
            pool.memset(tA[:, 0:PAD], 0.0)
            link(pool.memset(tB[:, 0:PAD], 0.0))
            link(pool.iota(icnt[:], pattern=[[0, 4], [1, PAD]], base=1, channel_multiplier=0,
                           allow_small_or_imprecise_dtypes=True))
            for k in range(4):
                last = pool.tensor_scalar(icnt[:, k], icnt[:, k], float(2 ** (k + 1)), None, ALU.min)
            last.then_inc(consts, 1)
            pool.memset(chid[:, :, :, NCMP:CP], 0.0).then_inc(consts, 1)

            def store(n, slot, row):
                pool.wait_ge(ev[0], n + 1)
                pool.wait_ge(ev[1], n + 1)
                pool.dma_start(proj[bass.ds(row, P), :], stage[:, slot]).then_inc(st_proj[slot], 16)

            for n in range(U_Q):
                store(n, n % 2, n * P)

            pool.wait_ge(st_proj[0], 32)
            pool.wait_ge(st_proj[1], 32)
            pool.dma_start(up[:, :, PAD:], proj[0:4 * P, :].rearrange("(k p) t -> p k t", p=P)).then_inc(u_in, 16)
            pool.dma_start(wp[:], w_pool[0].rearrange("g c d -> c g d")).then_inc(pool_w_in, 16)
            pool.wait_ge(u_in, 16)
            pool.wait_ge(consts, 4)
            for k in range(4):
                if k == 2:
                    with pool.Fori(0, 2) as j:
                        for u in range(2):
                            store(U_Q + u + 2 * j, (U_Q + u) % 2, 2 * P * j + P * (U_Q + u))
                cur = up[:, k]
                bufs = [tA, tB]
                for d in range(k + 1):
                    sft = 2 ** d
                    nxt = bufs[d % 2]
                    link(pool.tensor_tensor(nxt[:, PAD:], cur[:, PAD:], cur[:, PAD - sft:PAD + S - sft], ALU.add))
                    cur = nxt
                dst = bufs[(k + 1) % 2]
                pool.tensor_tensor(dst[:, PAD:2 * PAD], cur[:, PAD:2 * PAD], icnt[:, k], ALU.mult)
                link(pool.tensor_scalar(dst[:, 2 * PAD:], cur[:, 2 * PAD:], 2.0 ** -(k + 1), None, ALU.mult))
                ins = pool.tensor_tensor(up[:, k, PAD:], dst[:, PAD:], up[:, k, PAD:], ALU.subtract)
                ins.then_inc(pooled, 1)
                pool.wait_ge(pooled, k + 1)
            with pool.Fori(2, (N1 - U_Q) // 2) as j:
                for u in range(2):
                    store(U_Q + u + 2 * j, (U_Q + u) % 2, 2 * P * j + P * (U_Q + u))

            def rows(unit):
                return proj[unit * P:(unit + 1) * P, :]

            for s in range(2):
                pool.wait_ge(st_proj[s], 16 * ((N1 + 1 - s) // 2))
            pool.dma_start(cw1[:], cmp_w1[0].rearrange("b (j l) d h -> (l d) b j h", l=2)).then_inc(cw_in, 16)
            pool.dma_start(cw2[:, :, 0:HD], cmp_w2[0].rearrange("b h e -> h b e")).then_inc(cw_in, 16)
            pool.dma_start(cw2[:, :, HD:], cmp_w2[0].rearrange("b h e -> h b e")).then_inc(cw_in, 16)
            pool.dma_start(pet[:], cmp_pe[0].rearrange("b (j l) d -> j b (l d)", l=2)).then_inc(cw_in, 16)

            def load_cc(unit):
                src = rows(unit).rearrange("(g d) t -> d g t", d=HD)
                pool.dma_start(ccd[0:HD], src).then_inc(cc_in, 16)
                pool.dma_start(ccd[HD:P, :, 0:S - 1], src[:, :, 1:S]).then_inc(cc_in, 16)

            load_cc(U_KC)
            pool.dma_start(gtd[:], proj[U_GATE * P:U_GATE * P + NG, :]).then_inc(gate_in, 16)
            pool.dma_start(vsd[:], rows(U_VS)).then_inc(vs_in, 16)
            pool.dma_start(vwd[:], rows(U_VW)).then_inc(vw_in, 16)
            for k in range(4):
                pool.wait_ge(misc_ev, 2 * k + 2)
                pool.dma_start(yscr[k * P:(k + 1) * P, :], stage[:, k % 2]).then_inc(st_y[k % 2], 16)
            pool.wait_ge(misc, N_Y)
            for unit, dst, s in ((U_KS, ksd, ks_in), (U_KW, kwd, kw_in)):
                for side in range(2):
                    pool.dma_start(dst[side * HD:(side + 1) * HD], rows(unit).rearrange("(g d) t -> d g t", d=HD)).then_inc(s, 16)
            pool.wait_ge(misc, N_Y + 8)
            load_cc(U_VC)

            for it in range(NIT):
                g, i = ITER[it]
                for r in range(GR):
                    pool.wait_ge(rs_ready, it * GR + r + 1)
                    row = PB[it % 2]
                    a, b = n_slc(i), n_slc(i) + n_win(i)
                    for k, (lo, hi) in enumerate(((0, a), (a, b), (b, b + CP))):
                        last = pool.tensor_scalar(row[:, r, lo:hi], row[:, r, lo:hi], rs[:, it % 2, r, k:k + 1], None, ALU.mult)
                    last.then_inc(p_ready, 1)

            for m in range(KT):
                for h in range(2):
                    s = 2 * m + h
                    pool.wait_ge(res[h], m + 1)
                    xs = xT[:, m, h * HALF:(h + 1) * HALF]
                    if m == 0:
                        pool.tensor_tensor(sqa[:, h * HALF:(h + 1) * HALF], xs, xs, ALU.mult).then_inc(sq_sum, 1)
                    else:
                        link(pool.tensor_tensor(sqt[:], xs, xs, ALU.mult))
                        pool.wait_ge(sq_sum, s)
                        pool.tensor_tensor(sqa[:, h * HALF:(h + 1) * HALF], sqa[:, h * HALF:(h + 1) * HALF], sqt[:],
                                           ALU.add).then_inc(sq_sum, 1)
                        pool.wait_ge(sq_sum, s + 1)

        @block.scalar
        def _(act):
            def split_hi(n, slot, raw_count, first=False):
                act.wait_ge(w_raw[slot], raw_count)
                if not first:
                    act.wait_ge(u_done, 2 * (n - 1))
                nc.scalar.activation(whi[:, slot], wraw[:, slot], ACT.Copy).then_inc(w_hi, 1)

            def root(t):
                act.wait_ge(ms_ready, t + 1)
                nc.scalar.activation(rms[:, t:t + 1], msq[:, t:t + 1], ACT.Sqrt).then_inc(rms_ready, 1)

            def h_high(t):
                act.wait_ge(hraw_ready, t + 1)
                nc.scalar.activation(ahi[:, :, t * P:(t + 1) * P], hraw[:, t % 2], ACT.Copy).then_inc(h_hi, 1)

            for t in range(TT):
                act.wait_ge(x_in[t], 16)
                if t:
                    act.wait_ge(ss_ready, t)
                nc.scalar.activation(sqj[:], xt[:, t, :], ACT.Square, accum_out=ssum[:, t:t + 1]).then_inc(ss_ready, 1)
                if t >= 1:
                    root(t - 1)
                if t == 2:
                    split_hi(0, 0, 16, first=True)
                if t >= 3:
                    h_high(t - 3)
            root(TT - 1)
            for t in range(TT - 3, TT):
                h_high(t)

            def evac_proj(n, slot, col, reuse=None):
                act.wait_ge(u_done, 2 * n + 1)
                if reuse is not None:
                    act.wait_ge(st_proj[slot], reuse)
                nc.scalar.activation(stage[:, slot, 0:HALF], psU[:, 2 * slot], ACT.Copy, scale=qscale[:, col]).then_inc(ev[0], 1)

            act.wait_ge(consts, 1)
            act.wait_ge(h_lo, TT)
            for n in range(U_Q):
                split_hi(n + 1, (n + 1) % 2, raw_need(n + 1), first=(n == 0))
                evac_proj(n, n % 2, slice(n, n + 1), 16 * (n // 2) if n >= 2 else None)
            with act.Fori(0, (N1 - U_Q) // 2) as j:
                for u in range(2):
                    n = U_Q + u
                    split_hi(n + 1 + 2 * j, (n + 1) % 2, 16 * j + raw_need(n + 1))
                    evac_proj(n + 2 * j, n % 2, bass.ds(2 * j + n, 1), 16 * j + 16 * (n // 2))

            step = [N_Y]

            def wait_misc():
                step[0] += 1
                act.wait_ge(misc, step[0])

            wait_misc()
            nc.scalar.activation(gate_t[:], psX[:, (step[0] - 1) % 4, 0:TT * NG], ACT.Tanh, scale=0.5).then_inc(gate_tanh, 1)
            for vt, in ((vS,), (vW,)):
                for q in range(2):
                    wait_misc()
                    ps = psX[:, (step[0] - 1) % 4].rearrange("p (t g d) -> p t g d", t=4, g=GROUPS)
                    nc.scalar.activation(vt[:, 4 * q:4 * q + 4, :, 0:HD], ps, ACT.Copy).then_inc(v_hi, 1)
            for b, (dst, src, s) in enumerate(((kS, ksd, ks_in), (kW, kwd, kw_in))):
                act.wait_ge(s, 32)
                nc.scalar.activation(dst[:], src[:], ACT.Copy).then_inc(k_hi, 1)
            for b in range(2):
                act.wait_ge(gelu_arg, b + 1)
                nc.scalar.activation(cz[:, 0:GROUPS * NCMP], cv[:, 0:GROUPS * NCMP], ACT.Tanh, scale=GELU_C).then_inc(gelu_tanh, 1)

            def query_hi(it):
                act.wait_ge(q_in[it % 2], 32 * (it // 2 + 1))
                if it >= 2:
                    act.wait_ge(s_win, GR * (it - 1))
                nc.scalar.activation(qh[:, it % 2], qraw[:, it % 2], ACT.Copy).then_inc(q_hi, 1)

            def exps(it, r):
                g, i = ITER[it]
                head = g * GR + r
                act.wait_ge(nb_ready, it * GR + r + 1)
                row = PB[it % 2]
                a, b = n_slc(i), n_slc(i) + n_win(i)
                for k, (lo, hi) in enumerate(((0, a), (a, b), (b, b + CP))):
                    last = nc.scalar.activation(row[:, r, lo:hi], row[:, r, lo:hi], ACT.Exp, scale=2.0 ** -(head + 1),
                                                bias=nb[:, it % 2, r, k:k + 1], accum_out=esum[:, it % 2, r, k:k + 1])
                last.then_inc(exp_done, 1)

            def prob_hi(B, kind):
                rows = CP if kind == "cmp" else P
                act.wait_ge(t_done, B + 1)
                if B >= 2:
                    act.wait_ge(pv_done, B - 1)
                nc.scalar.activation(pth[0:rows, B % 2], psX[0:rows, B % 2], ACT.Copy).then_inc(pt_hi, 1)

            def out_half(it):
                act.wait_ge(pv_done, first_block[it + 1])
                if it >= 1:
                    act.wait_ge(o_ready, it)
                nc.scalar.activation(otmp[:], psX[HD:P, 2 + it % 2], ACT.Copy).then_inc(o_half, 1)

            query_hi(0)
            query_hi(1)
            for r in range(GR):
                exps(0, r)
            for it in range(NIT):
                for r in range(GR):
                    for B, k, kind, kb in chunk(it, r):
                        prob_hi(B, kind)
                    if it + 1 < NIT:
                        exps(it + 1, r)
                out_half(it)
                if it + 2 < NIT:
                    query_hi(it + 2)

            act.wait_ge(yo_in, 32)
            act.wait_ge(o_ready, NIT)
            nc.scalar.activation(yhi[:], cT[:, 0:4, :], ACT.Copy).then_inc(yo_hi, 1)
            nc.scalar.activation(ohi[:], cT[:, 4:8, :], ACT.Copy).then_inc(yo_hi, 1)

            def gate_evac(n, z, m2):
                for h in range(2):
                    act.wait_ge(u_done, 2 * n + h + 1)
                    act.wait_ge(ab_free, m2 + h + 1)
                    nc.scalar.activation((m0, m1)[z][:, h * HALF:(h + 1) * HALF], psU[:, 2 * z + h], ACT.Tanh,
                                         scale=0.5).then_inc(z_ready, 1)

            with act.Fori(0, KT // 2) as j:
                for mm in range(2):
                    n = N3 + 3 * mm
                    for z in range(2):
                        nn = n + z
                        split_hi(nn + 1 + 6 * j, (nn + 1) % 2, 64 * j + raw_need(nn + 1))
                        gate_evac(nn + 6 * j, z, 4 * j + 2 * mm)
                    nn = n + 2
                    split_hi(nn + 1 + 6 * j, (nn + 1) % 2, 64 * j + raw_need(nn + 1))

            act.wait_ge(c_ready, 2 * KT)
            for t in range(TT):
                act.wait_ge(xr_t, t + 1)
                nc.scalar.activation(xT[:, 0:4, t * P:(t + 1) * P],
                                     psX[:, 2 * (t % 2)].rearrange("p (k t) -> p k t", k=4), ACT.Copy).then_inc(xT_a, 1)
            for k in range(KT):
                nc.scalar.activation(ahi[:, k], cT[:, k], ACT.Copy, scale=0.5).then_inc(c_hi, 1)

            def out_evac(m):
                for h in range(2):
                    act.wait_ge(res[h], m + 1)
                    nc.scalar.activation(h2hi[:, bass.ds(m, 1), h * HALF:(h + 1) * HALF], xT[:, bass.ds(m, 1), h * HALF:(h + 1) * HALF],
                                         ACT.Copy, scale=g2[:, bass.ds(m, 1)]).then_inc(h2_hi, 1)

            with act.Fori(0, KT // 2) as j:
                for u in range(2):
                    n = N4 + u
                    split_hi(n + 1 + 2 * j, (n + 1) % 2, 16 * j + raw_need(n + 1))
                    out_evac(2 * j + u)

            def up_evac(n, slot, s, t):
                for h in range(2):
                    act.wait_ge(u_done, 2 * n + h + 1)
                    nc.scalar.activation(rel[:, h], psU[:, 2 * slot + h], ACT.Relu).then_inc(relu[h], 1)
                for h in range(2):
                    act.wait_ge(rsq_ready, s + h + 1)
                    nc.scalar.activation(ahi[:, bass.ds(t, 1), h * HALF:(h + 1) * HALF], rsq[:, h:h + 1], ACT.Copy).then_inc(hid_hi, 1)

            def mlp_round(r, last):
                with act.Fori(0, KT // 2) as j:
                    for u in range(2):
                        n = N5 + u
                        split_hi(n + 1 + 2 * j + 2 * KT * r, (n + 1) % 2, 16 * j + 16 * KT * r + raw_need(n + 1))
                        up_evac(n + 2 * j + 2 * KT * r, n % 2, 2 * KT * r + 4 * j + 2 * u, 2 * j + u)
                n = N5 + KT
                with act.Fori(0, KT // 2 - (1 if last else 0)) as j:
                    for u in range(2):
                        split_hi(n + u + 1 + 2 * j + 2 * KT * r, (n + u + 1) % 2,
                                 16 * j + 16 * KT * r + raw_need(n + u + 1))
                if last:
                    nl = N5 + 2 * KT * ROUNDS - 1
                    split_hi(nl, nl % 2, raw_need(nl))

            with act.Fori(0, ROUNDS - 1) as r:
                mlp_round(r, False)
            mlp_round(ROUNDS - 1, True)

            act.wait_ge(u_done, 2 * (N5 + 2 * KT * ROUNDS))
            for t in range(TT):
                act.wait_ge(fin_t, t + 1)
                if t:
                    act.wait_ge(fin_ss, t)
                nc.scalar.activation(sqo[:], psX[:, 2 * (t % 2):2 * (t % 2) + 2].rearrange("p b n -> p (b n)"),
                                     ACT.Square, accum_out=ssum[:, t:t + 1]).then_inc(fin_ss, 1)
                act.wait_ge(fin_ms, t + 1)
                nc.scalar.activation(rms[:, t:t + 1], msq[:, t:t + 1], ACT.Sqrt).then_inc(fin_rms, 1)

        @block.vector
        def _(dve):
            count = [0]

            def link(ins):
                count[0] += 1
                ins.then_inc(chain_v, 1)
                dve.wait_ge(chain_v, count[0])

            def split_lo(n, slot):
                dve.wait_ge(w_hi, n + 1)
                nc.vector.tensor_tensor(wlo[:, slot], wraw[:, slot], whi[:, slot].bitcast(f32), ALU.subtract).then_inc(w_lo, 1)

            def mean_sq(t):
                dve.wait_ge(ss_ready, t + 1)
                nc.vector.tensor_scalar(msq[:, t:t + 1], ssum[:, t:t + 1], 1.0 / D, EPS, ALU.mult, ALU.add).then_inc(ms_ready, 1)

            def normalize(t):
                dve.wait_ge(rms_ready, t + 1)
                nc.vector.reciprocal(rstd[:, t:t + 1], rms[:, t:t + 1]).then_inc(rstd_ready, 1)
                dve.wait_ge(rstd_ready, t + 1)
                nc.vector.tensor_scalar(xt[:, t, :], xt[:, t, :], rstd[:, t:t + 1], None, ALU.mult).then_inc(xs_ready, 1)

            def gain(t):
                dve.wait_ge(xt_ready, t + 1)
                if t >= 2:
                    dve.wait_ge(h_lo, t - 1)
                for q in range(2):
                    last = nc.vector.tensor_tensor(hraw[:, t % 2, 4 * q:4 * q + 4], psX[:, 2 * (t % 2) + q].rearrange("p (k t) -> p k t", k=4),
                                                   g1[:, 4 * q:4 * q + 4].unsqueeze(2).broadcast_to([P, 4, P]), ALU.mult)
                last.then_inc(hraw_ready, 1)

            dve.wait_ge(gain_t, 1)
            nc.vector.tensor_copy(gcol[:], psU[:, 0, 0:2 * KT + 4]).then_inc(gain_ready, 1)
            dve.wait_ge(gain_ready, 1)
            mean_sq(0)
            for t in range(TT):
                if t + 1 < TT:
                    mean_sq(t + 1)
                normalize(t)
                if t == 2:
                    split_lo(0, 0)
                if t >= 1:
                    gain(t - 1)
            gain(TT - 1)

            def evac_proj(n, slot, col, reuse=None):
                dve.wait_ge(u_done, 2 * n + 2)
                if reuse is not None:
                    dve.wait_ge(st_proj[slot], reuse)
                nc.vector.tensor_scalar(stage[:, slot, HALF:], psU[:, 2 * slot + 1], qscale[:, col], None, ALU.mult).then_inc(ev[1], 1)

            dve.wait_ge(h_lo, TT)
            for n in range(U_Q):
                split_lo(n + 1, (n + 1) % 2)
                evac_proj(n, n % 2, slice(n, n + 1), 16 * (n // 2) if n >= 2 else None)
                if n == 0:
                    dve.wait_ge(consts, 3)
                    nc.vector.reciprocal(icnt[:], icnt[:]).then_inc(consts, 1)
            with dve.Fori(0, (N1 - U_Q) // 2) as j:
                for u in range(2):
                    n = U_Q + u
                    split_lo(n + 1 + 2 * j, (n + 1) % 2)
                    evac_proj(n + 2 * j, n % 2, bass.ds(2 * j + n, 1), 16 * j + 16 * (n // 2))

            step = [0]

            def wait_misc():
                step[0] += 1
                dve.wait_ge(misc, step[0])

            for s in range(2):
                dve.wait_ge(st_proj[s], 16 * ((N1 + 1 - s) // 2))
            for k in range(4):
                if k >= 2:
                    dve.wait_ge(st_y[k % 2], 16)
                for h in range(2):
                    wait_misc()
                    nc.vector.tensor_scalar(stage[:, k % 2, h * HALF:(h + 1) * HALF], psX[:, (step[0] - 1) % 4],
                                            psc[:, k:k + 1], None, ALU.mult).then_inc(misc_ev, 1)
            wait_misc()
            dve.wait_ge(gate_tanh, 1)
            link(nc.vector.tensor_scalar(gates[:].rearrange("p t h b -> p (t h b)"), gate_t[:], 1.0, 0.5, ALU.add, ALU.mult))
            nc.vector.tensor_scalar(gates[:, 0, :, 0:1], gates[:, 0, :, 0:1], cvalid[:, 0:1], None, ALU.mult).then_inc(misc_ev, 1)
            nv = 0
            for vt in (vS, vW):
                for q in range(2):
                    wait_misc()
                    nv += 1
                    dve.wait_ge(v_hi, nv)
                    ps = psX[:, (step[0] - 1) % 4].rearrange("p (t g d) -> p t g d", t=4, g=GROUPS)
                    nc.vector.tensor_tensor(vt[:, 4 * q:4 * q + 4, :, HD:], ps, vt[:, 4 * q:4 * q + 4, :, 0:HD].bitcast(f32),
                                            ALU.subtract).then_inc(misc_ev, 1)
            for b, (dst, src) in enumerate(((kS, ksd), (kW, kwd))):
                dve.wait_ge(k_hi, b + 1)
                nc.vector.tensor_tensor(dst[HD:P], src[HD:P], dst[HD:P].bitcast(f32), ALU.subtract).then_inc(k_ready, 1)
            wait_misc()
            nc.vector.tensor_copy(pe2[:].rearrange("p b j -> p (b j)"), psX[:, (step[0] - 1) % 4, 0:CBLOCK]).then_inc(misc_ev, 1)
            wait_misc()
            nc.vector.tensor_copy(cb[:], psX[0:HD, (step[0] - 1) % 4, 0:2]).then_inc(misc_ev, 1)
            dve.wait_ge(misc_ev, step[0])
            n2 = GROUPS * NCMP

            for b in range(2):
                wait_misc()
                link(nc.vector.tensor_scalar(cu[:, b, 0:n2], psX[0:HD, (step[0] - 1) % 4, 0:n2], cb[:, b:b + 1], None, ALU.add))
                link(nc.vector.tensor_tensor(cv[:, 0:n2], cu[:, b, 0:n2], cu[:, b, 0:n2], ALU.mult))
                link(nc.vector.tensor_scalar(cv[:, 0:n2], cv[:, 0:n2], 0.044715, 1.0, ALU.mult, ALU.add))
                nc.vector.tensor_tensor(cv[:, 0:n2], cv[:, 0:n2], cu[:, b, 0:n2], ALU.mult).then_inc(gelu_arg, 1)
                dve.wait_ge(gelu_tanh, b + 1)
                dve.wait_ge(consts, 3)
                nc.vector.scalar_tensor_tensor(out=chid[:, b, :, 0:NCMP], in0=cz[:, 0:n2].rearrange("p (g c) -> p g c", g=GROUPS),
                                               scalar=1.0, in1=cu[:, b, 0:n2].rearrange("p (g c) -> p g c", g=GROUPS),
                                               op0=ALU.add, op1=ALU.mult).then_inc(misc_ev, 1)
                wait_misc()
                ps = psX[:, (step[0] - 1) % 4, 0:P]
                if b == 0:
                    link(nc.vector.tensor_scalar(kcs[:], ps, 0.5, None, ALU.mult))
                    link(nc.vector.tensor_copy(kC[:].rearrange("p g c -> p (g c)"), kcs[:]))
                    nc.vector.tensor_tensor(kC[HD:P].rearrange("p g c -> p (g c)"), kcs[HD:P],
                                            kC[HD:P].rearrange("p g c -> p (g c)").bitcast(f32), ALU.subtract).then_inc(misc_ev, 1)
                else:
                    link(nc.vector.tensor_scalar(kcs[0:CP], ps[0:CP], 0.5, None, ALU.mult))
                    kv = kcs[0:CP].rearrange("c (g d) -> c g d", g=GROUPS)
                    link(nc.vector.tensor_copy(vC[:, :, 0:HD], kv))
                    nc.vector.tensor_tensor(vC[:, :, HD:], kv, vC[:, :, 0:HD].bitcast(f32), ALU.subtract).then_inc(misc_ev, 1)

            def query_lo(it):
                dve.wait_ge(q_hi, it + 1)
                nc.vector.tensor_tensor(ql[:, it % 2], qraw[:, it % 2], qh[:, it % 2].bitcast(f32), ALU.subtract).then_inc(q_lo, 1)

            def maxima(it, r):
                g, i = ITER[it]
                e = it * GR + r
                head = g * GR + r
                row = PB[it % 2]
                a, b = n_slc(i), n_slc(i) + n_win(i)
                if it >= 2 and r == 0:
                    dve.wait_ge(t_done, first_block[it - 1])
                dve.wait_ge(s_slc, e + 1)
                nc.vector.tensor_tensor_reduce(out=row[:, r, 0:a], in0=psS0[:, 0:a], in1=T1[:, S - a:S], scale=1.0, scalar=-3e38,
                                               op0=ALU.add, op1=ALU.max, accum_out=mx[:, it % 2, r, 0:1]).then_inc(m_slc, 1)
                dve.wait_ge(s_win, e + 1)
                nc.vector.tensor_tensor_reduce(out=row[:, r, a:b], in0=psS1[:, 0:b - a], in1=TW[:, (WIN_TILES + 1) * P - (b - a):],
                                               scale=1.0, scalar=-3e38, op0=ALU.add, op1=ALU.max, accum_out=mx[:, it % 2, r, 1:2])
                nc.vector.tensor_tensor_reduce(out=row[:, r, b:b + CP], in0=psS1[:, b - a:b - a + CP], in1=TC[:, i], scale=1.0,
                                               scalar=-3e38, op0=ALU.add, op1=ALU.max, accum_out=mx[:, it % 2, r, 2:3]).then_inc(m_win, 1)
                dve.wait_ge(m_win, e + 1)
                nc.vector.tensor_scalar(nb[:, it % 2, r], mx[:, it % 2, r], -2.0 ** -(head + 1), None, ALU.mult).then_inc(nb_ready, 1)

            def weights(it, r):
                g, i = ITER[it]
                head = g * GR + r
                dve.wait_ge(exp_done, it * GR + r + 1)
                link(nc.vector.reciprocal(rs[:, it % 2, r], esum[:, it % 2, r]))
                nc.vector.tensor_tensor(rs[:, it % 2, r, 0:2], gates[:, i, head, 1:3], rs[:, it % 2, r, 0:2], ALU.mult)
                nc.vector.tensor_tensor(rs[:, it % 2, r, 2:3], gates[:, i, head, 0:1], rs[:, it % 2, r, 2:3], ALU.mult).then_inc(rs_ready, 1)

            def prob_lo(B, kind):
                rows = CP if kind == "cmp" else P
                dve.wait_ge(pt_hi, B + 1)
                nc.vector.tensor_tensor(ptl[0:rows, B % 2], psX[0:rows, B % 2], pth[0:rows, B % 2].bitcast(f32),
                                        ALU.subtract).then_inc(pt_lo, 1)

            def out_sum(it):
                dve.wait_ge(o_half, it + 1)
                if it >= 2:
                    dve.wait_ge(st_o[it % 2], 16 * (it // 2))
                nc.vector.tensor_tensor(ostg[:, it % 2], psX[0:HD, 2 + it % 2], otmp[:], ALU.add).then_inc(o_ready, 1)

            for s in range(2):
                dve.wait_ge(st_y[s], 32)
            query_lo(0)
            query_lo(1)
            for r in range(GR):
                maxima(0, r)
                if r:
                    weights(0, r - 1)
            weights(0, GR - 1)
            for it in range(NIT):
                for r in range(GR):
                    if it + 1 < NIT:
                        maxima(it + 1, r)
                    for B, k, kind, kb in chunk(it, r):
                        prob_lo(B, kind)
                    if it + 1 < NIT:
                        weights(it + 1, r)
                out_sum(it)
                if it + 2 < NIT:
                    query_lo(it + 2)

            dve.wait_ge(yo_hi, 1)
            nc.vector.tensor_tensor(ylo[:], cT[:, 0:4, :], yhi[:].bitcast(f32), ALU.subtract).then_inc(ab_free, 1)
            dve.wait_ge(yo_hi, 2)
            nc.vector.tensor_tensor(olo[:], cT[:, 4:8, :], ohi[:].bitcast(f32), ALU.subtract).then_inc(ab_free, 1)

            def mix(n, m, s):
                for h in range(2):
                    cols = slice(h * HALF, (h + 1) * HALF)
                    dve.wait_ge(u_done, 2 * n + h + 1)
                    dve.wait_ge(z_ready, 2 * s + 2 + h + 1)
                    nc.vector.scalar_tensor_tensor(out=mt[:, 0], in0=m0[:, cols], scalar=1.0, in1=psX[:, h], op0=ALU.add,
                                                   op1=ALU.mult)
                    nc.vector.scalar_tensor_tensor(out=mt[:, 1], in0=m1[:, cols], scalar=1.0, in1=psX[:, 2 + h], op0=ALU.add,
                                                   op1=ALU.mult).then_inc(ab_free, 1)
                    dve.wait_ge(ab_free, s + h + 3)
                    nc.vector.tensor_tensor(cT[:, bass.ds(m, 1), cols], mt[:, 0:1], mt[:, 1:2], ALU.add).then_inc(c_ready, 1)
                    dve.wait_ge(c_ready, s + h + 1)

            with dve.Fori(0, KT // 2) as j:
                for mm in range(2):
                    n = N3 + 3 * mm
                    for z in range(3):
                        split_lo(n + z + 1 + 6 * j, (n + z + 1) % 2)
                    mix(n + 2 + 6 * j, 2 * j + mm, 4 * j + 2 * mm)

            for t in range(TT):
                dve.wait_ge(xr_t, t + 1)
                nc.vector.tensor_copy(xT[:, 4:8, t * P:(t + 1) * P],
                                      psX[:, 2 * (t % 2) + 1].rearrange("p (k t) -> p k t", k=4)).then_inc(xT_v, 1)
            for k in range(KT):
                dve.wait_ge(c_hi, k + 1)
                nc.vector.scalar_tensor_tensor(out=alo[:, k], in0=cT[:, k], scalar=0.5, in1=ahi[:, k].bitcast(f32), op0=ALU.mult,
                                               op1=ALU.subtract).then_inc(c_lo, 1)
            dve.wait_ge(xT_a, TT)
            dve.wait_ge(xT_v, TT)

            def out_evac(n, slot, m, s):
                for h in range(2):
                    dve.wait_ge(u_done, 2 * n + h + 1)
                    cols = slice(h * HALF, (h + 1) * HALF)
                    nc.vector.tensor_tensor(xT[:, bass.ds(m, 1), cols], psU[:, 2 * slot + h:2 * slot + h + 1],
                                            xT[:, bass.ds(m, 1), cols], ALU.add).then_inc(res[h], 1)
                for h in range(2):
                    cols = slice(h * HALF, (h + 1) * HALF)
                    dve.wait_ge(h2_hi, s + h + 1)
                    nc.vector.scalar_tensor_tensor(out=h2lo[:, bass.ds(m, 1), cols], in0=xT[:, bass.ds(m, 1), cols],
                                                   scalar=g2[:, bass.ds(m, 1)], in1=h2hi[:, bass.ds(m, 1), cols].bitcast(f32),
                                                   op0=ALU.mult, op1=ALU.subtract).then_inc(h2_lo, 1)

            with dve.Fori(0, KT // 2) as j:
                for u in range(2):
                    n = N4 + u
                    split_lo(n + 1 + 2 * j, (n + 1) % 2)
                    out_evac(n + 2 * j, n % 2, 2 * j + u, 4 * j + 2 * u)

            for h in range(2):
                cols = slice(h * HALF, (h + 1) * HALF)
                dve.wait_ge(ms_done, h + 1)
                link(nc.vector.tensor_scalar(r2[:, cols], psX[:, h], 1.0 / D, EPS, ALU.mult, ALU.add))
                nc.vector.reciprocal(r2[:, cols], r2[:, cols]).then_inc(r2_ready, 1)
            dve.wait_ge(r2_ready, 2)

            def up_evac(s, c, t):
                for h in range(2):
                    dve.wait_ge(relu[h], c + 1)
                    nc.vector.tensor_tensor(rsq[:, h], rel[:, h], rel[:, h], ALU.mult).then_inc(rsq_ready, 1)
                for h in range(2):
                    dve.wait_ge(hid_hi, s + h + 1)
                    nc.vector.tensor_tensor(alo[:, bass.ds(t, 1), h * HALF:(h + 1) * HALF], rsq[:, h:h + 1],
                                            ahi[:, bass.ds(t, 1), h * HALF:(h + 1) * HALF].bitcast(f32), ALU.subtract).then_inc(hid_lo, 1)
                dve.wait_ge(hid_lo, s + 2)

            def down_evac(n, slot, m, s):
                for h in range(2):
                    cols = slice(h * HALF, (h + 1) * HALF)
                    dve.wait_ge(u_done, 2 * n + h + 1)
                    nc.vector.tensor_tensor(f2t[:, h], psU[:, 2 * slot + h], r2[:, cols], ALU.mult).then_inc(mul_r2, 1)
                    dve.wait_ge(mul_r2, s + h + 1)
                    nc.vector.tensor_tensor(xT[:, bass.ds(m, 1), cols], xT[:, bass.ds(m, 1), cols], f2t[:, h:h + 1], ALU.add).then_inc(res[h], 1)

            def mlp_round(r, last):
                with dve.Fori(0, KT // 2) as j:
                    for u in range(2):
                        n = N5 + u
                        split_lo(n + 1 + 2 * j + 2 * KT * r, (n + 1) % 2)
                        up_evac(2 * KT * r + 4 * j + 2 * u, KT * r + 2 * j + u, 2 * j + u)
                n = N5 + KT
                with dve.Fori(0, KT // 2 - (1 if last else 0)) as j:
                    for u in range(2):
                        split_lo(n + u + 1 + 2 * j + 2 * KT * r, (n + u + 1) % 2)
                        down_evac(n + u + 2 * j + 2 * KT * r, (n + u) % 2, 2 * j + u, 2 * KT * r + 4 * j + 2 * u)
                if last:
                    nl = N5 + 2 * KT * ROUNDS - 1
                    split_lo(nl, nl % 2)
                    for u in range(2):
                        down_evac(nl - 1 + u, (nl - 1 + u) % 2, KT - 2 + u, 2 * KT * ROUNDS - 4 + 2 * u)

            with dve.Fori(0, ROUNDS - 1) as r:
                mlp_round(r, False)
            mlp_round(ROUNDS - 1, True)

            dve.wait_ge(gf_in, 16)
            for t in range(TT):
                dve.wait_ge(fin_ss, t + 1)
                nc.vector.tensor_scalar(msq[:, t:t + 1], ssum[:, t:t + 1], 1.0 / D, EPS, ALU.mult, ALU.add).then_inc(fin_ms, 1)
                dve.wait_ge(fin_rms, t + 1)
                nc.vector.reciprocal(rstd[:, t:t + 1], rms[:, t:t + 1]).then_inc(fin_r, 1)
                dve.wait_ge(fin_r, t + 1)
                if t >= 2:
                    dve.wait_ge(st_out[t % 2], 16 * (t // 2))
                nc.vector.scalar_tensor_tensor(out=ost[:, t % 2], in0=psX[:, 2 * (t % 2):2 * (t % 2) + 2].rearrange("p b n -> p (b n)"),
                                               scalar=rstd[:, t:t + 1], in1=gfb[:], op0=ALU.mult, op1=ALU.mult).then_inc(fin_o, 1)

        @block.tensor
        def _(pe):
            def three(ps, slot, k, w, hi, lo, cols, start, stop):
                nc.tensor.matmul(ps, whi[:, slot, w], hi[:, k, cols], start=start, stop=False)
                nc.tensor.matmul(ps, whi[:, slot, w], lo[:, k, cols], start=False, stop=False)
                return nc.tensor.matmul(ps, wlo[:, slot, w], hi[:, k, cols], start=False, stop=stop)

            def unit(n, slot, hi, lo, bank, before=None):
                pe.wait_ge(w_lo, n + 1)
                for h in range(2):
                    for k in range(KT):
                        if before:
                            before(h, k)
                        last = three(psU[:, bank + h], slot, k, k, hi, lo, slice(h * HALF, (h + 1) * HALF), k == 0, k == KT - 1)
                    last.then_inc(u_done, 1)

            pe.wait_ge(consts, 1)
            pe.wait_ge(const_in, 48)
            nc.tensor.transpose(psU[:, 0, 0:2 * KT + 4], grow[:], ident[0:2 * KT + 4, 0:2 * KT + 4]).then_inc(gain_t, 1)
            pe.wait_ge(gain_ready, 1)

            for t in range(TT):
                pe.wait_ge(xs_ready, t + 1)
                if t >= 2:
                    pe.wait_ge(hraw_ready, t - 1)
                for k in range(KT):
                    last = nc.tensor.transpose(psX[:, 2 * (t % 2) + k // 4, (k % 4) * P:(k % 4 + 1) * P], xt[:, t, k * P:(k + 1) * P], ident[:])
                last.then_inc(xt_ready, 1)

            def proj_before(n, peeled):
                def before(h, k):
                    if k == 0:
                        pe.wait_ge(h_lo, 4 * (h + 1))
                        if peeled >= 2:
                            pe.wait_ge(ev[h], n - 1)
                return before

            for n in range(U_Q):
                unit(n, n % 2, ahi, alo, 2 * (n % 2), proj_before(n, n))
            with pe.Fori(0, (N1 - U_Q) // 2) as j:
                for u in range(2):
                    n = U_Q + u
                    unit(n + 2 * j, n % 2, ahi, alo, 2 * (n % 2), proj_before(n + 2 * j, 2))

            step = [0]

            def bank():
                if step[0] >= 4:
                    pe.wait_ge(misc_ev, step[0] - 3)
                step[0] += 1
                return psX[:, (step[0] - 1) % 4]

            pe.wait_ge(pool_w_in, 16)
            for k in range(4):
                pe.wait_ge(pooled, k + 1)
                for h in range(2):
                    nc.tensor.matmul(bank(), wp[:, k], up[:, k, PAD + h * HALF:PAD + (h + 1) * HALF], start=True, stop=True).then_inc(misc, 1)
            assert step[0] == N_Y
            pe.wait_ge(gate_in, 16)
            b = bank()
            for t in range(TT):
                last = nc.tensor.transpose(b[:, t * NG:(t + 1) * NG], gtd[:, t * P:(t + 1) * P], ident[0:NG, 0:NG])
            last.then_inc(misc, 1)
            for src, s in ((vsd, vs_in), (vwd, vw_in)):
                pe.wait_ge(s, 16)
                for q in range(2):
                    b = bank()
                    for t in range(4):
                        last = nc.tensor.transpose(b[:, t * P:(t + 1) * P], src[:, (4 * q + t) * P:(4 * q + t + 1) * P], ident[:])
                    last.then_inc(misc, 1)
            pe.wait_ge(cw_in, 64)
            b = bank()
            J = CBLOCK // 2
            for br in range(2):
                last = nc.tensor.transpose(b[:, br * J:(br + 1) * J], pet[:, br], ident[0:J, 0:J])
            last.then_inc(misc, 1)
            pe.wait_ge(misc_ev, step[0])
            b = bank()
            for br in range(2):
                for j in range(J):
                    last = nc.tensor.matmul(b[0:HD, br:br + 1], cw1[:, br, j], pe2[:, br, j:j + 1], start=(j == 0), stop=(j == J - 1))
            last.then_inc(misc, 1)
            for br in range(2):
                pe.wait_ge(cc_in, 32 * (br + 1))
                b = bank()
                for j in range(J):
                    rhs = ccd[:, :, 2 * j:2 * j + CSTRIDE * (NCMP - 1) + 1:CSTRIDE]
                    last = nc.tensor.matmul(b[0:HD, 0:GROUPS * NCMP], cw1[:, br, j], rhs, start=(j == 0), stop=(j == J - 1))
                last.then_inc(misc, 1)
                pe.wait_ge(misc_ev, step[0])
                b = bank()
                if br == 0:
                    nc.tensor.matmul(b[:, 0:GROUPS * CP], cw2[:, 0], chid[:, 0].rearrange("p g c -> p (g c)"), start=True, stop=True).then_inc(misc, 1)
                else:
                    for g in range(GROUPS):
                        last = nc.tensor.matmul(b[0:CP, g * HD:(g + 1) * HD], chid[:, 1, g], cw2[:, 1, 0:HD], start=True, stop=True)
                    last.then_inc(misc, 1)
            assert step[0] == N_MISC, step[0]

            def scores(it, r):
                g, i = ITER[it]
                e = it * GR + r
                s = it % 2
                if r == 0:
                    pe.wait_ge(q_lo, it + 1)
                if e >= 1:
                    pe.wait_ge(m_slc, e)
                a, w = n_slc(i), n_win(i)
                for c in range(0, a, HALF):
                    n = min(HALF, a - c)
                    nc.tensor.matmul(psS0[:, c:c + n], qh[:, s, r], kS[:, g, c:c + n], start=True, stop=False)
                    last = nc.tensor.matmul(psS0[:, c:c + n], ql[:, s, r], kS[:, g, c:c + n], start=False, stop=True)
                last.then_inc(s_slc, 1)
                if e >= 1:
                    pe.wait_ge(m_win, e)
                for c in range(0, w, HALF):
                    n = min(HALF, w - c)
                    ks = kW[:, g, a - w + c:a - w + c + n]
                    nc.tensor.matmul(psS1[:, c:c + n], qh[:, s, r], ks, start=True, stop=False)
                    nc.tensor.matmul(psS1[:, c:c + n], ql[:, s, r], ks, start=False, stop=True)
                nc.tensor.matmul(psS1[:, w:w + CP], qh[:, s, r], kC[:, g], start=True, stop=False)
                nc.tensor.matmul(psS1[:, w:w + CP], ql[:, s, r], kC[:, g], start=False, stop=True).then_inc(s_win, 1)

            def turn(it, B, kind, kb):
                g, i = ITER[it]
                if B >= 2:
                    pe.wait_ge(pt_lo, B - 1)
                width = CP if kind == "cmp" else P
                col = prob_col(i, kind, kb)
                for r in range(GR):
                    last = nc.tensor.transpose(psX[0:width, B % 2, r * P:(r + 1) * P], PB[it % 2][:, r, col:col + width], ident[:])
                last.then_inc(t_done, 1)

            def values(it, B, kind, kb):
                g, i = ITER[it]
                first, final = B == first_block[it], B == first_block[it + 1] - 1
                if first and it >= 2:
                    pe.wait_ge(o_ready, it - 1)
                pe.wait_ge(pt_lo, B + 1)
                v = {"slc": vS[:, kb, g], "win": vW[:, kb, g], "cmp": vC[:, g]}[kind]
                rows = CP if kind == "cmp" else P
                nc.tensor.matmul(psX[:, 2 + it % 2], v, pth[0:rows, B % 2], start=first, stop=False)
                nc.tensor.matmul(psX[:, 2 + it % 2], v, ptl[0:rows, B % 2], start=False, stop=final).then_inc(pv_done, 1)

            pe.wait_ge(ev[0], N1)
            pe.wait_ge(ev[1], N1)
            pe.wait_ge(misc_ev, N_MISC)
            pe.wait_ge(k_ready, 2)
            for r in range(GR):
                scores(0, r)
            pending = []
            for it in range(NIT):
                for r in range(GR):
                    if it + 1 < NIT:
                        scores(it + 1, r)
                    if r == 0:
                        pe.wait_ge(p_ready, GR * (it + 1))
                    for B, k, kind, kb in chunk(it, r):
                        turn(it, B, kind, kb)
                        if pending:
                            values(*pending.pop())
                        pending.append((it, B, kind, kb))
                if pending:
                    values(*pending.pop())

            pe.wait_ge(m_slc, GR * NIT)
            pe.wait_ge(m_win, GR * NIT)
            pe.wait_ge(o_ready, NIT)
            pe.wait_ge(misc_ev, N_MISC)

            def merge_tile(n, base, s, first=False):
                for z in range(2):
                    def before(h, k):
                        if k == 0 and not first:
                            pe.wait_ge(z_ready, 2 * s - 3 + 2 * z + h)
                    unit(n + z, (base + z) % 2, ahi, alo, 2 * z, before)
                slot = (base + 2) % 2
                pe.wait_ge(w_lo, n + 3)
                for h in range(2):
                    cols = slice(h * HALF, (h + 1) * HALF)
                    pe.wait_ge(ab_free, 2 if first else s + h + 1)
                    for k in range(4):
                        three(psX[:, h], slot, k, k, ohi, olo, cols, k == 0, k == 3)
                    for k in range(4):
                        last = three(psX[:, 2 + h], slot, k, 4 + k, yhi, ylo, cols, k == 0, k == 3)
                    last.then_inc(u_done, 1)

            merge_tile(N3, N3, 0, True)
            merge_tile(N3 + 3, N3 + 3, 2)
            with pe.Fori(1, KT // 2) as j:
                merge_tile(N3 + 6 * j, N3, 4 * j)
                merge_tile(N3 + 3 + 6 * j, N3 + 3, 4 * j + 2)

            pe.wait_ge(ab_free, 2 + 2 * KT)
            for t in range(TT):
                pe.wait_ge(xr_in[t % 2], 16 * (t // 2 + 1))
                if t >= 2:
                    pe.wait_ge(xT_a, t - 1)
                    pe.wait_ge(xT_v, t - 1)
                for k in range(KT):
                    last = nc.tensor.transpose(psX[:, 2 * (t % 2) + k // 4, (k % 4) * P:(k % 4 + 1) * P], xr[:, t % 2, k * P:(k + 1) * P], ident[:])
                last.then_inc(xr_t, 1)

            pe.wait_ge(z_ready, 4 * KT)

            def out_before(m, first):
                def before(h, k):
                    if h == 0 and first:
                        pe.wait_ge(c_lo, k + 1)
                    if k == 0 and not first:
                        pe.wait_ge(res[h], m - 1)
                return before

            for u in range(2):
                unit(N4 + u, (N4 + u) % 2, ahi, alo, 2 * ((N4 + u) % 2), out_before(u, True))
            with pe.Fori(1, KT // 2) as j:
                for u in range(2):
                    unit(N4 + u + 2 * j, (N4 + u) % 2, ahi, alo, 2 * ((N4 + u) % 2), out_before(2 * j + u, False))

            pe.wait_ge(sq_sum, 2 * KT)
            pe.wait_ge(xT_v, TT)
            pe.wait_ge(xT_a, TT)
            for h in range(2):
                nc.tensor.matmul(psX[:, h], ones[:], sqa[:, h * HALF:(h + 1) * HALF], start=True, stop=True).then_inc(ms_done, 1)

            def up_before(r, t, first):
                def before(h, k):
                    if k == 0 and first:
                        pe.wait_ge(res[h], KT * r + (KT - 1) + t)
                    elif k == 0:
                        pe.wait_ge(relu[h], KT * r + t - 1)
                    if first:
                        pe.wait_ge(h2_lo, 2 * k + h + 1)
                return before

            def down_before(r, m, first):
                def before(h, k):
                    if k == 0 and first:
                        pe.wait_ge(relu[h], KT * r + (KT - 1) + m)
                    elif k == 0:
                        pe.wait_ge(res[h], KT * r + (KT - 1) + m)
                    if first:
                        pe.wait_ge(hid_lo, 2 * KT * r + 2 * k + h + 1)
                return before

            with pe.Fori(0, ROUNDS) as r:
                for which, before, hi, lo in ((0, up_before, h2hi, h2lo), (1, down_before, ahi, alo)):
                    n = N5 + KT * which
                    for u in range(2):
                        unit(n + u + 2 * KT * r, (n + u) % 2, hi, lo, 2 * ((n + u) % 2), before(r, u, True))
                    with pe.Fori(1, KT // 2) as j:
                        for u in range(2):
                            unit(n + u + 2 * j + 2 * KT * r, (n + u) % 2, hi, lo, 2 * ((n + u) % 2), before(r, 2 * j + u, False))

            for h in range(2):
                pe.wait_ge(res[h], KT * (ROUNDS + 1))
            pe.wait_ge(r2_ready, 2)
            for t in range(TT):
                if t >= 2:
                    pe.wait_ge(fin_o, t - 1)
                for k in range(KT):
                    last = nc.tensor.transpose(psX[:, 2 * (t % 2) + k // 4, (k % 4) * P:(k % 4 + 1) * P], xT[:, k, t * P:(t + 1) * P], ident[:])
                last.then_inc(fin_t, 1)


_INS = ['x', 'norm1_g', 'w_in', 'cmp_pe', 'cmp_w1', 'cmp_w2', 'w_attn_proj', 'w_pool', 'pool_scale',
        'w_pool_proj', 'w_out', 'norm2_g', 'w_ff1', 'w_ff2', 'final_g']
_OUTS = [((1, 1024, 1024), 'float32')]


def kernel(**inputs):
    import numpy as _np
    import concourse.bacc as _bacc
    from concourse import mybir as _mybir
    from concourse.bass_utils import run_bass_kernel_spmd as _run

    nc = _bacc.Bacc("TRN2", target_bir_lowering=False, num_devices=1)
    arrays, args = {}, []
    for name in _INS:
        a = _np.ascontiguousarray(inputs[name])
        arrays[f"in_{name}_dram"] = a
        args.append(nc.dram_tensor(f"in_{name}_dram", a.shape, _mybir.dt.from_np(a.dtype), kind="ExternalInput").ap())
    for i, (shape, dtype) in enumerate(_OUTS):
        dt = _mybir.dt.from_np(_np.dtype(dtype))
        args.append(nc.dram_tensor(f"out_{i}_dram", shape, dt, kind="ExternalOutput").ap())
    hybrid_trunk(nc, *args)
    r = _run(nc, [arrays], core_ids=[0])
    got = tuple(r.results[0][f"out_{i}_dram"] for i in range(len(_OUTS)))
    return got[0]
```

```python
import concourse.bass as bass
from concourse import mybir
from contextlib import ExitStack



def hybrid_trunk(nc, x, norm1_g, w_in, cmp_pe, cmp_w1, cmp_w2, w_attn_proj, w_pool, pool_scale,
                 w_pool_proj, w_out, norm2_g, w_ff1, w_ff2, final_g, out):
    f32 = mybir.dt.float32
    f32r = mybir.dt.float32r
    ALU = mybir.AluOpType
    ACT = mybir.ActivationFunctionType

    P = 128
    S, D = x.shape[1], x.shape[2]
    KT = D // P
    TT = S // P
    HALF = 512
    FF = w_ff1.shape[2]
    HEADS, HD, GROUPS = 8, 64, 2
    GR = HEADS // GROUPS
    WIN_TILES = 512 // P
    NCMP, CSTRIDE, CBLOCK = 63, 16, 32
    CP = 64
    NEG = -1e30
    EPS = 1e-6
    O_GATE = HEADS * HD + 3 * 2 * GROUPS * HD
    O_POOL = O_GATE + 3 * HEADS
    O_MERGE = O_POOL + 512
    NG = 3 * HEADS
    PAD = 16

    U_POOL, U_GATE, U_KC, U_VC, U_KS, U_VS, U_KW, U_VW, U_Q = 0, 4, 5, 6, 7, 8, 9, 10, 11
    N1 = 15
    NZ = N1
    N3 = NZ + 2 * KT
    N4 = N3 + KT
    N5 = N4 + KT
    ROUNDS = FF // D
    N_CMP, N_Y = 6, 14
    N_MISC = 19
    GELU_C = 0.7978845608028654

    w_in_u = w_in[0].rearrange("(k p) n -> p k n", p=P)
    w_ap_u = w_attn_proj[0].rearrange("(k p) n -> p k n", p=P)
    w_pp_u = w_pool_proj[0].rearrange("(k p) n -> p k n", p=P)
    w_out_u = w_out[0].rearrange("(k p) n -> p k n", p=P)
    w_ff1_u = w_ff1[0].rearrange("(k p) n -> p k n", p=P)
    w_ff2_u = w_ff2[0].rearrange("(k p) n -> p k n", p=P)

    ctx = ExitStack()
    with ctx:
        def sem(name):
            return ctx.enter_context(nc.semaphore(name))

        START = (nc.sbuf_base + 63) // 64 * 64
        END = nc.sbuf_usable_end
        cursor = [START]

        def size_of(shape):
            n = 4
            for d in shape[1:]:
                n *= d
            return (n + 31) // 32 * 32

        def place(name, shape, dt=f32):
            off = cursor[0]
            cursor[0] += size_of(shape)
            assert cursor[0] <= END, (name, cursor[0] - END)
            return nc.alloc_sbuf_tensor_at(name, shape, dt, offset=off)

        wraw = place("wraw", [P, 2, KT, P])
        whi = place("whi", [P, 2, KT, P], f32r)
        wlo = place("wlo", [P, 2, KT, P], f32r)
        ahi = place("ahi", [P, KT, S], f32r)
        alo = place("alo", [P, KT, S], f32r)
        ident = place("ident", [P, P])
        ones = place("ones", [P, P])
        gcol = place("gcol", [P, 2 * KT + 4])
        g1, g2, psc = gcol[:, 0:KT], gcol[:, KT:2 * KT], gcol[:, 2 * KT:]
        qscale = place("qscale", [P, N1])
        ssum = place("ssum", [P, TT])
        msq = place("msq", [P, TT])
        rms = place("rms", [P, TT])
        rstd = place("rstd", [P, TT])
        gates = place("gates", [P, TT, HEADS, 3])
        cvalid = place("cvalid", [P, 1])
        mx = place("mx", [P, 2, GR, 3])
        nb = place("nb", [P, 2, GR, 3])
        esum = place("esum", [P, 2, GR, 3])
        rs = place("rs", [P, 2, GR, 3])
        ARENA = cursor[0]

        kS = place("kS", [P, GROUPS, S], f32r)
        kW = place("kW", [P, GROUPS, S], f32r)
        kC = place("kC", [P, GROUPS, CP], f32r)
        vS = place("vS", [P, TT, GROUPS, 2 * HD], f32r)
        vW = place("vW", [P, TT, GROUPS, 2 * HD], f32r)
        T1 = place("T1", [P, S])
        TW = place("TW", [P, (WIN_TILES + 1) * P])
        TC = place("TC", [P, TT, CP])
        REGION = cursor[0]
        ORDER = [7, 1, 6, 2, 5, 3, 4, 0]
        ITER = [(g, i) for g in range(GROUPS) for i in ORDER]
        NIT = len(ITER)

        def n_slc(i):
            return (i + 1) * P

        def n_win(i):
            return min(i + 1, WIN_TILES + 1) * P

        def n_row(i):
            return n_slc(i) + n_win(i) + CP

        def blocks(i):
            return [("slc", kb) for kb in range(i + 1)] + \
                   [("win", kb) for kb in range(i + 1 - n_win(i) // P, i + 1)] + [("cmp", 0)]

        PB = [place("prob0", [P, GR, n_row(7)])]
        ostg = place("ostg", [HD, 2, GR * P])
        vC = place("vC", [CP, GROUPS, 2 * HD], f32r)
        QUERIES = cursor[0]
        qraw = place("qraw", [P, 2, GR, P])
        qh = place("qh", [P, 2, GR, P], f32r)
        ql = place("ql", [P, 2, GR, P], f32r)
        STAGE = cursor[0]
        PB.append(place("prob1", [P, GR, n_row(3)]))
        pth = place("pth", [P, 2, GR * P], f32r)
        ptl = place("ptl", [P, 2, GR * P], f32r)
        otmp = place("otmp", [HD, GR * P])
        zst = place("zst", [P, 2, HALF])
        yraw = place("yraw", [P, 4, S])

        cursor[0] = REGION
        xt = place("xt", [P, TT, D])
        after_x = cursor[0]
        cw1 = place("cw1", [P, 2, CBLOCK // 2, HD])
        cw2 = place("cw2", [HD, 2, 2 * HD])
        pet = place("pet", [CBLOCK // 2, 2, 2 * HD])
        chid = place("chid", [HD, 2, GROUPS, CP])
        assert after_x == QUERIES and cursor[0] <= STAGE
        cursor[0] = STAGE
        hraw = place("hraw", [P, 2, KT, P])
        sqj = place("sqj", [P, D])
        grow = place("grow", [2 * KT + 4, P])
        cursor[0] = REGION
        up = place("up", [P, 4, PAD + S])
        tA = place("tA", [P, PAD + S])
        tB = place("tB", [P, PAD + S])
        icnt = place("icnt", [P, 4, PAD])
        wp = place("wp", [P, 4, P])
        gate_t = place("gate_t", [P, TT * NG])
        assert cursor[0] <= after_x
        cursor[0] = STAGE
        stage = place("stage", [P, 2, S])
        ldA = place("ldA", [P, GROUPS, S])
        ldB = place("ldB", [P, GROUPS, S])
        gtd = place("gtd", [NG, S])
        pe2 = place("pe2", [P, 2, CBLOCK // 2])
        cb = place("cb", [HD, 2])
        cu = place("cu", [HD, 2, P])
        cv = place("cv", [HD, P])
        cz = place("cz", [HD, P])
        kcs = place("kcs", [P, P])

        cursor[0] = ARENA
        yhi = place("yhi", [P, 4, S], f32r)
        ohi = place("ohi", [P, 4, S], f32r)
        olo = place("olo", [P, 4, S], f32r)
        ylo = place("ylo", [P, 4, S], f32r)
        RAW = cursor[0]
        xT = place("xT", [P, KT, S])
        TAIL = cursor[0]
        xr = place("xr", [P, 2, D])
        mg = place("mg", [P, 2, 2, HALF])
        mt = place("mt", [P, 2, HALF])
        ct = place("ct", [P, 2, HALF])
        cursor[0] = QUERIES - size_of([P, 2, S])
        oraw = [None, place("oraw1", [P, 2, S])]
        oraw[0] = place("oraw0", [P, 2, S])
        assert RAW <= QUERIES - size_of([P, 2, S]) and cursor[0] <= TAIL
        cursor[0] = ARENA
        h2hi = place("h2hi", [P, KT, S], f32r)
        h2lo = place("h2lo", [P, KT, S], f32r)
        assert cursor[0] == RAW
        cursor[0] = TAIL
        rel = place("rel", [P, 2, HALF])
        rsq = place("rsq", [P, 2, HALF])
        f2t = place("f2t", [P, 2, HALF])
        r2 = place("r2", [P, S])
        sqt = place("sqt", [P, HALF])
        sqa = place("sqa", [P, S])
        cursor[0] = ARENA
        gfb = place("gfb", [P, D])
        sqo = place("sqo", [P, D])
        ost = place("ost", [P, 2, D])

        psU = ctx.enter_context(nc.psum_tensor("psU", [P, 4, HALF], f32))
        psX = ctx.enter_context(nc.psum_tensor("psX", [P, 4, HALF], f32))
        psS0 = psU[:, 0:2, :].rearrange("p b n -> p (b n)")
        psS1 = psU[:, 2:4, :].rearrange("p b n -> p (b n)")

        proj = nc.dram_tensor("proj_scratch", [N1 * P, S], f32).ap()
        oscr = nc.dram_tensor("attn_scratch", [HEADS * HD, S], f32).ap()
        zscr = nc.dram_tensor("gate_scratch", [2 * D, S], f32).ap()

        x_in = [sem(f"x_in{t}") for t in range(TT)]
        const_in, gain_t, gain_ready = sem("const_in"), sem("gain_t"), sem("gain_ready")
        w_raw = [sem("w_raw0"), sem("w_raw1")]
        w_hi, w_lo = sem("w_hi"), sem("w_lo")
        u_done = sem("u_done")
        ev = [sem("ev0"), sem("ev1")]
        consts = sem("consts")
        chain_p, chain_v = sem("chain_p"), sem("chain_v")
        ss_ready, ms_ready, rms_ready, rstd_ready = sem("ss_ready"), sem("ms_ready"), sem("rms_ready"), sem("rstd_ready")
        xs_ready, xt_ready, hraw_ready, h_hi, h_lo = sem("xs_ready"), sem("xt_ready"), sem("hraw_ready"), sem("h_hi"), sem("h_lo")
        st_proj = [sem("st_proj0"), sem("st_proj1")]
        u_in, pool_w_in, pooled = sem("u_in"), sem("pool_w_in"), sem("pooled")
        gate_in, vs_in, vw_in, ks_in, kw_in = sem("gate_in"), sem("vs_in"), sem("vw_in"), sem("ks_in"), sem("kw_in")
        icnt_ready, pad_ready = sem("icnt_ready"), sem("pad_ready")
        st_z = [sem("st_z0"), sem("st_z1")]
        cw_in, kc_in, vc_in = sem("cw_in"), sem("kc_in"), sem("vc_in")
        misc, misc_ev = sem("misc"), sem("misc_ev")
        k_hi, v_hi, gate_tanh = sem("k_hi"), sem("v_hi"), sem("gate_tanh")
        gelu_arg, gelu_tanh = sem("gelu_arg"), sem("gelu_tanh")
        k_ready = sem("k_ready")
        q_in = [sem("q_in0"), sem("q_in1")]
        q_hi, q_lo = sem("q_hi"), sem("q_lo")
        s_slc, s_win, m_slc, m_win = sem("s_slc"), sem("s_win"), sem("m_slc"), sem("m_win")
        nb_ready, exp_done, p_ready = sem("nb_ready"), sem("exp_done"), sem("p_ready")
        t_done, pt_hi, pt_lo, pv_done = sem("t_done"), sem("pt_hi"), sem("pt_lo"), sem("pv_done")
        o_half, o_ready = sem("o_half"), sem("o_ready")
        st_o = [sem("st_o0"), sem("st_o1")]
        o_in, yo_hi, yo_lo, z_ready = [sem("o_in0"), sem("o_in1")], sem("yo_hi"), sem("yo_lo"), sem("z_ready")
        mg_in = [sem("mg_in0"), sem("mg_in1")]
        ab_read, c_sum = sem("ab_read"), sem("c_sum")
        xr_in = [sem("xr_in0"), sem("xr_in1")]
        xr_t, xT_a, xT_v, c_hi, c_lo = sem("xr_t"), sem("xT_a"), sem("xT_v"), sem("c_hi"), sem("c_lo")
        res = [sem("res0"), sem("res1")]
        relu = [sem("relu0"), sem("relu1")]
        h2_hi, h2_lo = sem("h2_hi"), sem("h2_lo")
        sq_sum, ms_done, r2_ready, mul_r2 = sem("sq_sum"), sem("ms_done"), sem("r2_ready"), sem("mul_r2")
        rsq_ready, hid_hi, hid_lo = sem("rsq_ready"), sem("hid_hi"), sem("hid_lo")
        gf_in, fin_t, fin_ss, fin_ms, fin_rms, fin_r, fin_o = (sem("gf_in"), sem("fin_t"), sem("fin_ss"),
                                                             sem("fin_ms"), sem("fin_rms"), sem("fin_r"), sem("fin_o"))
        st_out = [sem("st_out0"), sem("st_out1")]

        def raw_need(n):
            twice = [c for c in range(N3, N4 + 1) if c <= n and c % 2 == n % 2]
            return 16 * (n // 2 + 1) + 16 * len(twice)

        def proj_col(n):
            return O_POOL + P * n if n < U_GATE else O_GATE if n == U_GATE else O_GATE - 6 * P + P * (n - U_KC) if n < U_Q \
                else P * (n - U_Q)

        first_block = [0]
        for g, i in ITER:
            first_block.append(first_block[-1] + len(blocks(i)))

        BLOCK_SHARE = (0, 4, 8, 12, 16)
        GATE_SHARE = (0, 4, 8, 12, 16)
        W_POS = 1

        def chunk(it, r):
            b = blocks(ITER[it][1])
            lo, hi = [round(len(b) * c / 16) for c in BLOCK_SHARE[r:r + 2]]
            return [(first_block[it] + k, k, *b[k]) for k in range(lo, hi)]

        Z_STEPS = 2 * KT - 2

        def branch_cols(i):
            a, b = n_slc(i), n_slc(i) + n_win(i)
            return (0, a), (a, b), (b, b + CP)

        def prob_col(i, kind, kb):
            if kind == "slc":
                return kb * P
            if kind == "win":
                return n_slc(i) + (kb - (i + 1 - n_win(i) // P)) * P
            return n_slc(i) + n_win(i)

        def fin_bank(t):
            return (psX, psU)[t // 2 % 2][:, 2 * (t % 2):2 * (t % 2) + 2].rearrange("p b n -> p (b n)")

        block = ctx.enter_context(nc.Block())

        @block.sync
        def _(sp):
            def load(n, src, slot):
                sp.wait_ge(w_hi, n - 1)
                sp.wait_ge(w_lo, n - 1)
                sp.dma_start(wraw[:, slot], src).then_inc(w_raw[slot], 16)

            for lo, src in ((0, norm1_g), (KT, norm2_g), (2 * KT, pool_scale)):
                rows = src[0].rearrange("(k p) -> k p", p=P)
                sp.dma_start(grow[lo:lo + rows.shape[0]], rows).then_inc(const_in, 16)
            for t in range(4):
                sp.dma_start(xt[:, t, :], x[0, t * P:(t + 1) * P, :]).then_inc(x_in[t], 16)
            sp.dma_start(wraw[:, 0], w_in_u[:, :, bass.ds(proj_col(0), P)]).then_inc(w_raw[0], 16)
            for t in range(4, TT):
                sp.dma_start(xt[:, t, :], x[0, t * P:(t + 1) * P, :]).then_inc(x_in[t], 16)
            sp.dma_start(wraw[:, 1], w_in_u[:, :, bass.ds(proj_col(1), P)]).then_inc(w_raw[1], 16)
            sp.dma_start(cw1[:], cmp_w1[0].rearrange("b (j l) d h -> (l d) b j h", l=2)).then_inc(cw_in, 16)
            sp.dma_start(cw2[:, :, 0:HD], cmp_w2[0].rearrange("b h e -> h b e")).then_inc(cw_in, 16)
            sp.dma_start(cw2[:, :, HD:], cmp_w2[0].rearrange("b h e -> h b e")).then_inc(cw_in, 16)
            sp.dma_start(pet[:], cmp_pe[0].rearrange("b (j l) d -> j b (l d)", l=2)).then_inc(cw_in, 16)

            def load_unit(n):
                if n < N1:
                    load(n, w_in_u[:, :, bass.ds(proj_col(n), P)], n % 2)
                elif n < N3:
                    q = n - NZ
                    load(n, w_in_u[:, :, bass.ds(O_MERGE + (q % 2) * D + (q // 2) * P, P)], n % 2)
                else:
                    load_ab(n, n % 2, n - N3)

            def load_parts(n, slot, low, high):
                sp.wait_ge(w_hi, n - 1)
                sp.wait_ge(w_lo, n - 1)
                sp.dma_start(wraw[:, slot, 0:4], low).then_inc(w_raw[slot], 16)
                sp.dma_start(wraw[:, slot, 4:8], high).then_inc(w_raw[slot], 16)

            def load_ab(n, slot, m):
                load_parts(n, slot, w_ap_u[:, :, bass.ds(P * m, P)], w_pp_u[:, :, bass.ds(P * m, P)])

            def rows(unit):
                sp.wait_ge(st_proj[unit % 2], 16 * (unit // 2 + 1))
                return proj[unit * P:(unit + 1) * P, :]

            def load_shifted(dst, unit, s):
                src = rows(unit).rearrange("(g d) t -> d g t", d=HD)
                sp.dma_start(dst[0:HD], src).then_inc(s, 16)
                sp.dma_start(dst[HD:P, :, 0:S - 1], src[:, :, 1:S]).then_inc(s, 16)

            def load_twice(dst, unit, s):
                src = rows(unit).rearrange("(g d) t -> d g t", d=HD)
                for side in range(2):
                    sp.dma_start(dst[side * HD:(side + 1) * HD], src).then_inc(s, 16)

            def load_q(it):
                g, i = ITER[it]
                if it >= 2:
                    sp.wait_ge(q_lo, it - 1)
                src = proj[U_Q * P + g * GR * HD:U_Q * P + (g + 1) * GR * HD, i * P:(i + 1) * P]
                for side in range(2):
                    sp.dma_start(qraw[side * HD:(side + 1) * HD, it % 2], src.rearrange("(r d) t -> d r t", d=HD)) \
                        .then_inc(q_in[it % 2], 16)

            load_unit(2)
            load_unit(3)
            for n in range(N1):
                sp.wait_ge(ev[0], n + 1)
                sp.wait_ge(ev[1], n + 1)
                sp.dma_start(proj[n * P:(n + 1) * P, :], stage[:, n % 2]).then_inc(st_proj[n % 2], 16)
                if n == U_GATE:
                    for unit in range(4):
                        src = rows(unit)
                    sp.wait_ge(pad_ready, 1)
                    sp.dma_start(up[:, :, PAD:], proj[0:4 * P, :].rearrange("(k p) t -> p k t", p=P)).then_inc(u_in, 16)
                    sp.dma_start(wp[:], w_pool[0].rearrange("g c d -> c g d")).then_inc(pool_w_in, 16)
                if n == U_KC:
                    sp.dma_start(gtd[:], rows(U_GATE)[0:NG]).then_inc(gate_in, 16)
                if n == U_VC:
                    load_shifted(ldA, U_KC, kc_in)
                if n == U_KS:
                    load_shifted(ldB, U_VC, vc_in)
                if n == 9:
                    sp.wait_ge(misc, 3)
                    sp.dma_start(ldA[:, 0], rows(U_VS)).then_inc(vs_in, 16)
                if n == 10:
                    sp.wait_ge(misc, 5)
                    load_twice(ldB, U_KS, ks_in)
                if n == 11:
                    sp.dma_start(ldA[:, 1], rows(U_VW)).then_inc(vw_in, 16)
                load_unit(n + 4)
                if n == 12:
                    sp.wait_ge(misc, N_MISC)
                    load_twice(ldA, U_KW, kw_in)
                    for unit in (U_Q, U_Q + 1):
                        src = rows(unit)
                    sp.wait_ge(misc_ev, N_MISC)
                    load_q(0)
                    load_q(1)

            def store_z(q, h):
                sp.wait_ge(z_ready, 2 * q + h + 1)
                sp.dma_start(zscr[q * P:(q + 1) * P, h * HALF:(h + 1) * HALF], zst[:, h]).then_inc(st_z[h], 16)

            def store_o(it):
                g, i = ITER[it]
                sp.wait_ge(o_ready, it + 1)
                dst = oscr[g * GR * HD:(g + 1) * GR * HD, i * P:(i + 1) * P].rearrange("(r d) t -> d r t", d=HD)
                sp.dma_start(dst, ostg[:, it % 2].rearrange("d (r t) -> d r t", r=GR)).then_inc(st_o[it % 2], 16)

            for s in range(2):
                sp.wait_ge(st_proj[s], 16 * ((N1 + 1 - s) // 2))
            store_z(0, 0)
            store_z(0, 1)
            for it in range(NIT):
                if 1 <= it <= Z_STEPS:
                    store_z(it, 1)
                if it >= 1:
                    store_o(it - 1)
                if it + 2 < NIT:
                    load_q(it + 2)
                if it < Z_STEPS:
                    load_unit(NZ + it + 4)
                    store_z(it + 1, 0)
            def load_o(g):
                for s in range(2):
                    sp.wait_ge(st_o[s], 16 * (NIT // GROUPS // 2) * (g + 1))
                sp.dma_start(oraw[g][:], oscr[g * 2 * P:(g + 1) * 2 * P, :].rearrange("(k p) t -> p k t", p=P)).then_inc(o_in[g], 16)

            zscr_m = zscr.rearrange("(m z p) t -> m p z t", z=2, p=P)

            def load_gates(m, peeled):
                for h in range(2):
                    if not peeled:
                        sp.wait_ge(ab_read, 2 * m + h - 1)
                    sp.dma_start(mg[:, h], zscr_m[bass.ds(m, 1), :, :, h * HALF:(h + 1) * HALF]
                                 .rearrange("a p z t -> p (a z) t")).then_inc(mg_in[h], 16)

            def load_x(t, peeled, slot):
                if not peeled:
                    sp.wait_ge(xr_t, t - 1)
                sp.dma_start(xr[:, slot], x[0, bass.ds(P * t, P), :]).then_inc(xr_in[slot], 16)

            sp.wait_ge(s_win, GR * NIT)
            load_o(0)
            sp.wait_ge(pv_done, first_block[NIT])
            load_x(0, True, 0)
            load_x(1, True, 1)
            store_o(NIT - 1)
            load_o(1)
            load_ab(N3 + 2, N3 % 2, 2)
            load_gates(0, True)
            for h in range(2):
                store_z(2 * KT - 1, h)
            load_x(2, False, 0)
            load_ab(N3 + 3, (N3 + 1) % 2, 3)
            load_gates(1, False)
            with sp.Fori(1, KT // 2 - 1) as j:
                for u in range(2):
                    load_x(2 * j + u + 1, False, (u + 1) % 2)
                    load_ab(N3 + u + 2 + 2 * j, (N3 + u) % 2, 2 * j + u + 2)
                    load_gates(2 * j + u, False)
            load_x(KT - 1, False, (KT - 1) % 2)
            load_parts(N4, N4 % 2, w_out_u[:, 0:4, 0:P], w_out_u[:, 4:8, 0:P])
            load_gates(KT - 2, False)
            load(N4 + 1, w_out_u[:, :, P:2 * P], (N4 + 1) % 2)
            for h in range(2):
                sp.wait_ge(st_z[h], 16 * 2 * KT)
            load_gates(KT - 1, False)
            with sp.Fori(1, KT // 2) as j:
                for u in range(2):
                    load(N4 + u + 2 * j, w_out_u[:, :, bass.ds(P * (2 * j) + P * u, P)], (N4 + u) % 2)

            with sp.Fori(0, ROUNDS) as r:
                with sp.Fori(0, KT // 2) as j:
                    for u in range(2):
                        load(N5 + u + 2 * j + 2 * KT * r, w_ff1_u[:, :, bass.ds(D * r + P * 2 * j + P * u, P)], (N5 + u) % 2)
                with sp.Fori(0, KT // 2) as j:
                    for u in range(2):
                        load(N5 + KT + u + 2 * j + 2 * KT * r,
                             w_ff2_u[:, bass.ds(KT * r, KT), bass.ds(P * 2 * j + P * u, P)], (N5 + u) % 2)

            sp.wait_ge(u_done, 2 * (N5 + 2 * KT * ROUNDS))
            sp.dma_start(gfb[:], final_g.partition_broadcast(P)).then_inc(gf_in, 16)
            for t in range(TT):
                sp.wait_ge(fin_o, t + 1)
                sp.dma_start(out[0, t * P:(t + 1) * P, :], ost[:, t % 2]).then_inc(st_out[t % 2], 16)
            for s in range(2):
                sp.wait_ge(st_out[s], 16 * TT // 2)

        @block.gpsimd
        def _(pool):
            count = [0]

            def link(ins):
                count[0] += 1
                ins.then_inc(chain_p, 1)
                pool.wait_ge(chain_p, count[0])

            link(pool.memset(ident[:], 0.0))
            link(pool.affine_select(out=ident[:], in_=ident[:], compare_op=ALU.not_equal, fill=1.0, base=0,
                                    pattern=[[-1, P]], channel_multiplier=1))
            pool.memset(ones[:], 1.0)
            link(pool.memset(qscale[:], 1.0))
            for j in range(4):
                for side in range(2):
                    last = pool.memset(qscale[side * HD:(side + 1) * HD, U_Q + j:U_Q + j + 1],
                                       2.0 ** (2 * j + side + 1) * HD ** -0.5)
            last.then_inc(consts, 1)

            def h_low(t):
                pool.wait_ge(h_hi, t + 1)
                nc.gpsimd.tensor_tensor(alo[:, :, t * P:(t + 1) * P], hraw[:, t % 2],
                                        ahi[:, :, t * P:(t + 1) * P].bitcast(f32), ALU.subtract).then_inc(h_lo, 1)

            for t in range(TT):
                h_low(t)

            pool.iota(T1[:], pattern=[[1, S]], base=-(S - P), channel_multiplier=-1,
                      allow_small_or_imprecise_dtypes=True)
            pool.iota(TW[:], pattern=[[1, (WIN_TILES + 1) * P]], base=-WIN_TILES * P, channel_multiplier=-1,
                      allow_small_or_imprecise_dtypes=True)
            link(pool.iota(TC[:], pattern=[[-P, TT], [CSTRIDE, CP]], base=CBLOCK - 1, channel_multiplier=-1,
                           allow_small_or_imprecise_dtypes=True))
            pool.affine_select(out=T1[:], in_=T1[:], compare_op=ALU.is_ge, fill=NEG, base=S - P,
                               pattern=[[-1, S]], channel_multiplier=1)
            link(pool.affine_select(out=TW[:], in_=TW[:], compare_op=ALU.is_ge, fill=NEG, base=WIN_TILES * P,
                                    pattern=[[-1, (WIN_TILES + 1) * P]], channel_multiplier=1))
            link(pool.affine_select(out=TC[:], in_=TC[:], compare_op=ALU.is_ge, fill=NEG, base=-(CBLOCK - 1),
                                    pattern=[[P, TT], [-CSTRIDE, CP]], channel_multiplier=1))
            link(pool.affine_select(out=TW[:, 0:P], in_=TW[:, 0:P], compare_op=ALU.is_gt, fill=NEG, base=0,
                                    pattern=[[1, P]], channel_multiplier=-1))
            link(pool.memset(TC[:, :, NCMP:CP], NEG))
            link(pool.memset(cvalid[:], 1.0))
            link(pool.affine_select(out=cvalid[:], in_=cvalid[:], compare_op=ALU.is_ge, fill=0.0, base=-(CBLOCK - 1),
                                    pattern=[[0, 1]], channel_multiplier=1))
            pool.memset(up[:, :, 0:PAD], 0.0)
            pool.memset(tA[:, 0:PAD], 0.0)
            pool.memset(tB[:, 0:PAD], 0.0)
            link(pool.iota(icnt[:], pattern=[[0, 4], [1, PAD]], base=1, channel_multiplier=0,
                           allow_small_or_imprecise_dtypes=True))
            for k in range(4):
                last = pool.tensor_scalar(icnt[:, k], icnt[:, k], float(2 ** (k + 1)), None, ALU.min)
            last.then_inc(pad_ready, 1)
            pool.memset(chid[:, :, :, NCMP:CP], 0.0).then_inc(consts, 1)

            for m in range(KT):
                for h in range(2):
                    s = 2 * m + h
                    pool.wait_ge(res[h], m + 1)
                    xs = xT[:, m, h * HALF:(h + 1) * HALF]
                    if m == 0:
                        pool.tensor_tensor(sqa[:, h * HALF:(h + 1) * HALF], xs, xs, ALU.mult).then_inc(sq_sum, 1)
                    else:
                        link(pool.tensor_tensor(sqt[:], xs, xs, ALU.mult))
                        pool.wait_ge(sq_sum, s)
                        pool.tensor_tensor(sqa[:, h * HALF:(h + 1) * HALF], sqa[:, h * HALF:(h + 1) * HALF], sqt[:],
                                           ALU.add).then_inc(sq_sum, 1)
                        pool.wait_ge(sq_sum, s + 1)

        @block.scalar
        def _(act):
            def split_hi(n, slot, raw_count, first=False):
                act.wait_ge(w_raw[slot], raw_count)
                if not first:
                    act.wait_ge(u_done, 2 * (n - 1))
                nc.scalar.activation(whi[:, slot], wraw[:, slot], ACT.Copy).then_inc(w_hi, 1)

            def root(t):
                act.wait_ge(ms_ready, t + 1)
                nc.scalar.activation(rms[:, t:t + 1], msq[:, t:t + 1], ACT.Sqrt).then_inc(rms_ready, 1)

            def h_high(t):
                act.wait_ge(hraw_ready, t + 1)
                nc.scalar.activation(ahi[:, :, t * P:(t + 1) * P], hraw[:, t % 2], ACT.Copy).then_inc(h_hi, 1)

            for t in range(TT):
                act.wait_ge(x_in[t], 16)
                if t:
                    act.wait_ge(ss_ready, t)
                nc.scalar.activation(sqj[:], xt[:, t, :], ACT.Square, accum_out=ssum[:, t:t + 1]).then_inc(ss_ready, 1)
                if t >= 1:
                    root(t - 1)
                if t == 2:
                    split_hi(0, 0, 16, first=True)
                if t >= 3:
                    h_high(t - 3)
            root(TT - 1)
            for t in range(TT - 3, TT):
                h_high(t)

            def evac_proj(n, slot, col, reuse=None):
                act.wait_ge(u_done, 2 * n + 1)
                if reuse is not None:
                    act.wait_ge(st_proj[slot], reuse)
                nc.scalar.activation(stage[:, slot, 0:HALF], psU[:, 2 * slot], ACT.Copy, scale=qscale[:, col]).then_inc(ev[0], 1)

            act.wait_ge(consts, 1)
            act.wait_ge(h_lo, TT)
            step = [0]

            def wait_misc(s):
                assert s == step[0] + 1, (s, step)
                step[0] = s
                act.wait_ge(misc, s)

            def gelu_tanh_of(b):
                act.wait_ge(gelu_arg, b + 1)
                nc.scalar.activation(cz[:, 0:GROUPS * NCMP], cv[:, 0:GROUPS * NCMP], ACT.Tanh, scale=GELU_C).then_inc(gelu_tanh, 1)

            def value_hi(s, vt, q):
                act.wait_ge(misc, s)
                ps = psX[:, (s - 1) % 4].rearrange("p (t g d) -> p t g d", t=4, g=GROUPS)
                nc.scalar.activation(vt[:, 4 * q:4 * q + 4, :, 0:HD], ps, ACT.Copy).then_inc(v_hi, 1)

            def key_hi(dst, src, s):
                act.wait_ge(s, 32)
                nc.scalar.activation(dst[:], src[:], ACT.Copy).then_inc(k_hi, 1)

            def query_hi(it):
                act.wait_ge(q_in[it % 2], 32 * (it // 2 + 1))
                if it >= 2:
                    act.wait_ge(s_win, GR * (it - 1))
                nc.scalar.activation(qh[:, it % 2], qraw[:, it % 2], ACT.Copy).then_inc(q_hi, 1)

            for n in range(N1):
                split_hi(n + 1, (n + 1) % 2, raw_need(n + 1), first=(n == 0))
                if n == N1 - 1:
                    query_hi(0)
                    query_hi(1)
                evac_proj(n, n % 2, slice(n, n + 1), 16 * (n // 2) if n >= 2 else None)
                if n == 8:
                    gelu_tanh_of(0)
                if n == 9:
                    gelu_tanh_of(1)
                if n == 11:
                    value_hi(15, vS, 0)
                    value_hi(16, vS, 1)
                    key_hi(kS, ldB, ks_in)
                if n == 12:
                    act.wait_ge(misc, 17)
                    nc.scalar.activation(gate_t[:], psX[:, 16 % 4, 0:TT * NG], ACT.Tanh, scale=0.5).then_inc(gate_tanh, 1)
                    value_hi(18, vW, 0)
                    value_hi(19, vW, 1)
                if n == 13:
                    key_hi(kW, ldA, kw_in)

            def exponentials(it, r, k):
                g, i = ITER[it]
                lo, hi = branch_cols(i)[k]
                if k == 0:
                    act.wait_ge(nb_ready, it * GR + r + 1)
                nc.scalar.activation(PB[it % 2][:, r, lo:hi], PB[it % 2][:, r, lo:hi], ACT.Exp,
                                     scale=2.0 ** -(g * GR + r + 1), bias=nb[:, it % 2, r, k:k + 1],
                                     accum_out=esum[:, it % 2, r, k:k + 1]).then_inc(exp_done, 1)

            def prob_hi(B, kind):
                rows = CP if kind == "cmp" else P
                act.wait_ge(t_done, B + 1)
                if B >= 2:
                    act.wait_ge(pv_done, B - 1)
                nc.scalar.activation(pth[0:rows, B % 2], psX[0:rows, B % 2], ACT.Copy).then_inc(pt_hi, 1)

            def out_half(it):
                act.wait_ge(pv_done, first_block[it + 1])
                if it >= 1:
                    act.wait_ge(o_ready, it)
                nc.scalar.activation(otmp[:], psX[HD:P, 2], ACT.Copy).then_inc(o_half, 1)

            def gate_hi(q, h):
                act.wait_ge(u_done, 2 * (NZ + q) + h + 1)
                if q:
                    act.wait_ge(st_z[h], 16 * q)
                nc.scalar.activation(zst[:, h], psX[:, 3], ACT.Tanh, scale=0.5).then_inc(z_ready, 1)

            split_hi(NZ + 1, (NZ + 1) % 2, raw_need(NZ + 1))
            for r in range(GR):
                for k in range(3):
                    exponentials(0, r, k)
                if r == 0:
                    gate_hi(0, 0)
            gate_hi(0, 1)
            for it in range(NIT):
                for r in range(GR):
                    if r == 0 and 1 <= it <= Z_STEPS:
                        gate_hi(it, 1)
                    if r == 0 and it < Z_STEPS:
                        split_hi(NZ + it + 2, (NZ + it) % 2, raw_need(NZ + it + 2))
                    if r == 2 and it < Z_STEPS:
                        gate_hi(it + 1, 0)
                    if r == 2 and it + 2 < NIT:
                        query_hi(it + 2)
                    todo = chunk(it, r)
                    for k in range(max(len(todo), 3)):
                        if k < len(todo):
                            prob_hi(todo[k][0], todo[k][2])
                        if k < 3 and it + 1 < NIT:
                            exponentials(it + 1, r, k)
                out_half(it)

            def part_hi(dst, src):
                nc.scalar.activation(dst, src, ACT.Copy).then_inc(yo_hi, 1)

            split_hi(N3, N3 % 2, raw_need(N3))
            for h in range(2):
                part_hi(yhi[:, :, h * HALF:(h + 1) * HALF], yraw[:, :, h * HALF:(h + 1) * HALF])
            gate_hi(2 * KT - 1, 0)
            act.wait_ge(o_in[0], 16)
            part_hi(ohi[:, 0:2], oraw[0][:])
            act.wait_ge(o_in[1], 16)
            for h in range(2):
                part_hi(ohi[:, 2:4, h * HALF:(h + 1) * HALF], oraw[1][:, :, h * HALF:(h + 1) * HALF])
            gate_hi(2 * KT - 1, 1)
            act.wait_ge(yo_lo, 5)

            def mixed(n, slot, m, t_slot, need, tile):
                split_hi(n + 1, (slot + 1) % 2, need)
                act.wait_ge(xr_t, m + 1)
                nc.scalar.activation(xT[:, 0:4, bass.ds(P * m, P)],
                                     psX[:, 2 * t_slot].rearrange("p (k t) -> p k t", k=4), ACT.Copy).then_inc(xT_a, 1)
                for h in range(2):
                    act.wait_ge(c_sum, 2 * m + h + 1)
                    nc.scalar.activation(ahi[:, bass.ds(m, 1), h * HALF:(h + 1) * HALF], ct[:, h:h + 1], ACT.Copy,
                                         scale=0.5).then_inc(c_hi, 1)

            with act.Fori(0, KT // 2) as j:
                for u in range(2):
                    n = N3 + u
                    mixed(n + 2 * j, n % 2, 2 * j + u, u, 32 * j + raw_need(n + 1), None)

            def out_evac(m):
                for h in range(2):
                    act.wait_ge(res[h], m + 1)
                    nc.scalar.activation(h2hi[:, bass.ds(m, 1), h * HALF:(h + 1) * HALF], xT[:, bass.ds(m, 1), h * HALF:(h + 1) * HALF],
                                         ACT.Copy, scale=g2[:, bass.ds(m, 1)]).then_inc(h2_hi, 1)

            with act.Fori(0, KT // 2) as j:
                for u in range(2):
                    n = N4 + u
                    split_hi(n + 1 + 2 * j, (n + 1) % 2, 16 * j + raw_need(n + 1))
                    out_evac(2 * j + u)

            def up_evac(n, u, s, t):
                for h in range(2):
                    act.wait_ge(u_done, 2 * n + h + 1)
                    nc.scalar.activation(rel[:, h], psU[:, 2 * u + h], ACT.Relu).then_inc(relu[h], 1)
                for h in range(2):
                    act.wait_ge(rsq_ready, s + h + 1)
                    nc.scalar.activation(ahi[:, bass.ds(t, 1), h * HALF:(h + 1) * HALF], rsq[:, h:h + 1], ACT.Copy).then_inc(hid_hi, 1)

            def mlp_round(r, last):
                with act.Fori(0, KT // 2) as j:
                    for u in range(2):
                        n = N5 + u
                        split_hi(n + 1 + 2 * j + 2 * KT * r, (n + 1) % 2, 16 * j + 16 * KT * r + raw_need(n + 1))
                        up_evac(n + 2 * j + 2 * KT * r, u, 2 * KT * r + 4 * j + 2 * u, 2 * j + u)
                n = N5 + KT
                with act.Fori(0, KT // 2 - (1 if last else 0)) as j:
                    for u in range(2):
                        split_hi(n + u + 1 + 2 * j + 2 * KT * r, (n + u + 1) % 2,
                                 16 * j + 16 * KT * r + raw_need(n + u + 1))
                if last:
                    nl = N5 + 2 * KT * ROUNDS - 1
                    split_hi(nl, nl % 2, raw_need(nl))

            with act.Fori(0, ROUNDS - 1) as r:
                mlp_round(r, False)
            mlp_round(ROUNDS - 1, True)

            act.wait_ge(u_done, 2 * (N5 + 2 * KT * ROUNDS))
            def root_f(t):
                act.wait_ge(fin_ms, t + 1)
                nc.scalar.activation(rms[:, t:t + 1], msq[:, t:t + 1], ACT.Sqrt).then_inc(fin_rms, 1)

            for t in range(TT):
                act.wait_ge(fin_t, t + 1)
                if t:
                    act.wait_ge(fin_ss, t)
                nc.scalar.activation(sqo[:], fin_bank(t), ACT.Square, accum_out=ssum[:, t:t + 1]).then_inc(fin_ss, 1)
                if t:
                    root_f(t - 1)
            root_f(TT - 1)

        @block.vector
        def _(dve):
            count = [0]

            def link(ins):
                count[0] += 1
                ins.then_inc(chain_v, 1)
                dve.wait_ge(chain_v, count[0])

            def split_lo(n, slot):
                dve.wait_ge(w_hi, n + 1)
                nc.vector.tensor_tensor(wlo[:, slot], wraw[:, slot], whi[:, slot].bitcast(f32), ALU.subtract).then_inc(w_lo, 1)

            def mean_sq(t):
                dve.wait_ge(ss_ready, t + 1)
                nc.vector.tensor_scalar(msq[:, t:t + 1], ssum[:, t:t + 1], 1.0 / D, EPS, ALU.mult, ALU.add).then_inc(ms_ready, 1)

            def normalize(t):
                dve.wait_ge(rms_ready, t + 1)
                nc.vector.reciprocal(rstd[:, t:t + 1], rms[:, t:t + 1]).then_inc(rstd_ready, 1)
                dve.wait_ge(rstd_ready, t + 1)
                nc.vector.tensor_scalar(xt[:, t, :], xt[:, t, :], rstd[:, t:t + 1], None, ALU.mult).then_inc(xs_ready, 1)

            def gain(t):
                dve.wait_ge(xt_ready, t + 1)
                if t >= 2:
                    dve.wait_ge(h_lo, t - 1)
                for q in range(2):
                    last = nc.vector.tensor_tensor(hraw[:, t % 2, 4 * q:4 * q + 4], psX[:, 2 * (t % 2) + q].rearrange("p (k t) -> p k t", k=4),
                                                   g1[:, 4 * q:4 * q + 4].unsqueeze(2).broadcast_to([P, 4, P]), ALU.mult)
                last.then_inc(hraw_ready, 1)

            dve.wait_ge(gain_t, 1)
            nc.vector.tensor_copy(gcol[:], psU[:, 0, 0:2 * KT + 4]).then_inc(gain_ready, 1)
            dve.wait_ge(gain_ready, 1)
            mean_sq(0)
            for t in range(TT):
                if t + 1 < TT:
                    mean_sq(t + 1)
                normalize(t)
                if t == 2:
                    split_lo(0, 0)
                if t >= 1:
                    gain(t - 1)
            gain(TT - 1)

            def evac_proj(n, slot, col, reuse=None):
                dve.wait_ge(u_done, 2 * n + 2)
                if reuse is not None:
                    dve.wait_ge(st_proj[slot], reuse)
                nc.vector.tensor_scalar(stage[:, slot, HALF:], psU[:, 2 * slot + 1], qscale[:, col], None, ALU.mult).then_inc(ev[1], 1)

            dve.wait_ge(h_lo, TT)
            step = [0]

            def wait_misc():
                step[0] += 1
                dve.wait_ge(misc, step[0])
                return psX[:, (step[0] - 1) % 4]

            def pool_mix(k):
                cur, bufs = up[:, k], [tA, tB]
                for d in range(k + 1):
                    nxt = bufs[d % 2]
                    link(nc.vector.tensor_tensor(nxt[:, PAD:], cur[:, PAD:], cur[:, PAD - 2 ** d:PAD + S - 2 ** d], ALU.add))
                    cur = nxt
                dst = bufs[(k + 1) % 2]
                nc.vector.tensor_tensor(dst[:, PAD:2 * PAD], cur[:, PAD:2 * PAD], icnt[:, k], ALU.mult)
                link(nc.vector.tensor_scalar(dst[:, 2 * PAD:], cur[:, 2 * PAD:], 2.0 ** -(k + 1), None, ALU.mult))
                nc.vector.tensor_tensor(up[:, k, PAD:], dst[:, PAD:], up[:, k, PAD:], ALU.subtract).then_inc(pooled, 1)
                dve.wait_ge(pooled, k + 1)

            def take_y(s):
                k, h = s // 2, s % 2
                ps = wait_misc()
                nc.vector.tensor_scalar(yraw[:, k, h * HALF:(h + 1) * HALF], ps, psc[:, k:k + 1], None,
                                        ALU.mult).then_inc(misc_ev, 1)

            def value_lo(vt, q, count):
                ps = wait_misc().rearrange("p (t g d) -> p t g d", t=4, g=GROUPS)
                dve.wait_ge(v_hi, count)
                nc.vector.tensor_tensor(vt[:, 4 * q:4 * q + 4, :, HD:], ps, vt[:, 4 * q:4 * q + 4, :, 0:HD].bitcast(f32),
                                        ALU.subtract).then_inc(misc_ev, 1)

            def key_lo(b, dst, src):
                dve.wait_ge(k_hi, b + 1)
                nc.vector.tensor_tensor(dst[HD:P], src[HD:P], dst[HD:P].bitcast(f32), ALU.subtract).then_inc(k_ready, 1)

            n2 = GROUPS * NCMP

            def hidden(b):
                ps = wait_misc()
                link(nc.vector.tensor_scalar(cu[:, b, 0:n2], ps[0:HD, 0:n2], cb[:, b:b + 1], None, ALU.add))
                link(nc.vector.tensor_tensor(cv[:, 0:n2], cu[:, b, 0:n2], cu[:, b, 0:n2], ALU.mult))
                link(nc.vector.tensor_scalar(cv[:, 0:n2], cv[:, 0:n2], 0.044715, 1.0, ALU.mult, ALU.add))
                nc.vector.tensor_tensor(cv[:, 0:n2], cv[:, 0:n2], cu[:, b, 0:n2], ALU.mult).then_inc(gelu_arg, 1)
                dve.wait_ge(gelu_tanh, b + 1)
                nc.vector.scalar_tensor_tensor(out=chid[:, b, :, 0:NCMP], in0=cz[:, 0:n2].rearrange("p (g c) -> p g c", g=GROUPS),
                                               scalar=1.0, in1=cu[:, b, 0:n2].rearrange("p (g c) -> p g c", g=GROUPS),
                                               op0=ALU.add, op1=ALU.mult).then_inc(misc_ev, 1)

            def compressed(b):
                ps = wait_misc()[:, 0:P]
                if b == 0:
                    link(nc.vector.tensor_scalar(kcs[:], ps, 0.5, None, ALU.mult))
                    link(nc.vector.tensor_copy(kC[:].rearrange("p g c -> p (g c)"), kcs[:]))
                    nc.vector.tensor_tensor(kC[HD:P].rearrange("p g c -> p (g c)"), kcs[HD:P],
                                            kC[HD:P].rearrange("p g c -> p (g c)").bitcast(f32), ALU.subtract).then_inc(misc_ev, 1)
                else:
                    link(nc.vector.tensor_scalar(kcs[0:CP], ps[0:CP], 0.5, None, ALU.mult))
                    kv = kcs[0:CP].rearrange("c (g d) -> c g d", g=GROUPS)
                    link(nc.vector.tensor_copy(vC[:, :, 0:HD], kv))
                    nc.vector.tensor_tensor(vC[:, :, HD:], kv, vC[:, :, 0:HD].bitcast(f32), ALU.subtract).then_inc(misc_ev, 1)

            def query_lo(it):
                dve.wait_ge(q_hi, it + 1)
                nc.vector.tensor_tensor(ql[:, it % 2], qraw[:, it % 2], qh[:, it % 2].bitcast(f32), ALU.subtract).then_inc(q_lo, 1)

            for n in range(N1):
                split_lo(n + 1, (n + 1) % 2)
                if n == N1 - 1:
                    query_lo(0)
                    query_lo(1)
                evac_proj(n, n % 2, slice(n, n + 1), 16 * (n // 2) if n >= 2 else None)
                if n == 0:
                    dve.wait_ge(pad_ready, 1)
                    nc.vector.reciprocal(icnt[:], icnt[:]).then_inc(icnt_ready, 1)
                    dve.wait_ge(icnt_ready, 1)
                if n == 5:
                    dve.wait_ge(u_in, 16)
                    pool_mix(0)
                    pool_mix(1)
                if n == 6:
                    ps = wait_misc()
                    nc.vector.tensor_copy(pe2[:].rearrange("p b j -> p (b j)"), ps[:, 0:CBLOCK]).then_inc(misc_ev, 1)
                    pool_mix(2)
                if n == 7:
                    ps = wait_misc()
                    nc.vector.tensor_copy(cb[:], ps[0:HD, 0:2]).then_inc(misc_ev, 1)
                    pool_mix(3)
                if n == 8:
                    dve.wait_ge(consts, 2)
                    hidden(0)
                if n == 9:
                    compressed(0)
                    hidden(1)
                if n == 10:
                    compressed(1)
                    for s in range(4):
                        take_y(s)
                if n == 11:
                    for s in range(4, 8):
                        take_y(s)
                    value_lo(vS, 0, 1)
                    value_lo(vS, 1, 2)
                    key_lo(0, kS, ldB)
                if n == 12:
                    wait_misc()
                    dve.wait_ge(gate_tanh, 1)
                    link(nc.vector.tensor_scalar(gates[:].rearrange("p t h b -> p (t h b)"), gate_t[:], 1.0, 0.5, ALU.add, ALU.mult))
                    nc.vector.tensor_scalar(gates[:, 0, :, 0:1], gates[:, 0, :, 0:1], cvalid[:, 0:1], None, ALU.mult).then_inc(misc_ev, 1)
                    value_lo(vW, 0, 3)
                    value_lo(vW, 1, 4)
                if n == 13:
                    key_lo(1, kW, ldA)

            def maxima(it, r):
                g, i = ITER[it]
                e = it * GR + r
                head = g * GR + r
                row = PB[it % 2]
                a, b = n_slc(i), n_slc(i) + n_win(i)
                if it == 1 and r == 0:
                    for slot in range(2):
                        dve.wait_ge(st_proj[slot], 16 * ((N1 + 1 - slot) // 2))
                if it >= 2 and r == 0:
                    dve.wait_ge(t_done, first_block[it - 1])
                dve.wait_ge(s_slc, e + 1)
                nc.vector.tensor_tensor_reduce(out=row[:, r, 0:a], in0=psS0[:, 0:a], in1=T1[:, S - a:S], scale=1.0, scalar=-3e38,
                                               op0=ALU.add, op1=ALU.max, accum_out=mx[:, it % 2, r, 0:1]).then_inc(m_slc, 1)
                dve.wait_ge(s_win, e + 1)
                nc.vector.tensor_tensor_reduce(out=row[:, r, a:b], in0=psS1[:, 0:b - a], in1=TW[:, (WIN_TILES + 1) * P - (b - a):],
                                               scale=1.0, scalar=-3e38, op0=ALU.add, op1=ALU.max, accum_out=mx[:, it % 2, r, 1:2])
                nc.vector.tensor_tensor_reduce(out=row[:, r, b:b + CP], in0=psS1[:, b - a:b - a + CP], in1=TC[:, i], scale=1.0,
                                               scalar=-3e38, op0=ALU.add, op1=ALU.max, accum_out=mx[:, it % 2, r, 2:3]).then_inc(m_win, 1)
                dve.wait_ge(m_win, e + 1)
                nc.vector.tensor_scalar(nb[:, it % 2, r], mx[:, it % 2, r], -2.0 ** -(head + 1), None, ALU.mult).then_inc(nb_ready, 1)

            def weights(it, r):
                g, i = ITER[it]
                head = g * GR + r
                w = rs[:, it % 2, r]
                row = PB[it % 2]
                dve.wait_ge(exp_done, 3 * (it * GR + r + 1))
                link(nc.vector.reciprocal(w, esum[:, it % 2, r]))
                nc.vector.tensor_tensor(w[:, 0:2], gates[:, i, head, 1:3], w[:, 0:2], ALU.mult)
                link(nc.vector.tensor_tensor(w[:, 2:3], gates[:, i, head, 0:1], w[:, 2:3], ALU.mult))
                for k, (lo, hi) in enumerate(branch_cols(i)):
                    last = nc.vector.tensor_scalar(row[:, r, lo:hi], row[:, r, lo:hi], w[:, k:k + 1], None, ALU.mult)
                last.then_inc(p_ready, 1)

            def prob_lo(B, kind):
                rows = CP if kind == "cmp" else P
                dve.wait_ge(pt_hi, B + 1)
                nc.vector.tensor_tensor(ptl[0:rows, B % 2], psX[0:rows, B % 2], pth[0:rows, B % 2].bitcast(f32),
                                        ALU.subtract).then_inc(pt_lo, 1)

            def out_sum(it):
                dve.wait_ge(o_half, it + 1)
                if it >= 2:
                    dve.wait_ge(st_o[it % 2], 16 * (it // 2))
                nc.vector.tensor_tensor(ostg[:, it % 2], psX[0:HD, 2], otmp[:], ALU.add).then_inc(o_ready, 1)

            split_lo(NZ + 1, (NZ + 1) % 2)
            for r in range(GR):
                maxima(0, r)
                if r:
                    weights(0, r - 1)
            weights(0, GR - 1)
            for it in range(NIT):
                for r in range(GR):
                    if it + 1 < NIT:
                        maxima(it + 1, r)
                    if r == 1 and it < Z_STEPS:
                        split_lo(NZ + it + 2, (NZ + it) % 2)
                    if r == 0 and it:
                        out_sum(it - 1)
                    if r == 2 and it + 2 < NIT:
                        query_lo(it + 2)
                    todo = chunk(it, r)
                    own = min(len(todo), 3) if r == GR - 1 else None
                    for k in range(len(todo) + 1):
                        if k == W_POS and r and it + 1 < NIT or k == len(todo) < W_POS and r and it + 1 < NIT:
                            weights(it + 1, r - 1)
                        if k == own and it + 1 < NIT:
                            weights(it + 1, r)
                        if k < len(todo):
                            prob_lo(todo[k][0], todo[k][2])
            out_sum(NIT - 1)

            def part_lo(dst, src, hi, count):
                dve.wait_ge(yo_hi, count)
                nc.vector.tensor_tensor(dst, src, hi.bitcast(f32), ALU.subtract).then_inc(yo_lo, 1)

            split_lo(N3, N3 % 2)
            for h in range(2):
                cols = slice(h * HALF, (h + 1) * HALF)
                part_lo(ylo[:, :, cols], yraw[:, :, cols], yhi[:, :, cols], h + 1)
            part_lo(olo[:, 0:2], oraw[0][:], ohi[:, 0:2], 3)
            for h in range(2):
                cols = slice(h * HALF, (h + 1) * HALF)
                part_lo(olo[:, 2:4, cols], oraw[1][:, :, cols], ohi[:, 2:4, cols], h + 4)
            for h in range(2):
                dve.wait_ge(st_z[h], 16 * 2 * KT)

            def mix(n, slot, m, t_slot, need):
                split_lo(n + 1, (slot + 1) % 2)
                dve.wait_ge(xr_t, m + 1)
                nc.vector.tensor_copy(xT[:, 4:8, bass.ds(P * m, P)],
                                      psX[:, 2 * t_slot + 1].rearrange("p (k t) -> p k t", k=4)).then_inc(xT_v, 1)
                for h in range(2):
                    dve.wait_ge(u_done, 2 * n + h + 1)
                    dve.wait_ge(mg_in[h], 16 * (m + 1))
                    nc.vector.scalar_tensor_tensor(out=mt[:, 0], in0=mg[:, h, 0], scalar=1.0, in1=psU[:, 2 * h], op0=ALU.add,
                                                   op1=ALU.mult)
                    nc.vector.scalar_tensor_tensor(out=mt[:, 1], in0=mg[:, h, 1], scalar=1.0, in1=psU[:, 2 * h + 1], op0=ALU.add,
                                                   op1=ALU.mult).then_inc(ab_read, 1)
                    dve.wait_ge(ab_read, 2 * m + h + 1)
                    nc.vector.tensor_tensor(ct[:, h], mt[:, 0], mt[:, 1], ALU.add).then_inc(c_sum, 1)
                    dve.wait_ge(c_sum, 2 * m + h + 1)
                for h in range(2):
                    cols = slice(h * HALF, (h + 1) * HALF)
                    dve.wait_ge(c_hi, 2 * m + h + 1)
                    nc.vector.scalar_tensor_tensor(out=alo[:, bass.ds(m, 1), cols], in0=ct[:, h:h + 1], scalar=0.5,
                                                   in1=ahi[:, bass.ds(m, 1), cols].bitcast(f32), op0=ALU.mult,
                                                   op1=ALU.subtract).then_inc(c_lo, 1)
                dve.wait_ge(c_lo, 2 * m + 2)

            with dve.Fori(0, KT // 2) as j:
                for u in range(2):
                    n = N3 + u
                    mix(n + 2 * j, n % 2, 2 * j + u, u, None)
            dve.wait_ge(xT_a, TT)
            dve.wait_ge(xT_v, TT)

            def out_evac(n, u, m, s):
                for h in range(2):
                    dve.wait_ge(u_done, 2 * n + h + 1)
                    cols = slice(h * HALF, (h + 1) * HALF)
                    nc.vector.tensor_tensor(xT[:, bass.ds(m, 1), cols], psU[:, 2 * u + h:2 * u + h + 1],
                                            xT[:, bass.ds(m, 1), cols], ALU.add).then_inc(res[h], 1)
                for h in range(2):
                    cols = slice(h * HALF, (h + 1) * HALF)
                    dve.wait_ge(h2_hi, s + h + 1)
                    nc.vector.scalar_tensor_tensor(out=h2lo[:, bass.ds(m, 1), cols], in0=xT[:, bass.ds(m, 1), cols],
                                                   scalar=g2[:, bass.ds(m, 1)], in1=h2hi[:, bass.ds(m, 1), cols].bitcast(f32),
                                                   op0=ALU.mult, op1=ALU.subtract).then_inc(h2_lo, 1)

            with dve.Fori(0, KT // 2) as j:
                for u in range(2):
                    n = N4 + u
                    split_lo(n + 1 + 2 * j, (n + 1) % 2)
                    out_evac(n + 2 * j, u, 2 * j + u, 4 * j + 2 * u)

            def up_evac(s, c, t):
                for h in range(2):
                    dve.wait_ge(relu[h], c + 1)
                    nc.vector.tensor_tensor(rsq[:, h], rel[:, h], rel[:, h], ALU.mult).then_inc(rsq_ready, 1)
                for h in range(2):
                    dve.wait_ge(hid_hi, s + h + 1)
                    nc.vector.tensor_tensor(alo[:, bass.ds(t, 1), h * HALF:(h + 1) * HALF], rsq[:, h:h + 1],
                                            ahi[:, bass.ds(t, 1), h * HALF:(h + 1) * HALF].bitcast(f32), ALU.subtract).then_inc(hid_lo, 1)
                dve.wait_ge(hid_lo, s + 2)

            def down_evac(n, u, m, s):
                for h in range(2):
                    cols = slice(h * HALF, (h + 1) * HALF)
                    dve.wait_ge(u_done, 2 * n + h + 1)
                    nc.vector.tensor_tensor(f2t[:, h], psU[:, 2 * u + h], r2[:, cols], ALU.mult).then_inc(mul_r2, 1)
                    dve.wait_ge(mul_r2, s + h + 1)
                    nc.vector.tensor_tensor(xT[:, bass.ds(m, 1), cols], xT[:, bass.ds(m, 1), cols], f2t[:, h:h + 1], ALU.add).then_inc(res[h], 1)

            def norm2_factor():
                for h in range(2):
                    cols = slice(h * HALF, (h + 1) * HALF)
                    dve.wait_ge(ms_done, h + 1)
                    link(nc.vector.tensor_scalar(r2[:, cols], psX[:, h], 1.0 / D, EPS, ALU.mult, ALU.add))
                    nc.vector.reciprocal(r2[:, cols], r2[:, cols]).then_inc(r2_ready, 1)
                dve.wait_ge(r2_ready, 2)

            def mlp_round(r, last, first=False):
                with dve.Fori(0, KT // 2) as j:
                    for u in range(2):
                        n = N5 + u
                        split_lo(n + 1 + 2 * j + 2 * KT * r, (n + 1) % 2)
                        up_evac(2 * KT * r + 4 * j + 2 * u, KT * r + 2 * j + u, 2 * j + u)
                if first:
                    norm2_factor()
                n = N5 + KT
                with dve.Fori(0, KT // 2 - (1 if last else 0)) as j:
                    for u in range(2):
                        split_lo(n + u + 1 + 2 * j + 2 * KT * r, (n + u + 1) % 2)
                        down_evac(n + u + 2 * j + 2 * KT * r, u, 2 * j + u, 2 * KT * r + 4 * j + 2 * u)
                if last:
                    nl = N5 + 2 * KT * ROUNDS - 1
                    split_lo(nl, nl % 2)
                    for u in range(2):
                        down_evac(nl - 1 + u, u, KT - 2 + u, 2 * KT * ROUNDS - 4 + 2 * u)

            mlp_round(0, False, True)
            with dve.Fori(1, ROUNDS - 1) as r:
                mlp_round(r, False)
            mlp_round(ROUNDS - 1, True)

            dve.wait_ge(gf_in, 16)
            def result(t):
                dve.wait_ge(fin_rms, t + 1)
                nc.vector.reciprocal(rstd[:, t:t + 1], rms[:, t:t + 1]).then_inc(fin_r, 1)
                dve.wait_ge(fin_r, t + 1)
                if t >= 2:
                    dve.wait_ge(st_out[t % 2], 16 * (t // 2))
                nc.vector.scalar_tensor_tensor(out=ost[:, t % 2], in0=fin_bank(t), scalar=rstd[:, t:t + 1], in1=gfb[:],
                                               op0=ALU.mult, op1=ALU.mult).then_inc(fin_o, 1)

            for t in range(TT):
                dve.wait_ge(fin_ss, t + 1)
                nc.vector.tensor_scalar(msq[:, t:t + 1], ssum[:, t:t + 1], 1.0 / D, EPS, ALU.mult, ALU.add).then_inc(fin_ms, 1)
                if t:
                    result(t - 1)
            result(TT - 1)

        @block.tensor
        def _(pe):
            def three(ps, slot, k, w, hi, lo, cols, start, stop):
                nc.tensor.matmul(ps, whi[:, slot, w], hi[:, k, cols], start=start, stop=False)
                nc.tensor.matmul(ps, whi[:, slot, w], lo[:, k, cols], start=False, stop=False)
                return nc.tensor.matmul(ps, wlo[:, slot, w], hi[:, k, cols], start=False, stop=stop)

            def unit(n, slot, hi, lo, bank, before=None):
                pe.wait_ge(w_lo, n + 1)
                for h in range(2):
                    for k in range(KT):
                        if before:
                            before(h, k)
                        last = three(psU[:, bank + h], slot, k, k, hi, lo, slice(h * HALF, (h + 1) * HALF), k == 0, k == KT - 1)
                    last.then_inc(u_done, 1)

            pe.wait_ge(consts, 1)
            pe.wait_ge(const_in, 48)
            nc.tensor.transpose(psU[:, 0, 0:2 * KT + 4], grow[:], ident[0:2 * KT + 4, 0:2 * KT + 4]).then_inc(gain_t, 1)
            pe.wait_ge(gain_ready, 1)

            for t in range(TT):
                pe.wait_ge(xs_ready, t + 1)
                if t >= 2:
                    pe.wait_ge(hraw_ready, t - 1)
                for k in range(KT):
                    last = nc.tensor.transpose(psX[:, 2 * (t % 2) + k // 4, (k % 4) * P:(k % 4 + 1) * P], xt[:, t, k * P:(k + 1) * P], ident[:])
                last.then_inc(xt_ready, 1)

            def proj_before(n, peeled):
                def before(h, k):
                    if k == 0:
                        pe.wait_ge(h_lo, 4 * (h + 1))
                        if peeled >= 2:
                            pe.wait_ge(ev[h], n - 1)
                return before

            step = [0]
            J = CBLOCK // 2

            def bank():
                if step[0] >= 4:
                    pe.wait_ge(misc_ev, step[0] - 3)
                step[0] += 1
                return psX[:, (step[0] - 1) % 4]

            def encodings():
                pe.wait_ge(cw_in, 64)
                b = bank()
                for br in range(2):
                    last = nc.tensor.transpose(b[:, br * J:(br + 1) * J], pet[:, br], ident[0:J, 0:J])
                last.then_inc(misc, 1)

            def encodings_hidden():
                pe.wait_ge(misc_ev, 1)
                b = bank()
                for br in range(2):
                    for j in range(J):
                        last = nc.tensor.matmul(b[0:HD, br:br + 1], cw1[:, br, j], pe2[:, br, j:j + 1], start=(j == 0), stop=(j == J - 1))
                last.then_inc(misc, 1)

            def hidden(br, src, s):
                pe.wait_ge(s, 32)
                b = bank()
                for j in range(J):
                    rhs = src[:, :, 2 * j:2 * j + CSTRIDE * (NCMP - 1) + 1:CSTRIDE]
                    last = nc.tensor.matmul(b[0:HD, 0:GROUPS * NCMP], cw1[:, br, j], rhs, start=(j == 0), stop=(j == J - 1))
                last.then_inc(misc, 1)

            def compressed(br):
                pe.wait_ge(misc_ev, step[0])
                b = bank()
                if br == 0:
                    last = nc.tensor.matmul(b[:, 0:GROUPS * CP], cw2[:, 0], chid[:, 0].rearrange("p g c -> p (g c)"), start=True, stop=True)
                else:
                    for g in range(GROUPS):
                        last = nc.tensor.matmul(b[0:CP, g * HD:(g + 1) * HD], chid[:, 1, g], cw2[:, 1, 0:HD], start=True, stop=True)
                last.then_inc(misc, 1)

            def pool_product(k, h):
                if h == 0:
                    pe.wait_ge(pooled, k + 1)
                nc.tensor.matmul(bank(), wp[:, k], up[:, k, PAD + h * HALF:PAD + (h + 1) * HALF], start=True, stop=True).then_inc(misc, 1)

            def value_turn(src, s, q):
                if q == 0:
                    pe.wait_ge(s, 16)
                b = bank()
                for t in range(4):
                    last = nc.tensor.transpose(b[:, t * P:(t + 1) * P], src[:, (4 * q + t) * P:(4 * q + t + 1) * P], ident[:])
                last.then_inc(misc, 1)

            def gate_turn():
                pe.wait_ge(gate_in, 16)
                b = bank()
                for t in range(TT):
                    last = nc.tensor.transpose(b[:, t * NG:(t + 1) * NG], gtd[:, t * P:(t + 1) * P], ident[0:NG, 0:NG])
                last.then_inc(misc, 1)

            for n in range(N1):
                unit(n, n % 2, ahi, alo, 2 * (n % 2), proj_before(n, n))
                if n == 6:
                    encodings()
                if n == 7:
                    encodings_hidden()
                if n == 8:
                    hidden(0, ldA, kc_in)
                if n == 9:
                    compressed(0)
                    hidden(1, ldB, vc_in)
                if n == 10:
                    compressed(1)
                    assert step[0] == N_CMP
                    pe.wait_ge(pool_w_in, 16)
                    for s in range(4):
                        pool_product(s // 2, s % 2)
                if n == 11:
                    for s in range(4, 8):
                        pool_product(s // 2, s % 2)
                    assert step[0] == N_Y
                    value_turn(ldA[:, 0], vs_in, 0)
                    value_turn(ldA[:, 0], vs_in, 1)
                if n == 12:
                    gate_turn()
                    value_turn(ldA[:, 1], vw_in, 0)
                    value_turn(ldA[:, 1], vw_in, 1)
            assert step[0] == N_MISC, step[0]

            def scores(it, r):
                g, i = ITER[it]
                e = it * GR + r
                s = it % 2
                if r == 0:
                    pe.wait_ge(q_lo, it + 1)
                if e >= 1:
                    pe.wait_ge(m_slc, e)
                a, w = n_slc(i), n_win(i)
                for c in range(0, a, HALF):
                    n = min(HALF, a - c)
                    nc.tensor.matmul(psS0[:, c:c + n], qh[:, s, r], kS[:, g, c:c + n], start=True, stop=False)
                    last = nc.tensor.matmul(psS0[:, c:c + n], ql[:, s, r], kS[:, g, c:c + n], start=False, stop=True)
                last.then_inc(s_slc, 1)
                if e >= 1:
                    pe.wait_ge(m_win, e)
                for c in range(0, w, HALF):
                    n = min(HALF, w - c)
                    ks = kW[:, g, a - w + c:a - w + c + n]
                    nc.tensor.matmul(psS1[:, c:c + n], qh[:, s, r], ks, start=True, stop=False)
                    nc.tensor.matmul(psS1[:, c:c + n], ql[:, s, r], ks, start=False, stop=True)
                nc.tensor.matmul(psS1[:, w:w + CP], qh[:, s, r], kC[:, g], start=True, stop=False)
                nc.tensor.matmul(psS1[:, w:w + CP], ql[:, s, r], kC[:, g], start=False, stop=True).then_inc(s_win, 1)

            def turn(it, B, kind, kb):
                g, i = ITER[it]
                if B >= 2:
                    pe.wait_ge(pt_lo, B - 1)
                width = CP if kind == "cmp" else P
                col = prob_col(i, kind, kb)
                for r in range(GR):
                    last = nc.tensor.transpose(psX[0:width, B % 2, r * P:(r + 1) * P], PB[it % 2][:, r, col:col + width], ident[:])
                last.then_inc(t_done, 1)

            def values(it, B, kind, kb):
                g, i = ITER[it]
                first, final = B == first_block[it], B == first_block[it + 1] - 1
                if first and it >= 1:
                    pe.wait_ge(o_ready, it)
                pe.wait_ge(pt_lo, B + 1)
                v = {"slc": vS[:, kb, g], "win": vW[:, kb, g], "cmp": vC[:, g]}[kind]
                rows = CP if kind == "cmp" else P
                nc.tensor.matmul(psX[:, 2], v, pth[0:rows, B % 2], start=first, stop=False)
                nc.tensor.matmul(psX[:, 2], v, ptl[0:rows, B % 2], start=False, stop=final).then_inc(pv_done, 1)

            def gates(q, lo, hi):
                n, slot = NZ + q, (NZ + q) % 2
                for h, k in [divmod(c, KT) for c in range(lo, hi)]:
                    if h == 0 and k == 0:
                        pe.wait_ge(w_lo, n + 1)
                    if k == 0 and (q or h):
                        pe.wait_ge(z_ready, 2 * q + h)
                    last = three(psX[:, 3], slot, k, k, ahi, alo, slice(h * HALF, (h + 1) * HALF), k == 0, k == KT - 1)
                    if k == KT - 1:
                        last.then_inc(u_done, 1)

            pe.wait_ge(misc_ev, N_MISC)
            gates(0, 0, 2)
            pe.wait_ge(ev[0], N1)
            pe.wait_ge(ev[1], N1)
            pe.wait_ge(k_ready, 2)
            for r, (lo, hi) in enumerate(((2, 6), (6, 10), (10, 13), (13, 2 * KT))):
                scores(0, r)
                gates(0, lo, hi)
            pending = []
            for it in range(NIT):
                for r in range(GR):
                    if it + 1 < NIT:
                        scores(it + 1, r)
                    todo = chunk(it, r)
                    g0, g1 = GATE_SHARE[r:r + 2]
                    lead = g1 - g0 if it == r == 0 or not todo else 0
                    share = [g0 + lead + (g1 - g0 - lead) * k // max(1, 2 * len(todo)) for k in range(2 * len(todo) + 1)]
                    if it < Z_STEPS:
                        gates(it + 1, g0, g0 + lead)
                    if r == 0:
                        pe.wait_ge(p_ready, GR * (it + 1))
                    for k, (B, _k, kind, kb) in enumerate(todo):
                        turn(it, B, kind, kb)
                        if it < Z_STEPS:
                            gates(it + 1, share[2 * k], share[2 * k + 1])
                        if pending:
                            values(*pending.pop())
                        pending.append((it, B, kind, kb))
                        if it < Z_STEPS:
                            gates(it + 1, share[2 * k + 1], share[2 * k + 2])
                if pending:
                    values(*pending.pop())
            gates(2 * KT - 1, 0, 2 * KT)

            pe.wait_ge(m_slc, GR * NIT)
            pe.wait_ge(m_win, GR * NIT)

            def mixers(n, slot, m, t_slot, peeled):
                if peeled is None:
                    pe.wait_ge(xr_in[t_slot], 8 * m - 8 * t_slot + 16)
                    pe.wait_ge(xT_a, m - 1)
                    pe.wait_ge(xT_v, m - 1)
                else:
                    pe.wait_ge(xr_in[t_slot], 16)
                    if peeled == 1:
                        pe.wait_ge(z_ready, 4 * KT)
                for k in range(KT):
                    last = nc.tensor.transpose(psX[:, 2 * t_slot + k // 4, (k % 4) * P:(k % 4 + 1) * P], xr[:, t_slot, k * P:(k + 1) * P], ident[:])
                last.then_inc(xr_t, 1)
                pe.wait_ge(w_lo, n + 1)

                def pool_part(h):
                    for k in range(4):
                        three(psU[:, 2 * h + 1], slot, k, 4 + k, yhi, ylo, slice(h * HALF, (h + 1) * HALF), k == 0, k == 3)

                def attention_part(h):
                    for k in range(4):
                        if peeled == 0 and k % 2 == 0:
                            pe.wait_ge(yo_lo, 3 if k == 0 else 4 + h)
                        last = three(psU[:, 2 * h], slot, k, k, ohi, olo, slice(h * HALF, (h + 1) * HALF), k == 0, k == 3)
                    last.then_inc(u_done, 1)

                if peeled == 0:
                    for h in range(2):
                        pe.wait_ge(yo_lo, h + 1)
                        pool_part(h)
                    for h in range(2):
                        attention_part(h)
                else:
                    for h in range(2):
                        pe.wait_ge(ab_read, 2 * m + h - 1)
                        pool_part(h)
                        attention_part(h)

            for m in range(2):
                mixers(N3 + m, (N3 + m) % 2, m, m, m)
            with pe.Fori(1, KT // 2) as j:
                for u in range(2):
                    mixers(N3 + u + 2 * j, (N3 + u) % 2, 2 * j + u, u, None)

            def out_before(m, first):
                def before(h, k):
                    if k == 0 and first:
                        pe.wait_ge(ab_read, 2 * KT - 1 + m)
                    if first:
                        pe.wait_ge(c_lo, 2 * k + h + 1)
                    if k == 0 and not first:
                        pe.wait_ge(res[h], m - 1)
                return before

            for u in range(2):
                unit(N4 + u, (N4 + u) % 2, ahi, alo, 2 * u, out_before(u, True))
            with pe.Fori(1, KT // 2) as j:
                for u in range(2):
                    unit(N4 + u + 2 * j, (N4 + u) % 2, ahi, alo, 2 * u, out_before(2 * j + u, False))

            def up_before(r, t, first):
                def before(h, k):
                    if k == 0 and first:
                        pe.wait_ge(res[h], KT * r + (KT - 1) + t)
                    elif k == 0:
                        pe.wait_ge(relu[h], KT * r + t - 1)
                    if first:
                        pe.wait_ge(h2_lo, 2 * k + h + 1)
                return before

            def down_before(r, m, first):
                def before(h, k):
                    if k == 0 and first:
                        pe.wait_ge(relu[h], KT * r + (KT - 1) + m)
                    elif k == 0:
                        pe.wait_ge(res[h], KT * r + (KT - 1) + m)
                    if first:
                        pe.wait_ge(hid_lo, 2 * KT * r + 2 * k + h + 1)
                return before

            def norm2_sums():
                pe.wait_ge(sq_sum, 2 * KT)
                for h in range(2):
                    nc.tensor.matmul(psX[:, h], ones[:], sqa[:, h * HALF:(h + 1) * HALF], start=True, stop=True).then_inc(ms_done, 1)

            def mlp_round(r, first_round=False):
                for which, before, hi, lo in ((0, up_before, h2hi, h2lo), (1, down_before, ahi, alo)):
                    n = N5 + KT * which
                    for u in range(2):
                        unit(n + u + 2 * KT * r, (n + u) % 2, hi, lo, 2 * u, before(r, u, True))
                    if first_round and which == 0:
                        norm2_sums()
                    with pe.Fori(1, KT // 2) as j:
                        for u in range(2):
                            unit(n + u + 2 * j + 2 * KT * r, (n + u) % 2, hi, lo, 2 * u, before(r, 2 * j + u, False))

            mlp_round(0, True)
            with pe.Fori(1, ROUNDS) as r:
                mlp_round(r)

            for h in range(2):
                pe.wait_ge(res[h], KT * (ROUNDS + 1))
            pe.wait_ge(r2_ready, 2)
            for t in range(TT):
                if t >= 4:
                    pe.wait_ge(fin_o, t - 3)
                for k in range(KT):
                    last = nc.tensor.transpose(fin_bank(t)[:, k * P:(k + 1) * P], xT[:, k, t * P:(t + 1) * P], ident[:])
                last.then_inc(fin_t, 1)


_INS = ['x', 'norm1_g', 'w_in', 'cmp_pe', 'cmp_w1', 'cmp_w2', 'w_attn_proj', 'w_pool', 'pool_scale',
        'w_pool_proj', 'w_out', 'norm2_g', 'w_ff1', 'w_ff2', 'final_g']
_OUTS = [((1, 1024, 1024), 'float32')]


def kernel(**inputs):
    import numpy as _np
    import concourse.bacc as _bacc
    from concourse import mybir as _mybir
    from concourse.bass_utils import run_bass_kernel_spmd as _run

    nc = _bacc.Bacc("TRN2", target_bir_lowering=False, num_devices=1, dynamic_dma_scratch_size=1024)
    arrays, args = {}, []
    for name in _INS:
        a = _np.ascontiguousarray(inputs[name])
        arrays[f"in_{name}_dram"] = a
        args.append(nc.dram_tensor(f"in_{name}_dram", a.shape, _mybir.dt.from_np(a.dtype), kind="ExternalInput").ap())
    for i, (shape, dtype) in enumerate(_OUTS):
        dt = _mybir.dt.from_np(_np.dtype(dtype))
        args.append(nc.dram_tensor(f"out_{i}_dram", shape, dt, kind="ExternalOutput").ap())
    hybrid_trunk(nc, *args)
    r = _run(nc, [arrays], core_ids=[0])
    got = tuple(r.results[0][f"out_{i}_dram"] for i in range(len(_OUTS)))
    return got[0]
```

```python
import concourse.bass as bass
from concourse import mybir
from contextlib import ExitStack



def hybrid_trunk(nc, x, norm1_g, w_in, cmp_pe, cmp_w1, cmp_w2, w_attn_proj, w_pool, pool_scale,
                 w_pool_proj, w_out, norm2_g, w_ff1, w_ff2, final_g, out):
    f32 = mybir.dt.float32
    f32r = mybir.dt.float32r
    ALU = mybir.AluOpType
    ACT = mybir.ActivationFunctionType

    P = 128
    S, D = x.shape[1], x.shape[2]
    KT = D // P
    TT = S // P
    HALF = 512
    FF = w_ff1.shape[2]
    HEADS, HD, GROUPS = 8, 64, 2
    GR = HEADS // GROUPS
    WIN_TILES = 512 // P
    NCMP, CSTRIDE, CBLOCK = 63, 16, 32
    CP = 64
    NEG = -1e30
    EPS = 1e-6
    O_GATE = HEADS * HD + 3 * 2 * GROUPS * HD
    O_POOL = O_GATE + 3 * HEADS
    O_MERGE = O_POOL + 512
    NG = 3 * HEADS
    PAD = 16

    U_POOL, U_GATE, U_KC, U_VC, U_KS, U_VS, U_KW, U_VW, U_Q = 0, 4, 5, 6, 7, 8, 9, 10, 11
    N1 = 15
    NZ = N1
    N3 = NZ + 2 * KT
    N4 = N3 + KT
    N5 = N4 + KT
    ROUNDS = FF // D
    NL = N5 + 2 * KT * ROUNDS - KT
    HALVES = 2 * KT
    FIN_STEP = KT + 1
    M_KHID, M_VHID, M_CMP, M_POOL, M_VS, M_GATE, M_VW, N_MISC = 3, 5, 6, 14, 15, 17, 18, 19
    GELU_C = 0.7978845608028654

    w_in_u = w_in[0].rearrange("(k p) n -> p k n", p=P)
    w_ap_u = w_attn_proj[0].rearrange("(k p) n -> p k n", p=P)
    w_pp_u = w_pool_proj[0].rearrange("(k p) n -> p k n", p=P)
    w_out_u = w_out[0].rearrange("(k p) n -> p k n", p=P)
    w_ff1_u = w_ff1[0].rearrange("(k p) n -> p k n", p=P)
    w_ff2_u = w_ff2[0].rearrange("(k p) n -> p k n", p=P)

    ctx = ExitStack()
    with ctx:
        def sem(name):
            return ctx.enter_context(nc.semaphore(name))

        START = (nc.sbuf_base + 63) // 64 * 64
        END = nc.sbuf_usable_end
        cursor = [START]

        def size_of(shape):
            n = 4
            for d in shape[1:]:
                n *= d
            return (n + 31) // 32 * 32

        def place(name, shape, dt=f32):
            off = cursor[0]
            cursor[0] += size_of(shape)
            assert cursor[0] <= END, (name, cursor[0] - END)
            return nc.alloc_sbuf_tensor_at(name, shape, dt, offset=off)

        wraw = place("wraw", [P, 2, KT, P])
        whi = place("whi", [P, 2, KT, P], f32r)
        wlo = place("wlo", [P, 2, KT, P], f32r)
        ahi = place("ahi", [P, KT, S], f32r)
        alo = place("alo", [P, KT, S], f32r)
        ident = place("ident", [P, P])
        ones = place("ones", [P, P])
        gcol = place("gcol", [P, KT + 4])
        g2, psc = gcol[:, 0:KT], gcol[:, KT:]
        qscale = place("qscale", [P, N1])
        ssum = place("ssum", [P, TT])
        msq = place("msq", [P, TT])
        rms = place("rms", [P, TT])
        rstd = place("rstd", [P, TT])
        gates = place("gates", [P, TT, HEADS, 3])
        cvalid = place("cvalid", [P, 1])
        mx = place("mx", [P, 2, GR, 3])
        nb = place("nb", [P, 2, GR, 3])
        esum = place("esum", [P, 2, GR, 3])
        rs = place("rs", [P, 2, GR, 3])
        ARENA = cursor[0]

        kS = place("kS", [P, GROUPS, S], f32r)
        kW = place("kW", [P, GROUPS, S], f32r)
        kC = place("kC", [P, GROUPS, CP], f32r)
        vS = place("vS", [P, TT, GROUPS, 2 * HD], f32r)
        vW = place("vW", [P, TT, GROUPS, 2 * HD], f32r)
        T1 = place("T1", [P, S])
        TW = place("TW", [P, (WIN_TILES + 1) * P])
        TC = place("TC", [P, TT, CP])
        REGION = cursor[0]
        ORDER = [7, 1, 6, 2, 5, 3, 4, 0]
        ITER = [(g, i) for g in range(GROUPS) for i in ORDER]
        NIT = len(ITER)

        def n_slc(i):
            return (i + 1) * P

        def n_win(i):
            return min(i + 1, WIN_TILES + 1) * P

        def n_row(i):
            return n_slc(i) + n_win(i) + CP

        def blocks(i):
            return [("slc", kb) for kb in range(i + 1)] + \
                   [("win", kb) for kb in range(i + 1 - n_win(i) // P, i + 1)] + [("cmp", 0)]

        PB = [place("prob0", [P, GR, n_row(7)])]
        ostg = place("ostg", [HD, 2, GR * P])
        vC = place("vC", [CP, GROUPS, 2 * HD], f32r)
        QUERIES = cursor[0]
        qraw = place("qraw", [P, 2, GR, P])
        qh = place("qh", [P, 2, GR, P], f32r)
        ql = place("ql", [P, 2, GR, P], f32r)
        STAGE = cursor[0]
        PB.append(place("prob1", [P, GR, n_row(3)]))
        pth = place("pth", [P, 2, GR * P], f32r)
        ptl = place("ptl", [P, 2, GR * P], f32r)
        otmp = place("otmp", [HD, GR * P])
        zst = place("zst", [P, 2, HALF])
        yraw = place("yraw", [P, 4, S])

        cursor[0] = REGION
        xt = place("xt", [P, TT, D])
        after_x = cursor[0]
        cw1 = place("cw1", [P, 2, CBLOCK // 2, HD])
        cw2 = place("cw2", [HD, 2, 2 * HD])
        pet = place("pet", [CBLOCK // 2, 2, 2 * HD])
        chid = place("chid", [HD, 2, GROUPS, CP])
        assert after_x == QUERIES and cursor[0] <= STAGE
        cursor[0] = STAGE
        g1b = place("g1b", [P, D])
        sqj = place("sqj", [P, D])
        grow = place("grow", [KT + 4, P])
        cursor[0] = REGION
        up = place("up", [P, 4, PAD + S])
        tA = place("tA", [P, PAD + S])
        tB = place("tB", [P, PAD + S])
        icnt = place("icnt", [P, 4, PAD])
        wp = place("wp", [P, 4, P])
        gate_t = place("gate_t", [P, TT * NG])
        assert cursor[0] <= after_x
        cursor[0] = STAGE
        stage = place("stage", [P, 2, S])
        ldA = place("ldA", [P, GROUPS, S])
        ldB = place("ldB", [P, GROUPS, S])
        gtd = place("gtd", [NG, S])
        pe2 = place("pe2", [P, 2, CBLOCK // 2])
        cb = place("cb", [HD, 2])
        cu = place("cu", [HD, 2, P])
        cv = place("cv", [HD, P])
        cz = place("cz", [HD, P])
        kcs = place("kcs", [P, P])

        cursor[0] = ARENA
        yhi = place("yhi", [P, 4, S], f32r)
        ohi = place("ohi", [P, 4, S], f32r)
        olo = place("olo", [P, 4, S], f32r)
        ylo = place("ylo", [P, 4, S], f32r)
        RAW = cursor[0]
        xT = place("xT", [P, KT, S])
        TAIL = cursor[0]
        xr = place("xr", [P, 2, D])
        mg = place("mg", [P, 2, 2, HALF])
        mt = place("mt", [P, 2, HALF])
        ct = place("ct", [P, 2, HALF])
        cursor[0] = QUERIES - size_of([P, 2, S])
        oraw = [None, place("oraw1", [P, 2, S])]
        oraw[0] = place("oraw0", [P, 2, S])
        assert RAW <= QUERIES - size_of([P, 2, S]) and cursor[0] <= TAIL
        cursor[0] = ARENA
        h2hi = place("h2hi", [P, KT, S], f32r)
        h2lo = place("h2lo", [P, KT, S], f32r)
        assert cursor[0] == RAW
        cursor[0] = TAIL
        rel = place("rel", [P, 2, HALF])
        rsq = place("rsq", [P, 2, HALF])
        f2t = place("f2t", [P, 2, HALF])
        r2 = place("r2", [P, S])
        sqt = place("sqt", [P, HALF])
        sqa = place("sqa", [P, S])
        cursor[0] = ARENA
        gfb = place("gfb", [P, D])
        sqo = place("sqo", [P, D])
        ost = place("ost", [P, 2, D])

        psU = ctx.enter_context(nc.psum_tensor("psU", [P, 4, HALF], f32))
        psX = ctx.enter_context(nc.psum_tensor("psX", [P, 4, HALF], f32))
        psS0 = psU[:, 0:2, :].rearrange("p b n -> p (b n)")
        psS1 = psU[:, 2:4, :].rearrange("p b n -> p (b n)")

        proj = nc.dram_tensor("proj_scratch", [N1 * P, S], f32).ap()
        oscr = nc.dram_tensor("attn_scratch", [HEADS * HD, S], f32).ap()
        zscr = nc.dram_tensor("gate_scratch", [2 * D, S], f32).ap()

        x_in = [sem(f"x_in{t}") for t in range(TT)]
        const_in, gain_t, gain_ready = sem("const_in"), sem("gain_t"), sem("gain_ready")
        w_raw = [sem("w_raw0"), sem("w_raw1")]
        w_hi, w_lo = sem("w_hi"), sem("w_lo")
        u_done = sem("u_done")
        ev = [sem("ev0"), sem("ev1")]
        consts = sem("consts")
        chain_p, chain_v = sem("chain_p"), sem("chain_v")
        ss_ready, ms_ready, rms_ready, rstd_ready = sem("ss_ready"), sem("ms_ready"), sem("rms_ready"), sem("rstd_ready")
        g1_in, xg_ready = sem("g1_in"), sem("xg_ready")
        xs_ready, xt_ready, h_hi, h_lo = sem("xs_ready"), sem("xt_ready"), sem("h_hi"), sem("h_lo")
        st_proj = [sem("st_proj0"), sem("st_proj1")]
        u_in, pool_w_in, pooled = sem("u_in"), sem("pool_w_in"), sem("pooled")
        gate_in, vs_in, vw_in, ks_in, kw_in = sem("gate_in"), sem("vs_in"), sem("vw_in"), sem("ks_in"), sem("kw_in")
        icnt_ready, pad_ready = sem("icnt_ready"), sem("pad_ready")
        st_z = [sem("st_z0"), sem("st_z1")]
        cw_in, kc_in, vc_in = sem("cw_in"), sem("kc_in"), sem("vc_in")
        misc, misc_ev = sem("misc"), sem("misc_ev")
        k_hi, v_hi, gate_tanh = sem("k_hi"), sem("v_hi"), sem("gate_tanh")
        gelu_arg, gelu_tanh = sem("gelu_arg"), sem("gelu_tanh")
        k_ready = sem("k_ready")
        q_in = [sem("q_in0"), sem("q_in1")]
        q_hi, q_lo = sem("q_hi"), sem("q_lo")
        s_slc, s_win, m_slc, m_win = sem("s_slc"), sem("s_win"), sem("m_slc"), sem("m_win")
        nb_ready, exp_done, p_ready = sem("nb_ready"), sem("exp_done"), sem("p_ready")
        t_done, pt_hi, pt_lo, pv_done = sem("t_done"), sem("pt_hi"), sem("pt_lo"), sem("pv_done")
        o_half, o_ready = sem("o_half"), sem("o_ready")
        st_o = [sem("st_o0"), sem("st_o1")]
        o_in, yo_hi, yo_lo, z_ready = [sem("o_in0"), sem("o_in1")], sem("yo_hi"), sem("yo_lo"), sem("z_ready")
        mg_in = [sem("mg_in0"), sem("mg_in1")]
        ab_read, c_sum = sem("ab_read"), sem("c_sum")
        xr_in = [sem("xr_in0"), sem("xr_in1")]
        xr_t, xT_a, xT_v, c_hi, c_lo = sem("xr_t"), sem("xT_a"), sem("xT_v"), sem("c_hi"), sem("c_lo")
        res = [sem("res0"), sem("res1")]
        relu = [sem("relu0"), sem("relu1")]
        h2_hi, h2_lo = sem("h2_hi"), sem("h2_lo")
        sq_sum, ms_done, r2_ready, mul_r2 = sem("sq_sum"), sem("ms_done"), sem("r2_ready"), sem("mul_r2")
        rsq_ready, hid_hi, hid_lo = sem("rsq_ready"), sem("hid_hi"), sem("hid_lo")
        gf_in, fin_t, fin_ss, fin_ms, fin_rms, fin_r, fin_o = (sem("gf_in"), sem("fin_t"), sem("fin_ss"),
                                                             sem("fin_ms"), sem("fin_rms"), sem("fin_r"), sem("fin_o"))
        st_out = [sem("st_out0"), sem("st_out1")]

        BY_POOL = tuple(range(1, TT))

        def raw_need(n):
            twice = [c for c in range(N3, N4 + 1) if c <= n and c % 2 == n % 2]
            return 16 * (n // 2 + 1) + 16 * len(twice)

        def proj_col(n):
            return O_POOL + P * n if n < U_GATE else O_GATE if n == U_GATE else O_GATE - 6 * P + P * (n - U_KC) if n < U_Q \
                else P * (n - U_Q)

        first_block = [0]
        for g, i in ITER:
            first_block.append(first_block[-1] + len(blocks(i)))

        def chunk(it, r):
            b = blocks(ITER[it][1])
            lo, hi = [round(len(b) * c / GR) for c in (r, r + 1)]
            return [(first_block[it] + k, *b[k]) for k in range(lo, hi)]

        Z_STEPS = 2 * KT - 2

        def gate_share(it, r):
            if it < Z_STEPS:
                return it + 1, KT // 2 * r, KT // 2 * (r + 1)
            c, n = (2 * r, 2) if it == Z_STEPS else (2 * GR + r, 1)
            return Z_STEPS + 1, c, c + n

        def branch_cols(i):
            a, b = n_slc(i), n_slc(i) + n_win(i)
            return (0, a), (a, b), (b, b + CP)

        def prob_col(i, kind, kb):
            if kind == "slc":
                return kb * P
            if kind == "win":
                return n_slc(i) + (kb - (i + 1 - n_win(i) // P)) * P
            return n_slc(i) + n_win(i)

        def fin_bank(t):
            return (psU if t >= 6 else psX)[:, 2 * (t % 2):2 * (t % 2) + 2].rearrange("p b n -> p (b n)")

        def turn_bank(t, q):
            return (psX[:, q], psX[:, 2 + q], psU[:, 2 + q])[t % 3]

        block = ctx.enter_context(nc.Block())

        @block.sync
        def _(sp):
            def load(n, src, slot):
                sp.wait_ge(w_hi, n - 1)
                sp.wait_ge(w_lo, n - 1)
                sp.dma_start(wraw[:, slot], src).then_inc(w_raw[slot], 16)

            for t in range(2):
                sp.dma_start(xt[:, t, :], x[0, t * P:(t + 1) * P, :]).then_inc(x_in[t], 16)
            sp.dma_start(g1b[:], norm1_g.partition_broadcast(P)).then_inc(g1_in, 16)
            for t in range(2, 4):
                sp.dma_start(xt[:, t, :], x[0, t * P:(t + 1) * P, :]).then_inc(x_in[t], 16)
            sp.dma_start(wraw[:, 0], w_in_u[:, :, bass.ds(proj_col(0), P)]).then_inc(w_raw[0], 16)
            for t in range(4, TT):
                sp.dma_start(xt[:, t, :], x[0, t * P:(t + 1) * P, :]).then_inc(x_in[t], 16)
            for lo, src in ((0, norm2_g), (KT, pool_scale)):
                gain_rows = src[0].rearrange("(k p) -> k p", p=P)
                sp.dma_start(grow[lo:lo + gain_rows.shape[0]], gain_rows).then_inc(const_in, 16)
            sp.dma_start(wraw[:, 1], w_in_u[:, :, bass.ds(proj_col(1), P)]).then_inc(w_raw[1], 16)
            sp.dma_start(cw1[:], cmp_w1[0].rearrange("b (j l) d h -> (l d) b j h", l=2)).then_inc(cw_in, 16)
            sp.dma_start(cw2[:, :, 0:HD], cmp_w2[0].rearrange("b h e -> h b e")).then_inc(cw_in, 16)
            sp.dma_start(cw2[:, :, HD:], cmp_w2[0].rearrange("b h e -> h b e")).then_inc(cw_in, 16)
            sp.dma_start(pet[:], cmp_pe[0].rearrange("b (j l) d -> j b (l d)", l=2)).then_inc(cw_in, 16)

            def load_unit(n):
                if n < N1:
                    load(n, w_in_u[:, :, bass.ds(proj_col(n), P)], n % 2)
                elif n < N3:
                    q = n - NZ
                    load(n, w_in_u[:, :, bass.ds(O_MERGE + (q % 2) * D + (q // 2) * P, P)], n % 2)
                else:
                    load_ab(n, n % 2, n - N3)

            def load_parts(n, slot, low, high):
                sp.wait_ge(w_hi, n - 1)
                sp.wait_ge(w_lo, n - 1)
                sp.dma_start(wraw[:, slot, 0:4], low).then_inc(w_raw[slot], 16)
                sp.dma_start(wraw[:, slot, 4:8], high).then_inc(w_raw[slot], 16)

            def load_ab(n, slot, m):
                load_parts(n, slot, w_ap_u[:, :, bass.ds(P * m, P)], w_pp_u[:, :, bass.ds(P * m, P)])

            def rows(unit):
                sp.wait_ge(st_proj[unit % 2], 16 * (unit // 2 + 1))
                return proj[unit * P:(unit + 1) * P, :]

            def load_shifted(dst, unit, s):
                src = rows(unit).rearrange("(g d) t -> d g t", d=HD)
                sp.dma_start(dst[0:HD], src).then_inc(s, 16)
                sp.dma_start(dst[HD:P, :, 0:S - 1], src[:, :, 1:S]).then_inc(s, 16)

            def load_twice(dst, unit, s):
                src = rows(unit).rearrange("(g d) t -> d g t", d=HD)
                for side in range(2):
                    sp.dma_start(dst[side * HD:(side + 1) * HD], src).then_inc(s, 16)

            def load_q(it):
                g, i = ITER[it]
                if it >= 2:
                    sp.wait_ge(q_lo, it - 1)
                src = proj[U_Q * P + g * GR * HD:U_Q * P + (g + 1) * GR * HD, i * P:(i + 1) * P]
                for side in range(2):
                    sp.dma_start(qraw[side * HD:(side + 1) * HD, it % 2], src.rearrange("(r d) t -> d r t", d=HD)) \
                        .then_inc(q_in[it % 2], 16)

            load_unit(2)
            load_unit(3)
            for n in range(N1):
                sp.wait_ge(ev[0], n + 1)
                sp.wait_ge(ev[1], n + 1)
                sp.dma_start(proj[n * P:(n + 1) * P, :], stage[:, n % 2]).then_inc(st_proj[n % 2], 16)
                if n == U_GATE:
                    for unit in range(4):
                        rows(unit)
                    sp.wait_ge(pad_ready, 1)
                    sp.dma_start(up[:, :, PAD:], proj[0:4 * P, :].rearrange("(k p) t -> p k t", p=P)).then_inc(u_in, 16)
                    sp.dma_start(wp[:], w_pool[0].rearrange("g c d -> c g d")).then_inc(pool_w_in, 16)
                if n == U_KC:
                    sp.dma_start(gtd[:], rows(U_GATE)[0:NG]).then_inc(gate_in, 16)
                if n == U_VC:
                    load_shifted(ldA, U_KC, kc_in)
                if n == U_KS:
                    load_shifted(ldB, U_VC, vc_in)
                if n == 9:
                    sp.wait_ge(misc, M_KHID)
                    sp.dma_start(ldA[:, 0], rows(U_VS)).then_inc(vs_in, 16)
                if n == 10:
                    sp.wait_ge(misc, M_VHID)
                    load_twice(ldB, U_KS, ks_in)
                if n == 11:
                    sp.dma_start(ldA[:, 1], rows(U_VW)).then_inc(vw_in, 16)
                load_unit(n + 4)
                if n == 12:
                    sp.wait_ge(misc, N_MISC)
                    load_twice(ldA, U_KW, kw_in)
                    for unit in (U_Q, U_Q + 1):
                        rows(unit)
                    sp.wait_ge(misc_ev, N_MISC)
                    load_q(0)
                    load_q(1)

            def store_z(q, h):
                sp.wait_ge(z_ready, 2 * q + h + 1)
                sp.dma_start(zscr[q * P:(q + 1) * P, h * HALF:(h + 1) * HALF], zst[:, h]).then_inc(st_z[h], 16)

            def store_o(it):
                g, i = ITER[it]
                sp.wait_ge(o_ready, it + 1)
                dst = oscr[g * GR * HD:(g + 1) * GR * HD, i * P:(i + 1) * P].rearrange("(r d) t -> d r t", d=HD)
                sp.dma_start(dst, ostg[:, it % 2].rearrange("d (r t) -> d r t", r=GR)).then_inc(st_o[it % 2], 16)

            for s in range(2):
                sp.wait_ge(st_proj[s], 16 * ((N1 + 1 - s) // 2))
            store_z(0, 0)
            store_z(0, 1)
            for it in range(NIT):
                if 1 <= it <= Z_STEPS:
                    store_z(it, 1)
                if it >= 1:
                    store_o(it - 1)
                if it + 2 < NIT:
                    load_q(it + 2)
                if it < Z_STEPS:
                    load_unit(NZ + it + 4)
                    store_z(it + 1, 0)
            def load_o(g):
                for s in range(2):
                    sp.wait_ge(st_o[s], 16 * (NIT // GROUPS // 2) * (g + 1))
                sp.dma_start(oraw[g][:], oscr[g * 2 * P:(g + 1) * 2 * P, :].rearrange("(k p) t -> p k t", p=P)).then_inc(o_in[g], 16)

            zscr_m = zscr.rearrange("(m z p) t -> m p z t", z=2, p=P)

            def load_gates(m, peeled):
                for h in range(2):
                    if not peeled:
                        sp.wait_ge(ab_read, 2 * m + h - 1)
                    sp.dma_start(mg[:, h], zscr_m[bass.ds(m, 1), :, :, h * HALF:(h + 1) * HALF]
                                 .rearrange("a p z t -> p (a z) t")).then_inc(mg_in[h], 16)

            def load_x(t, peeled, slot):
                if not peeled:
                    sp.wait_ge(xr_t, t - 1)
                sp.dma_start(xr[:, slot], x[0, bass.ds(P * t, P), :]).then_inc(xr_in[slot], 16)

            sp.wait_ge(s_win, GR * NIT)
            load_o(0)
            sp.wait_ge(pv_done, first_block[NIT])
            load_x(0, True, 0)
            load_x(1, True, 1)
            store_o(NIT - 1)
            load_o(1)
            load_ab(N3 + 2, N3 % 2, 2)
            load_gates(0, True)
            for h in range(2):
                store_z(2 * KT - 1, h)
            load_x(2, False, 0)
            load_ab(N3 + 3, (N3 + 1) % 2, 3)
            load_gates(1, False)
            with sp.Fori(1, KT // 2 - 1) as j:
                for u in range(2):
                    load_x(2 * j + u + 1, False, (u + 1) % 2)
                    load_ab(N3 + u + 2 + 2 * j, (N3 + u) % 2, 2 * j + u + 2)
                    load_gates(2 * j + u, False)
            load_x(KT - 1, False, (KT - 1) % 2)
            load_parts(N4, N4 % 2, w_out_u[:, 0:4, 0:P], w_out_u[:, 4:8, 0:P])
            load_gates(KT - 2, False)
            load(N4 + 1, w_out_u[:, :, P:2 * P], (N4 + 1) % 2)
            for h in range(2):
                sp.wait_ge(st_z[h], 16 * 2 * KT)
            load_gates(KT - 1, False)
            with sp.Fori(1, KT // 2) as j:
                for u in range(2):
                    load(N4 + u + 2 * j, w_out_u[:, :, bass.ds(P * (2 * j) + P * u, P)], (N4 + u) % 2)

            def load_up(r):
                with sp.Fori(0, KT // 2) as j:
                    for u in range(2):
                        load(N5 + u + 2 * j + 2 * KT * r, w_ff1_u[:, :, bass.ds(D * r + P * 2 * j + P * u, P)], (N5 + u) % 2)

            with sp.Fori(0, ROUNDS - 1) as r:
                load_up(r)
                with sp.Fori(0, KT // 2) as j:
                    for u in range(2):
                        load(N5 + KT + u + 2 * j + 2 * KT * r,
                             w_ff2_u[:, bass.ds(KT * r, KT), bass.ds(P * 2 * j + P * u, P)], (N5 + u) % 2)
            load_up(ROUNDS - 1)

            def store_out(t):
                sp.wait_ge(fin_o, t + 1)
                sp.dma_start(out[0, t * P:(t + 1) * P, :], ost[:, t % 2]).then_inc(st_out[t % 2], 16)

            for i in range(HALVES):
                m = i % KT
                load(NL + i, w_ff2_u[:, KT * (ROUNDS - 1):KT * ROUNDS, m * P:(m + 1) * P], (NL + i) % 2)
                if i == 3:
                    sp.wait_ge(u_done, 2 * NL)
                    sp.dma_start(gfb[:], final_g.partition_broadcast(P)).then_inc(gf_in, 16)
                if i >= HALVES - TT // 2:
                    store_out(i - (HALVES - TT // 2))
            for t in range(TT // 2, TT):
                store_out(t)
            for s in range(2):
                sp.wait_ge(st_out[s], 16 * TT // 2)

        @block.gpsimd
        def _(pool):
            count = [0]

            def link(ins):
                count[0] += 1
                ins.then_inc(chain_p, 1)
                pool.wait_ge(chain_p, count[0])

            link(pool.memset(ident[:], 0.0))
            link(pool.affine_select(out=ident[:], in_=ident[:], compare_op=ALU.not_equal, fill=1.0, base=0,
                                    pattern=[[-1, P]], channel_multiplier=1))
            pool.memset(ones[:], 1.0)
            link(pool.memset(qscale[:], 1.0))
            for j in range(4):
                for side in range(2):
                    last = pool.memset(qscale[side * HD:(side + 1) * HD, U_Q + j:U_Q + j + 1],
                                       2.0 ** (2 * j + side + 1) * HD ** -0.5)
            last.then_inc(consts, 1)

            pool.wait_ge(consts, 1)
            pool.wait_ge(g1_in, 16)
            for t in BY_POOL:
                pool.wait_ge(ss_ready, t + 1)
                nc.gpsimd.tensor_tensor(xt[:, t, :], xt[:, t, :], g1b[:], ALU.mult).then_inc(xg_ready, 1)

            pool.iota(T1[:], pattern=[[1, S]], base=-(S - P), channel_multiplier=-1,
                      allow_small_or_imprecise_dtypes=True)
            pool.iota(TW[:], pattern=[[1, (WIN_TILES + 1) * P]], base=-WIN_TILES * P, channel_multiplier=-1,
                      allow_small_or_imprecise_dtypes=True)
            link(pool.iota(TC[:], pattern=[[-P, TT], [CSTRIDE, CP]], base=CBLOCK - 1, channel_multiplier=-1,
                           allow_small_or_imprecise_dtypes=True))
            pool.affine_select(out=T1[:], in_=T1[:], compare_op=ALU.is_ge, fill=NEG, base=S - P,
                               pattern=[[-1, S]], channel_multiplier=1)
            link(pool.affine_select(out=TW[:], in_=TW[:], compare_op=ALU.is_ge, fill=NEG, base=WIN_TILES * P,
                                    pattern=[[-1, (WIN_TILES + 1) * P]], channel_multiplier=1))
            link(pool.affine_select(out=TC[:], in_=TC[:], compare_op=ALU.is_ge, fill=NEG, base=-(CBLOCK - 1),
                                    pattern=[[P, TT], [-CSTRIDE, CP]], channel_multiplier=1))
            link(pool.affine_select(out=TW[:, 0:P], in_=TW[:, 0:P], compare_op=ALU.is_gt, fill=NEG, base=0,
                                    pattern=[[1, P]], channel_multiplier=-1))
            link(pool.memset(TC[:, :, NCMP:CP], NEG))
            link(pool.memset(cvalid[:], 1.0))
            link(pool.affine_select(out=cvalid[:], in_=cvalid[:], compare_op=ALU.is_ge, fill=0.0, base=-(CBLOCK - 1),
                                    pattern=[[0, 1]], channel_multiplier=1))
            pool.wait_ge(xt_ready, TT)
            pool.memset(up[:, :, 0:PAD], 0.0)
            pool.memset(tA[:, 0:PAD], 0.0)
            pool.memset(tB[:, 0:PAD], 0.0)
            link(pool.iota(icnt[:], pattern=[[0, 4], [1, PAD]], base=1, channel_multiplier=0,
                           allow_small_or_imprecise_dtypes=True))
            for k in range(4):
                last = pool.tensor_scalar(icnt[:, k], icnt[:, k], float(2 ** (k + 1)), None, ALU.min)
            last.then_inc(pad_ready, 1)
            pool.memset(chid[:, :, :, NCMP:CP], 0.0).then_inc(consts, 1)

            for n in range(NZ + 2, N3):
                pool.wait_ge(w_hi, n + 1)
                pool.wait_ge(w_lo, n)
                nc.gpsimd.tensor_tensor(wlo[:, n % 2], wraw[:, n % 2], whi[:, n % 2].bitcast(f32), ALU.subtract).then_inc(w_lo, 1)

            for m in range(KT):
                for h in range(2):
                    s = 2 * m + h
                    pool.wait_ge(res[h], m + 1)
                    xs = xT[:, m, h * HALF:(h + 1) * HALF]
                    if m == 0:
                        pool.tensor_tensor(sqa[:, h * HALF:(h + 1) * HALF], xs, xs, ALU.mult).then_inc(sq_sum, 1)
                    else:
                        link(pool.tensor_tensor(sqt[:], xs, xs, ALU.mult))
                        pool.wait_ge(sq_sum, s)
                        pool.tensor_tensor(sqa[:, h * HALF:(h + 1) * HALF], sqa[:, h * HALF:(h + 1) * HALF], sqt[:],
                                           ALU.add).then_inc(sq_sum, 1)
                        pool.wait_ge(sq_sum, s + 1)

        @block.scalar
        def _(act):
            def split_hi(n, slot, raw_count, first=False):
                act.wait_ge(w_raw[slot], raw_count)
                if not first:
                    act.wait_ge(u_done, 2 * (n - 1))
                nc.scalar.activation(whi[:, slot], wraw[:, slot], ACT.Copy).then_inc(w_hi, 1)

            def root(t):
                act.wait_ge(ms_ready, t + 1)
                nc.scalar.activation(rms[:, t:t + 1], msq[:, t:t + 1], ACT.Sqrt).then_inc(rms_ready, 1)

            def h_high(t):
                act.wait_ge(xt_ready, t + 1)
                for q in range(2):
                    nc.scalar.activation(ahi[:, 4 * q:4 * q + 4, t * P:(t + 1) * P],
                                         turn_bank(t, q).rearrange("p (k t) -> p k t", k=4), ACT.Copy).then_inc(h_hi, 1)

            for t in range(TT):
                act.wait_ge(x_in[t], 16)
                if t:
                    act.wait_ge(ss_ready, t)
                nc.scalar.activation(sqj[:], xt[:, t, :], ACT.Square, accum_out=ssum[:, t:t + 1]).then_inc(ss_ready, 1)
                if t >= 1:
                    root(t - 1)
                if t == 2:
                    split_hi(0, 0, 16, first=True)
                if t >= 3:
                    h_high(t - 3)
            root(TT - 1)
            for t in range(TT - 3, TT):
                h_high(t)

            def evac_proj(n, slot, col, reuse=None):
                act.wait_ge(u_done, 2 * n + 1)
                if reuse is not None:
                    act.wait_ge(st_proj[slot], reuse)
                nc.scalar.activation(stage[:, slot, 0:HALF], psU[:, 2 * slot], ACT.Copy, scale=qscale[:, col]).then_inc(ev[0], 1)

            act.wait_ge(consts, 1)
            act.wait_ge(xs_ready, TT)

            def gelu_tanh_of(b):
                act.wait_ge(gelu_arg, b + 1)
                nc.scalar.activation(cz[:, 0:GROUPS * NCMP], cv[:, 0:GROUPS * NCMP], ACT.Tanh, scale=GELU_C).then_inc(gelu_tanh, 1)

            def value_hi(s, vt, q):
                act.wait_ge(misc, s)
                ps = psX[:, (s - 1) % 4].rearrange("p (t g d) -> p t g d", t=4, g=GROUPS)
                nc.scalar.activation(vt[:, 4 * q:4 * q + 4, :, 0:HD], ps, ACT.Copy).then_inc(v_hi, 1)

            def key_hi(dst, src, s):
                act.wait_ge(s, 32)
                nc.scalar.activation(dst[:], src[:], ACT.Copy).then_inc(k_hi, 1)

            def query_hi(it):
                act.wait_ge(q_in[it % 2], 32 * (it // 2 + 1))
                if it >= 2:
                    act.wait_ge(s_win, GR * (it - 1))
                nc.scalar.activation(qh[:, it % 2], qraw[:, it % 2], ACT.Copy).then_inc(q_hi, 1)

            for n in range(N1):
                split_hi(n + 1, (n + 1) % 2, raw_need(n + 1), first=(n == 0))
                if n == N1 - 1:
                    query_hi(0)
                    query_hi(1)
                evac_proj(n, n % 2, slice(n, n + 1), 16 * (n // 2) if n >= 2 else None)
                if n == 8:
                    gelu_tanh_of(0)
                if n == 9:
                    gelu_tanh_of(1)
                if n == 11:
                    value_hi(M_VS, vS, 0)
                    value_hi(M_VS + 1, vS, 1)
                    key_hi(kS, ldB, ks_in)
                if n == 12:
                    act.wait_ge(misc, M_GATE)
                    nc.scalar.activation(gate_t[:], psX[:, (M_GATE - 1) % 4, 0:TT * NG], ACT.Tanh, scale=0.5).then_inc(gate_tanh, 1)
                    value_hi(M_VW, vW, 0)
                    value_hi(M_VW + 1, vW, 1)
                if n == 13:
                    key_hi(kW, ldA, kw_in)

            def exponentials(it, r, k):
                g, i = ITER[it]
                lo, hi = branch_cols(i)[k]
                if k == 0:
                    act.wait_ge(nb_ready, it * GR + r + 1)
                nc.scalar.activation(PB[it % 2][:, r, lo:hi], PB[it % 2][:, r, lo:hi], ACT.Exp,
                                     scale=2.0 ** -(g * GR + r + 1), bias=nb[:, it % 2, r, k:k + 1],
                                     accum_out=esum[:, it % 2, r, k:k + 1]).then_inc(exp_done, 1)

            def prob_hi(B, kind):
                rows = CP if kind == "cmp" else P
                act.wait_ge(t_done, B + 1)
                if B >= 2:
                    act.wait_ge(pv_done, B - 1)
                nc.scalar.activation(pth[0:rows, B % 2], psX[0:rows, B % 2], ACT.Copy).then_inc(pt_hi, 1)

            def out_half(it):
                act.wait_ge(pv_done, first_block[it + 1])
                if it >= 1:
                    act.wait_ge(o_ready, it)
                nc.scalar.activation(otmp[:], psX[HD:P, 2], ACT.Copy).then_inc(o_half, 1)

            def gate_hi(q, h):
                act.wait_ge(u_done, 2 * (NZ + q) + h + 1)
                if q:
                    act.wait_ge(st_z[h], 16 * q)
                nc.scalar.activation(zst[:, h], psX[:, 3], ACT.Tanh, scale=0.5).then_inc(z_ready, 1)

            split_hi(NZ + 1, (NZ + 1) % 2, raw_need(NZ + 1))
            for r in range(GR):
                for k in range(3):
                    exponentials(0, r, k)
                if r == 0:
                    gate_hi(0, 0)
            gate_hi(0, 1)
            for it in range(NIT):
                for r in range(GR):
                    if r == 0 and 1 <= it <= Z_STEPS:
                        gate_hi(it, 1)
                    if r == 0 and it == Z_STEPS + 1:
                        gate_hi(it, 0)
                    if r == 0 and it < Z_STEPS:
                        split_hi(NZ + it + 2, (NZ + it) % 2, raw_need(NZ + it + 2))
                    if r == 2 and it < Z_STEPS:
                        gate_hi(it + 1, 0)
                    if r == 1 and it + 2 < NIT:
                        query_hi(it + 2)
                    todo = chunk(it, r)
                    for k in range(max(len(todo), 3)):
                        if k < len(todo):
                            prob_hi(todo[k][0], todo[k][1])
                        if k < 3 and it + 1 < NIT:
                            exponentials(it + 1, r, k)
                out_half(it)

            def part_hi(dst, src):
                nc.scalar.activation(dst, src, ACT.Copy).then_inc(yo_hi, 1)

            split_hi(N3, N3 % 2, raw_need(N3))
            for h in range(2):
                part_hi(yhi[:, :, h * HALF:(h + 1) * HALF], yraw[:, :, h * HALF:(h + 1) * HALF])
            act.wait_ge(o_in[0], 16)
            part_hi(ohi[:, 0:2], oraw[0][:])
            act.wait_ge(o_in[1], 16)
            for h in range(2):
                part_hi(ohi[:, 2:4, h * HALF:(h + 1) * HALF], oraw[1][:, :, h * HALF:(h + 1) * HALF])
            gate_hi(2 * KT - 1, 1)
            act.wait_ge(yo_lo, 5)

            def mixed(m, u):
                act.wait_ge(xr_t, m + 1)
                nc.scalar.activation(xT[:, 0:4, bass.ds(P * m, P)],
                                     psX[:, 2 * u].rearrange("p (k t) -> p k t", k=4), ACT.Copy).then_inc(xT_a, 1)
                for h in range(2):
                    act.wait_ge(c_sum, 2 * m + h + 1)
                    nc.scalar.activation(ahi[:, bass.ds(m, 1), h * HALF:(h + 1) * HALF], ct[:, h:h + 1], ACT.Copy,
                                         scale=0.5).then_inc(c_hi, 1)

            with act.Fori(0, KT // 2) as j:
                for u in range(2):
                    n = N3 + u
                    split_hi(n + 1 + 2 * j, (n + 1) % 2, 32 * j + raw_need(n + 1))
                    mixed(2 * j + u, u)

            def out_evac(m):
                for h in range(2):
                    act.wait_ge(res[h], m + 1)
                    nc.scalar.activation(h2hi[:, bass.ds(m, 1), h * HALF:(h + 1) * HALF], xT[:, bass.ds(m, 1), h * HALF:(h + 1) * HALF],
                                         ACT.Copy, scale=g2[:, bass.ds(m, 1)]).then_inc(h2_hi, 1)

            with act.Fori(0, KT // 2) as j:
                for u in range(2):
                    n = N4 + u
                    split_hi(n + 1 + 2 * j, (n + 1) % 2, 16 * j + raw_need(n + 1))
                    out_evac(2 * j + u)

            def up_evac(n, u, s, t):
                for h in range(2):
                    act.wait_ge(u_done, 2 * n + h + 1)
                    nc.scalar.activation(rel[:, h], psU[:, 2 * u + h], ACT.Relu).then_inc(relu[h], 1)
                for h in range(2):
                    act.wait_ge(rsq_ready, s + h + 1)
                    nc.scalar.activation(ahi[:, bass.ds(t, 1), h * HALF:(h + 1) * HALF], rsq[:, h:h + 1], ACT.Copy).then_inc(hid_hi, 1)

            def up_round(r):
                with act.Fori(0, KT // 2) as j:
                    for u in range(2):
                        n = N5 + u
                        split_hi(n + 1 + 2 * j + 2 * KT * r, (n + 1) % 2, 16 * j + 16 * KT * r + raw_need(n + 1))
                        up_evac(n + 2 * j + 2 * KT * r, u, 2 * KT * r + 4 * j + 2 * u, 2 * j + u)

            with act.Fori(0, ROUNDS - 1) as r:
                up_round(r)
                n = N5 + KT
                with act.Fori(0, KT // 2) as j:
                    for u in range(2):
                        split_hi(n + u + 1 + 2 * j + 2 * KT * r, (n + u + 1) % 2,
                                 16 * j + 16 * KT * r + raw_need(n + u + 1))
            up_round(ROUNDS - 1)

            def square_f(t):
                act.wait_ge(fin_t, t + 1)
                if t:
                    act.wait_ge(fin_ss, t)
                nc.scalar.activation(sqo[:], fin_bank(t), ACT.Square, accum_out=ssum[:, t:t + 1]).then_inc(fin_ss, 1)

            def root_f(t):
                act.wait_ge(fin_ms, t + 1)
                nc.scalar.activation(rms[:, t:t + 1], msq[:, t:t + 1], ACT.Sqrt).then_inc(fin_rms, 1)

            for i in range(HALVES):
                if i + 1 < HALVES:
                    n = NL + i + 1
                    act.wait_ge(w_raw[n % 2], raw_need(n))
                    act.wait_ge(u_done, 2 * NL + i)
                    nc.scalar.activation(whi[:, n % 2], wraw[:, n % 2], ACT.Copy).then_inc(w_hi, 1)
                if FIN_STEP <= i < FIN_STEP + TT // 2:
                    square_f(i - FIN_STEP)
                    root_f(i - FIN_STEP)
            for t in range(TT // 2, TT):
                square_f(t)
                if t > TT // 2:
                    root_f(t - 1)
            root_f(TT - 1)

        @block.vector
        def _(dve):
            count = [0]

            def link(ins):
                count[0] += 1
                ins.then_inc(chain_v, 1)
                dve.wait_ge(chain_v, count[0])

            def split_lo(n, slot):
                dve.wait_ge(w_hi, n + 1)
                nc.vector.tensor_tensor(wlo[:, slot], wraw[:, slot], whi[:, slot].bitcast(f32), ALU.subtract).then_inc(w_lo, 1)

            def mean_sq(t):
                dve.wait_ge(ss_ready, t + 1)
                nc.vector.tensor_scalar(msq[:, t:t + 1], ssum[:, t:t + 1], 1.0 / D, EPS, ALU.mult, ALU.add).then_inc(ms_ready, 1)

            def normalize(t):
                dve.wait_ge(rms_ready, t + 1)
                nc.vector.reciprocal(rstd[:, t:t + 1], rms[:, t:t + 1]).then_inc(rstd_ready, 1)
                dve.wait_ge(rstd_ready, t + 1)
                if t in BY_POOL:
                    dve.wait_ge(xg_ready, BY_POOL.index(t) + 1)
                    nc.vector.tensor_scalar(xt[:, t, :], xt[:, t, :], rstd[:, t:t + 1], None, ALU.mult).then_inc(xs_ready, 1)
                else:
                    dve.wait_ge(g1_in, 16)
                    nc.vector.scalar_tensor_tensor(out=xt[:, t, :], in0=xt[:, t, :], scalar=rstd[:, t:t + 1], in1=g1b[:],
                                                   op0=ALU.mult, op1=ALU.mult).then_inc(xs_ready, 1)

            def h_low(t):
                for q in range(2):
                    dve.wait_ge(h_hi, 2 * t + q + 1)
                    last = nc.vector.tensor_tensor(alo[:, 4 * q:4 * q + 4, t * P:(t + 1) * P],
                                                   turn_bank(t, q).rearrange("p (k t) -> p k t", k=4),
                                                   ahi[:, 4 * q:4 * q + 4, t * P:(t + 1) * P].bitcast(f32), ALU.subtract)
                last.then_inc(h_lo, 1)

            mean_sq(0)
            for t in range(TT):
                if t + 1 < TT:
                    mean_sq(t + 1)
                normalize(t)
                if t == 2:
                    split_lo(0, 0)
                if t >= 2:
                    h_low(t - 2)
            dve.wait_ge(gain_t, 1)
            nc.vector.tensor_copy(gcol[:], psU[:, 1, 0:KT + 4]).then_inc(gain_ready, 1)
            h_low(TT - 2)
            h_low(TT - 1)

            def evac_proj(n, slot, col, reuse=None):
                dve.wait_ge(u_done, 2 * n + 2)
                if reuse is not None:
                    dve.wait_ge(st_proj[slot], reuse)
                nc.vector.tensor_scalar(stage[:, slot, HALF:], psU[:, 2 * slot + 1], qscale[:, col], None, ALU.mult).then_inc(ev[1], 1)

            step = [0]

            def wait_misc():
                step[0] += 1
                dve.wait_ge(misc, step[0])
                return psX[:, (step[0] - 1) % 4]

            def pool_mix(k):
                cur, bufs = up[:, k], [tA, tB]
                for d in range(k + 1):
                    nxt = bufs[d % 2]
                    link(nc.vector.tensor_tensor(nxt[:, PAD:], cur[:, PAD:], cur[:, PAD - 2 ** d:PAD + S - 2 ** d], ALU.add))
                    cur = nxt
                dst = bufs[(k + 1) % 2]
                nc.vector.tensor_tensor(dst[:, PAD:2 * PAD], cur[:, PAD:2 * PAD], icnt[:, k], ALU.mult)
                link(nc.vector.tensor_scalar(dst[:, 2 * PAD:], cur[:, 2 * PAD:], 2.0 ** -(k + 1), None, ALU.mult))
                nc.vector.tensor_tensor(up[:, k, PAD:], dst[:, PAD:], up[:, k, PAD:], ALU.subtract).then_inc(pooled, 1)
                dve.wait_ge(pooled, k + 1)

            def take_y(s):
                k, h = s // 2, s % 2
                ps = wait_misc()
                nc.vector.tensor_scalar(yraw[:, k, h * HALF:(h + 1) * HALF], ps, psc[:, k:k + 1], None,
                                        ALU.mult).then_inc(misc_ev, 1)

            def value_lo(vt, q, count):
                ps = wait_misc().rearrange("p (t g d) -> p t g d", t=4, g=GROUPS)
                dve.wait_ge(v_hi, count)
                nc.vector.tensor_tensor(vt[:, 4 * q:4 * q + 4, :, HD:], ps, vt[:, 4 * q:4 * q + 4, :, 0:HD].bitcast(f32),
                                        ALU.subtract).then_inc(misc_ev, 1)

            def key_lo(b, dst, src):
                dve.wait_ge(k_hi, b + 1)
                nc.vector.tensor_tensor(dst[HD:P], src[HD:P], dst[HD:P].bitcast(f32), ALU.subtract).then_inc(k_ready, 1)

            n2 = GROUPS * NCMP

            def hidden(b):
                ps = wait_misc()
                link(nc.vector.tensor_scalar(cu[:, b, 0:n2], ps[0:HD, 0:n2], cb[:, b:b + 1], None, ALU.add))
                link(nc.vector.tensor_tensor(cv[:, 0:n2], cu[:, b, 0:n2], cu[:, b, 0:n2], ALU.mult))
                link(nc.vector.tensor_scalar(cv[:, 0:n2], cv[:, 0:n2], 0.044715, 1.0, ALU.mult, ALU.add))
                nc.vector.tensor_tensor(cv[:, 0:n2], cv[:, 0:n2], cu[:, b, 0:n2], ALU.mult).then_inc(gelu_arg, 1)
                dve.wait_ge(gelu_tanh, b + 1)
                nc.vector.scalar_tensor_tensor(out=chid[:, b, :, 0:NCMP], in0=cz[:, 0:n2].rearrange("p (g c) -> p g c", g=GROUPS),
                                               scalar=1.0, in1=cu[:, b, 0:n2].rearrange("p (g c) -> p g c", g=GROUPS),
                                               op0=ALU.add, op1=ALU.mult).then_inc(misc_ev, 1)

            def compressed(b):
                ps = wait_misc()[:, 0:P]
                if b == 0:
                    link(nc.vector.tensor_scalar(kcs[:], ps, 0.5, None, ALU.mult))
                    link(nc.vector.tensor_copy(kC[:].rearrange("p g c -> p (g c)"), kcs[:]))
                    nc.vector.tensor_tensor(kC[HD:P].rearrange("p g c -> p (g c)"), kcs[HD:P],
                                            kC[HD:P].rearrange("p g c -> p (g c)").bitcast(f32), ALU.subtract).then_inc(misc_ev, 1)
                else:
                    link(nc.vector.tensor_scalar(kcs[0:CP], ps[0:CP], 0.5, None, ALU.mult))
                    kv = kcs[0:CP].rearrange("c (g d) -> c g d", g=GROUPS)
                    link(nc.vector.tensor_copy(vC[:, :, 0:HD], kv))
                    nc.vector.tensor_tensor(vC[:, :, HD:], kv, vC[:, :, 0:HD].bitcast(f32), ALU.subtract).then_inc(misc_ev, 1)

            def query_lo(it):
                dve.wait_ge(q_hi, it + 1)
                nc.vector.tensor_tensor(ql[:, it % 2], qraw[:, it % 2], qh[:, it % 2].bitcast(f32), ALU.subtract).then_inc(q_lo, 1)

            for n in range(N1):
                split_lo(n + 1, (n + 1) % 2)
                if n == N1 - 1:
                    query_lo(0)
                    query_lo(1)
                evac_proj(n, n % 2, slice(n, n + 1), 16 * (n // 2) if n >= 2 else None)
                if n == 0:
                    dve.wait_ge(pad_ready, 1)
                    nc.vector.reciprocal(icnt[:], icnt[:]).then_inc(icnt_ready, 1)
                    dve.wait_ge(icnt_ready, 1)
                if n == 5:
                    dve.wait_ge(u_in, 16)
                    pool_mix(0)
                    pool_mix(1)
                if n == 6:
                    ps = wait_misc()
                    nc.vector.tensor_copy(pe2[:].rearrange("p b j -> p (b j)"), ps[:, 0:CBLOCK]).then_inc(misc_ev, 1)
                    pool_mix(2)
                if n == 7:
                    ps = wait_misc()
                    nc.vector.tensor_copy(cb[:], ps[0:HD, 0:2]).then_inc(misc_ev, 1)
                    pool_mix(3)
                if n == 8:
                    dve.wait_ge(consts, 2)
                    hidden(0)
                if n == 9:
                    compressed(0)
                    hidden(1)
                if n == 10:
                    compressed(1)
                    for s in range(4):
                        take_y(s)
                if n == 11:
                    for s in range(4, 8):
                        take_y(s)
                    value_lo(vS, 0, 1)
                    value_lo(vS, 1, 2)
                    key_lo(0, kS, ldB)
                if n == 12:
                    wait_misc()
                    dve.wait_ge(gate_tanh, 1)
                    link(nc.vector.tensor_scalar(gates[:].rearrange("p t h b -> p (t h b)"), gate_t[:], 1.0, 0.5, ALU.add, ALU.mult))
                    nc.vector.tensor_scalar(gates[:, 0, :, 0:1], gates[:, 0, :, 0:1], cvalid[:, 0:1], None, ALU.mult).then_inc(misc_ev, 1)
                    value_lo(vW, 0, 3)
                    value_lo(vW, 1, 4)
                if n == 13:
                    key_lo(1, kW, ldA)

            def maxima(it, r):
                g, i = ITER[it]
                e = it * GR + r
                head = g * GR + r
                row = PB[it % 2]
                a, b = n_slc(i), n_slc(i) + n_win(i)
                if it == 1 and r == 0:
                    for slot in range(2):
                        dve.wait_ge(st_proj[slot], 16 * ((N1 + 1 - slot) // 2))
                if it >= 2 and r == 0:
                    dve.wait_ge(t_done, first_block[it - 1])
                dve.wait_ge(s_slc, e + 1)
                nc.vector.tensor_tensor_reduce(out=row[:, r, 0:a], in0=psS0[:, 0:a], in1=T1[:, S - a:S], scale=1.0, scalar=-3e38,
                                               op0=ALU.add, op1=ALU.max, accum_out=mx[:, it % 2, r, 0:1]).then_inc(m_slc, 1)
                dve.wait_ge(s_win, e + 1)
                nc.vector.tensor_tensor_reduce(out=row[:, r, a:b], in0=psS1[:, 0:b - a], in1=TW[:, (WIN_TILES + 1) * P - (b - a):],
                                               scale=1.0, scalar=-3e38, op0=ALU.add, op1=ALU.max, accum_out=mx[:, it % 2, r, 1:2])
                nc.vector.tensor_tensor_reduce(out=row[:, r, b:b + CP], in0=psS1[:, b - a:b - a + CP], in1=TC[:, i], scale=1.0,
                                               scalar=-3e38, op0=ALU.add, op1=ALU.max, accum_out=mx[:, it % 2, r, 2:3]).then_inc(m_win, 1)
                dve.wait_ge(m_win, e + 1)
                nc.vector.tensor_scalar(nb[:, it % 2, r], mx[:, it % 2, r], -2.0 ** -(head + 1), None, ALU.mult).then_inc(nb_ready, 1)

            def weights(it, r):
                g, i = ITER[it]
                head = g * GR + r
                w = rs[:, it % 2, r]
                row = PB[it % 2]
                dve.wait_ge(exp_done, 3 * (it * GR + r + 1))
                link(nc.vector.reciprocal(w, esum[:, it % 2, r]))
                nc.vector.tensor_tensor(w[:, 0:2], gates[:, i, head, 1:3], w[:, 0:2], ALU.mult)
                link(nc.vector.tensor_tensor(w[:, 2:3], gates[:, i, head, 0:1], w[:, 2:3], ALU.mult))
                for k, (lo, hi) in enumerate(branch_cols(i)):
                    last = nc.vector.tensor_scalar(row[:, r, lo:hi], row[:, r, lo:hi], w[:, k:k + 1], None, ALU.mult)
                last.then_inc(p_ready, 1)

            def prob_lo(B, kind):
                rows = CP if kind == "cmp" else P
                dve.wait_ge(pt_hi, B + 1)
                nc.vector.tensor_tensor(ptl[0:rows, B % 2], psX[0:rows, B % 2], pth[0:rows, B % 2].bitcast(f32),
                                        ALU.subtract).then_inc(pt_lo, 1)

            def out_sum(it):
                dve.wait_ge(o_half, it + 1)
                if it >= 2:
                    dve.wait_ge(st_o[it % 2], 16 * (it // 2))
                nc.vector.tensor_tensor(ostg[:, it % 2], psX[0:HD, 2], otmp[:], ALU.add).then_inc(o_ready, 1)

            split_lo(NZ + 1, (NZ + 1) % 2)
            for r in range(GR):
                maxima(0, r)
                if r:
                    weights(0, r - 1)
            weights(0, GR - 1)
            for it in range(NIT):
                for r in range(GR):
                    if r == 0 and it:
                        out_sum(it - 1)
                    if it + 1 < NIT:
                        maxima(it + 1, r)
                    if r == 1 and it + 2 < NIT:
                        query_lo(it + 2)
                    todo = chunk(it, r)
                    own = min(len(todo), 3) if r == GR - 1 else None
                    for k in range(len(todo) + 1):
                        if k == min(len(todo), 1) and r and it + 1 < NIT:
                            weights(it + 1, r - 1)
                        if k == own and it + 1 < NIT:
                            weights(it + 1, r)
                        if k < len(todo):
                            prob_lo(todo[k][0], todo[k][1])
            out_sum(NIT - 1)

            def part_lo(dst, src, hi, count):
                dve.wait_ge(yo_hi, count)
                nc.vector.tensor_tensor(dst, src, hi.bitcast(f32), ALU.subtract).then_inc(yo_lo, 1)

            dve.wait_ge(w_lo, N3)
            split_lo(N3, N3 % 2)
            for h in range(2):
                cols = slice(h * HALF, (h + 1) * HALF)
                part_lo(ylo[:, :, cols], yraw[:, :, cols], yhi[:, :, cols], h + 1)
            part_lo(olo[:, 0:2], oraw[0][:], ohi[:, 0:2], 3)
            for h in range(2):
                cols = slice(h * HALF, (h + 1) * HALF)
                part_lo(olo[:, 2:4, cols], oraw[1][:, :, cols], ohi[:, 2:4, cols], h + 4)
            for h in range(2):
                dve.wait_ge(st_z[h], 16 * 2 * KT)

            def mix(n, m, u):
                dve.wait_ge(xr_t, m + 1)
                nc.vector.tensor_copy(xT[:, 4:8, bass.ds(P * m, P)],
                                      psX[:, 2 * u + 1].rearrange("p (k t) -> p k t", k=4)).then_inc(xT_v, 1)
                for h in range(2):
                    dve.wait_ge(u_done, 2 * n + h + 1)
                    dve.wait_ge(mg_in[h], 16 * (m + 1))
                    nc.vector.scalar_tensor_tensor(out=mt[:, 0], in0=mg[:, h, 0], scalar=1.0, in1=psU[:, 2 * h], op0=ALU.add,
                                                   op1=ALU.mult)
                    nc.vector.scalar_tensor_tensor(out=mt[:, 1], in0=mg[:, h, 1], scalar=1.0, in1=psU[:, 2 * h + 1], op0=ALU.add,
                                                   op1=ALU.mult).then_inc(ab_read, 1)
                    dve.wait_ge(ab_read, 2 * m + h + 1)
                    nc.vector.tensor_tensor(ct[:, h], mt[:, 0], mt[:, 1], ALU.add).then_inc(c_sum, 1)
                    dve.wait_ge(c_sum, 2 * m + h + 1)
                for h in range(2):
                    cols = slice(h * HALF, (h + 1) * HALF)
                    dve.wait_ge(c_hi, 2 * m + h + 1)
                    nc.vector.scalar_tensor_tensor(out=alo[:, bass.ds(m, 1), cols], in0=ct[:, h:h + 1], scalar=0.5,
                                                   in1=ahi[:, bass.ds(m, 1), cols].bitcast(f32), op0=ALU.mult,
                                                   op1=ALU.subtract).then_inc(c_lo, 1)
                dve.wait_ge(c_lo, 2 * m + 2)

            with dve.Fori(0, KT // 2) as j:
                for u in range(2):
                    n = N3 + u
                    split_lo(n + 1 + 2 * j, (n + 1) % 2)
                    mix(n + 2 * j, 2 * j + u, u)
            dve.wait_ge(xT_a, TT)
            dve.wait_ge(xT_v, TT)

            def out_evac(n, u, m, s):
                for h in range(2):
                    dve.wait_ge(u_done, 2 * n + h + 1)
                    cols = slice(h * HALF, (h + 1) * HALF)
                    nc.vector.tensor_tensor(xT[:, bass.ds(m, 1), cols], psU[:, 2 * u + h:2 * u + h + 1],
                                            xT[:, bass.ds(m, 1), cols], ALU.add).then_inc(res[h], 1)
                for h in range(2):
                    cols = slice(h * HALF, (h + 1) * HALF)
                    dve.wait_ge(h2_hi, s + h + 1)
                    nc.vector.scalar_tensor_tensor(out=h2lo[:, bass.ds(m, 1), cols], in0=xT[:, bass.ds(m, 1), cols],
                                                   scalar=g2[:, bass.ds(m, 1)], in1=h2hi[:, bass.ds(m, 1), cols].bitcast(f32),
                                                   op0=ALU.mult, op1=ALU.subtract).then_inc(h2_lo, 1)

            with dve.Fori(0, KT // 2) as j:
                for u in range(2):
                    n = N4 + u
                    split_lo(n + 1 + 2 * j, (n + 1) % 2)
                    out_evac(n + 2 * j, u, 2 * j + u, 4 * j + 2 * u)

            def up_evac(s, c, t):
                for h in range(2):
                    dve.wait_ge(relu[h], c + 1)
                    nc.vector.tensor_tensor(rsq[:, h], rel[:, h], rel[:, h], ALU.mult).then_inc(rsq_ready, 1)
                for h in range(2):
                    dve.wait_ge(hid_hi, s + h + 1)
                    nc.vector.tensor_tensor(alo[:, bass.ds(t, 1), h * HALF:(h + 1) * HALF], rsq[:, h:h + 1],
                                            ahi[:, bass.ds(t, 1), h * HALF:(h + 1) * HALF].bitcast(f32), ALU.subtract).then_inc(hid_lo, 1)
                dve.wait_ge(hid_lo, s + 2)

            def down_evac(n, u, m, s):
                for h in range(2):
                    cols = slice(h * HALF, (h + 1) * HALF)
                    dve.wait_ge(u_done, 2 * n + h + 1)
                    nc.vector.tensor_tensor(f2t[:, h], psU[:, 2 * u + h], r2[:, cols], ALU.mult).then_inc(mul_r2, 1)
                    dve.wait_ge(mul_r2, s + h + 1)
                    nc.vector.tensor_tensor(xT[:, bass.ds(m, 1), cols], xT[:, bass.ds(m, 1), cols], f2t[:, h:h + 1], ALU.add).then_inc(res[h], 1)

            def norm2_factor():
                for h in range(2):
                    cols = slice(h * HALF, (h + 1) * HALF)
                    dve.wait_ge(ms_done, h + 1)
                    link(nc.vector.tensor_scalar(r2[:, cols], psX[:, h], 1.0 / D, EPS, ALU.mult, ALU.add))
                    nc.vector.reciprocal(r2[:, cols], r2[:, cols]).then_inc(r2_ready, 1)
                dve.wait_ge(r2_ready, 2)

            def mlp_round(r, first=False, last=False):
                with dve.Fori(0, KT // 2) as j:
                    for u in range(2):
                        n = N5 + u
                        split_lo(n + 1 + 2 * j + 2 * KT * r, (n + 1) % 2)
                        up_evac(2 * KT * r + 4 * j + 2 * u, KT * r + 2 * j + u, 2 * j + u)
                if last:
                    return

                def down(j, peeled=False):
                    for u in range(2):
                        n = N5 + KT + u
                        split_lo(n + 1 + 2 * j + 2 * KT * r, (n + 1) % 2)
                        if first and peeled and u == 0:
                            norm2_factor()
                        down_evac(n + 2 * j + 2 * KT * r, u, 2 * j + u, 2 * KT * r + 4 * j + 2 * u)

                if first:
                    down(0, peeled=True)
                with dve.Fori(1 if first else 0, KT // 2) as j:
                    down(j)

            mlp_round(0, first=True)
            with dve.Fori(1, ROUNDS - 1) as r:
                mlp_round(r)
            mlp_round(ROUNDS - 1, last=True)

            def mean_f(t):
                dve.wait_ge(fin_ss, t + 1)
                nc.vector.tensor_scalar(msq[:, t:t + 1], ssum[:, t:t + 1], 1.0 / D, EPS, ALU.mult, ALU.add).then_inc(fin_ms, 1)

            def result(t):
                dve.wait_ge(fin_rms, t + 1)
                nc.vector.reciprocal(rstd[:, t:t + 1], rms[:, t:t + 1]).then_inc(fin_r, 1)
                dve.wait_ge(fin_r, t + 1)
                if t >= 2:
                    dve.wait_ge(st_out[t % 2], 16 * (t // 2))
                nc.vector.scalar_tensor_tensor(out=ost[:, t % 2], in0=fin_bank(t), scalar=rstd[:, t:t + 1], in1=gfb[:],
                                               op0=ALU.mult, op1=ALU.mult).then_inc(fin_o, 1)

            for i in range(HALVES):
                m, h = i % KT, i // KT
                cols = slice(h * HALF, (h + 1) * HALF)
                if i + 1 < HALVES:
                    split_lo(NL + i + 1, (NL + i + 1) % 2)
                dve.wait_ge(u_done, 2 * NL + i + 1)
                nc.vector.tensor_tensor(f2t[:, i % 2], psU[:, i % 4], r2[:, cols], ALU.mult).then_inc(mul_r2, 1)
                dve.wait_ge(mul_r2, 2 * KT * (ROUNDS - 1) + i + 1)
                nc.vector.tensor_tensor(xT[:, m, cols], xT[:, m, cols], f2t[:, i % 2], ALU.add).then_inc(res[h], 1)
                if i == FIN_STEP:
                    dve.wait_ge(gf_in, 16)
                if FIN_STEP <= i < FIN_STEP + TT // 2:
                    mean_f(i - FIN_STEP)
                    result(i - FIN_STEP)
            for t in range(TT // 2, TT):
                mean_f(t)
                if t > TT // 2:
                    result(t - 1)
            result(TT - 1)

        @block.tensor
        def _(pe):
            def three(ps, slot, k, w, hi, lo, cols, start, stop):
                nc.tensor.matmul(ps, whi[:, slot, w], hi[:, k, cols], start=start, stop=False)
                nc.tensor.matmul(ps, whi[:, slot, w], lo[:, k, cols], start=False, stop=False)
                return nc.tensor.matmul(ps, wlo[:, slot, w], hi[:, k, cols], start=False, stop=stop)

            def unit(n, slot, hi, lo, bank, before):
                pe.wait_ge(w_lo, n + 1)
                for h in range(2):
                    part(h, 0, KT, slot, hi, lo, bank, before)

            def part(h, k0, k1, slot, hi, lo, bank, before=None):
                for k in range(k0, k1):
                    if before:
                        before(h, k)
                    last = three(psU[:, bank + h], slot, k, k, hi, lo, slice(h * HALF, (h + 1) * HALF), k == 0, k == KT - 1)
                if k1 == KT:
                    last.then_inc(u_done, 1)

            pe.wait_ge(consts, 1)
            FILL = {TT - 3: (0, 2), TT - 2: (2, 4), TT - 1: (4, KT)}
            for t in range(TT):
                pe.wait_ge(xs_ready, t + 1)
                if t >= 3:
                    pe.wait_ge(h_lo, t - 2)
                for k in range(KT):
                    last = nc.tensor.transpose(turn_bank(t, k // 4)[:, (k % 4) * P:(k % 4 + 1) * P], xt[:, t, k * P:(k + 1) * P], ident[:])
                last.then_inc(xt_ready, 1)
                if t == TT - 3:
                    pe.wait_ge(const_in, 32)
                    nc.tensor.transpose(psU[:, 1, 0:KT + 4], grow[:], ident[0:KT + 4, 0:KT + 4]).then_inc(gain_t, 1)
                if t in FILL:
                    pe.wait_ge(w_lo, 1)
                    pe.wait_ge(h_lo, TT // 2)
                    part(0, *FILL[t], 0, ahi, alo, 0)

            def proj_before(n, peeled):
                def before(h, k):
                    if k == 0:
                        pe.wait_ge(h_lo, 4 * (h + 1))
                        if peeled >= 2:
                            pe.wait_ge(ev[h], n - 1)
                return before

            step = [0]
            J = CBLOCK // 2

            def bank():
                if step[0] >= 4:
                    pe.wait_ge(misc_ev, step[0] - 3)
                step[0] += 1
                return psX[:, (step[0] - 1) % 4]

            def encodings():
                pe.wait_ge(cw_in, 64)
                b = bank()
                for br in range(2):
                    last = nc.tensor.transpose(b[:, br * J:(br + 1) * J], pet[:, br], ident[0:J, 0:J])
                last.then_inc(misc, 1)

            def encodings_hidden():
                pe.wait_ge(misc_ev, 1)
                b = bank()
                for br in range(2):
                    for j in range(J):
                        last = nc.tensor.matmul(b[0:HD, br:br + 1], cw1[:, br, j], pe2[:, br, j:j + 1], start=(j == 0), stop=(j == J - 1))
                last.then_inc(misc, 1)

            def hidden(br, src, s):
                pe.wait_ge(s, 32)
                b = bank()
                for j in range(J):
                    rhs = src[:, :, 2 * j:2 * j + CSTRIDE * (NCMP - 1) + 1:CSTRIDE]
                    last = nc.tensor.matmul(b[0:HD, 0:GROUPS * NCMP], cw1[:, br, j], rhs, start=(j == 0), stop=(j == J - 1))
                last.then_inc(misc, 1)

            def compressed(br):
                pe.wait_ge(misc_ev, step[0])
                b = bank()
                if br == 0:
                    last = nc.tensor.matmul(b[:, 0:GROUPS * CP], cw2[:, 0], chid[:, 0].rearrange("p g c -> p (g c)"), start=True, stop=True)
                else:
                    for g in range(GROUPS):
                        last = nc.tensor.matmul(b[0:CP, g * HD:(g + 1) * HD], chid[:, 1, g], cw2[:, 1, 0:HD], start=True, stop=True)
                last.then_inc(misc, 1)

            def pool_product(k, h):
                if h == 0:
                    pe.wait_ge(pooled, k + 1)
                nc.tensor.matmul(bank(), wp[:, k], up[:, k, PAD + h * HALF:PAD + (h + 1) * HALF], start=True, stop=True).then_inc(misc, 1)

            def value_turn(src, s, q):
                if q == 0:
                    pe.wait_ge(s, 16)
                b = bank()
                for t in range(4):
                    last = nc.tensor.transpose(b[:, t * P:(t + 1) * P], src[:, (4 * q + t) * P:(4 * q + t + 1) * P], ident[:])
                last.then_inc(misc, 1)

            def gate_turn():
                pe.wait_ge(gate_in, 16)
                b = bank()
                for t in range(TT):
                    last = nc.tensor.transpose(b[:, t * NG:(t + 1) * NG], gtd[:, t * P:(t + 1) * P], ident[0:NG, 0:NG])
                last.then_inc(misc, 1)

            for n in range(N1):
                if n == 0:
                    pe.wait_ge(gain_ready, 1)
                    part(1, 0, KT, 0, ahi, alo, 0, proj_before(n, n))
                else:
                    unit(n, n % 2, ahi, alo, 2 * (n % 2), proj_before(n, n))
                if n == 6:
                    encodings()
                if n == 7:
                    encodings_hidden()
                if n == 8:
                    hidden(0, ldA, kc_in)
                if n == 9:
                    compressed(0)
                    hidden(1, ldB, vc_in)
                if n == 10:
                    compressed(1)
                    assert step[0] == M_CMP
                    pe.wait_ge(pool_w_in, 16)
                    for s in range(4):
                        pool_product(s // 2, s % 2)
                if n == 11:
                    for s in range(4, 8):
                        pool_product(s // 2, s % 2)
                    assert step[0] == M_POOL
                    value_turn(ldA[:, 0], vs_in, 0)
                    value_turn(ldA[:, 0], vs_in, 1)
                if n == 12:
                    gate_turn()
                    value_turn(ldA[:, 1], vw_in, 0)
                    value_turn(ldA[:, 1], vw_in, 1)
            assert step[0] == N_MISC, step[0]

            def scores(it, r):
                g, i = ITER[it]
                e = it * GR + r
                s = it % 2
                if r == 0:
                    pe.wait_ge(q_lo, it + 1)
                if e >= 1:
                    pe.wait_ge(m_slc, e)
                a, w = n_slc(i), n_win(i)
                for c in range(0, a, HALF):
                    n = min(HALF, a - c)
                    nc.tensor.matmul(psS0[:, c:c + n], qh[:, s, r], kS[:, g, c:c + n], start=True, stop=False)
                    last = nc.tensor.matmul(psS0[:, c:c + n], ql[:, s, r], kS[:, g, c:c + n], start=False, stop=True)
                last.then_inc(s_slc, 1)
                if e >= 1:
                    pe.wait_ge(m_win, e)
                for c in range(0, w, HALF):
                    n = min(HALF, w - c)
                    ks = kW[:, g, a - w + c:a - w + c + n]
                    nc.tensor.matmul(psS1[:, c:c + n], qh[:, s, r], ks, start=True, stop=False)
                    nc.tensor.matmul(psS1[:, c:c + n], ql[:, s, r], ks, start=False, stop=True)
                nc.tensor.matmul(psS1[:, w:w + CP], qh[:, s, r], kC[:, g], start=True, stop=False)
                nc.tensor.matmul(psS1[:, w:w + CP], ql[:, s, r], kC[:, g], start=False, stop=True).then_inc(s_win, 1)

            def turn(it, B, kind, kb):
                g, i = ITER[it]
                if B >= 2:
                    pe.wait_ge(pt_lo, B - 1)
                width = CP if kind == "cmp" else P
                col = prob_col(i, kind, kb)
                for r in range(GR):
                    last = nc.tensor.transpose(psX[0:width, B % 2, r * P:(r + 1) * P], PB[it % 2][:, r, col:col + width], ident[:])
                last.then_inc(t_done, 1)

            def values(it, B, kind, kb):
                g, i = ITER[it]
                first, final = B == first_block[it], B == first_block[it + 1] - 1
                if first and it >= 1:
                    pe.wait_ge(o_ready, it)
                pe.wait_ge(pt_lo, B + 1)
                v = {"slc": vS[:, kb, g], "win": vW[:, kb, g], "cmp": vC[:, g]}[kind]
                rows = CP if kind == "cmp" else P
                nc.tensor.matmul(psX[:, 2], v, pth[0:rows, B % 2], start=first, stop=False)
                nc.tensor.matmul(psX[:, 2], v, ptl[0:rows, B % 2], start=False, stop=final).then_inc(pv_done, 1)

            def gates(q, lo, hi):
                n, slot = NZ + q, (NZ + q) % 2
                for h, k in [divmod(c, KT) for c in range(lo, hi)]:
                    if h == 0 and k == 0:
                        pe.wait_ge(w_lo, n + 1)
                    if k == 0 and (q or h):
                        pe.wait_ge(z_ready, 2 * q + h)
                    last = three(psX[:, 3], slot, k, k, ahi, alo, slice(h * HALF, (h + 1) * HALF), k == 0, k == KT - 1)
                    if k == KT - 1:
                        last.then_inc(u_done, 1)

            pe.wait_ge(misc_ev, N_MISC)
            gates(0, 0, 2)
            pe.wait_ge(ev[0], N1)
            pe.wait_ge(ev[1], N1)
            pe.wait_ge(k_ready, 2)
            for r, (lo, hi) in enumerate(((2, 5), (5, 8), (8, 12), (12, 2 * KT))):
                scores(0, r)
                gates(0, lo, hi)
            for it in range(NIT):
                previous = None
                for r in range(GR):
                    if it + 1 < NIT:
                        scores(it + 1, r)
                    todo = chunk(it, r)
                    q, g0, g1 = gate_share(it, r)
                    lead = g1 - g0 if it == r == 0 or not todo else 0
                    share = [g0 + lead + (g1 - g0 - lead) * k // max(1, 2 * len(todo)) for k in range(2 * len(todo) + 1)]
                    gates(q, g0, g0 + lead)
                    if r == 0:
                        pe.wait_ge(p_ready, GR * (it + 1))
                    for k, (B, kind, kb) in enumerate(todo):
                        turn(it, B, kind, kb)
                        gates(q, share[2 * k], share[2 * k + 1])
                        if previous:
                            values(it, *previous)
                        previous = (B, kind, kb)
                        gates(q, share[2 * k + 1], share[2 * k + 2])
                values(it, *previous)
            gates(2 * KT - 1, KT + GR, 2 * KT)

            pe.wait_ge(m_slc, GR * NIT)
            pe.wait_ge(m_win, GR * NIT)

            def mixers(n, slot, m, t_slot, peeled):
                if peeled is None:
                    pe.wait_ge(xr_in[t_slot], 8 * m - 8 * t_slot + 16)
                    pe.wait_ge(xT_a, m - 1)
                    pe.wait_ge(xT_v, m - 1)
                else:
                    pe.wait_ge(xr_in[t_slot], 16)
                    if peeled == 1:
                        pe.wait_ge(z_ready, 4 * KT)
                for k in range(KT):
                    last = nc.tensor.transpose(psX[:, 2 * t_slot + k // 4, (k % 4) * P:(k % 4 + 1) * P], xr[:, t_slot, k * P:(k + 1) * P], ident[:])
                last.then_inc(xr_t, 1)
                pe.wait_ge(w_lo, n + 1)

                def pool_part(h):
                    for k in range(4):
                        three(psU[:, 2 * h + 1], slot, k, 4 + k, yhi, ylo, slice(h * HALF, (h + 1) * HALF), k == 0, k == 3)

                def attention_part(h):
                    for k in range(4):
                        if peeled == 0 and k % 2 == 0:
                            pe.wait_ge(yo_lo, 3 if k == 0 else 4 + h)
                        last = three(psU[:, 2 * h], slot, k, k, ohi, olo, slice(h * HALF, (h + 1) * HALF), k == 0, k == 3)
                    last.then_inc(u_done, 1)

                if peeled == 0:
                    for h in range(2):
                        pe.wait_ge(yo_lo, h + 1)
                        pool_part(h)
                    for h in range(2):
                        attention_part(h)
                else:
                    for h in range(2):
                        pe.wait_ge(ab_read, 2 * m + h - 1)
                        pool_part(h)
                        attention_part(h)

            for m in range(2):
                mixers(N3 + m, (N3 + m) % 2, m, m, m)
            with pe.Fori(1, KT // 2) as j:
                for u in range(2):
                    mixers(N3 + u + 2 * j, (N3 + u) % 2, 2 * j + u, u, None)

            def out_before(m, first):
                def before(h, k):
                    if k == 0 and first:
                        pe.wait_ge(ab_read, 2 * KT - 1 + m)
                    if first:
                        pe.wait_ge(c_lo, 2 * k + h + 1)
                    if k == 0 and not first:
                        pe.wait_ge(res[h], m - 1)
                return before

            for u in range(2):
                unit(N4 + u, (N4 + u) % 2, ahi, alo, 2 * u, out_before(u, True))
            with pe.Fori(1, KT // 2) as j:
                for u in range(2):
                    unit(N4 + u + 2 * j, (N4 + u) % 2, ahi, alo, 2 * u, out_before(2 * j + u, False))

            def up_before(r, t, first):
                def before(h, k):
                    if k == 0 and first:
                        pe.wait_ge(res[h], KT * r + (KT - 1) + t)
                    elif k == 0:
                        pe.wait_ge(relu[h], KT * r + t - 1)
                    if first:
                        pe.wait_ge(h2_lo, 2 * k + h + 1)
                return before

            def down_before(r, m, first):
                def before(h, k):
                    if k == 0 and first:
                        pe.wait_ge(relu[h], KT * r + (KT - 1) + m)
                    elif k == 0:
                        pe.wait_ge(res[h], KT * r + (KT - 1) + m)
                    if first:
                        pe.wait_ge(hid_lo, 2 * KT * r + 2 * k + h + 1)
                return before

            def norm2_sums():
                pe.wait_ge(sq_sum, 2 * KT)
                for h in range(2):
                    nc.tensor.matmul(psX[:, h], ones[:], sqa[:, h * HALF:(h + 1) * HALF], start=True, stop=True).then_inc(ms_done, 1)

            def mlp_round(r, first_round=False, ways=2):
                for which, before, hi, lo in ((0, up_before, h2hi, h2lo), (1, down_before, ahi, alo))[:ways]:
                    n = N5 + KT * which
                    for u in range(2):
                        unit(n + u + 2 * KT * r, (n + u) % 2, hi, lo, 2 * u, before(r, u, True))
                    if first_round and which == 0:
                        norm2_sums()
                    with pe.Fori(1, KT // 2) as j:
                        for u in range(2):
                            unit(n + u + 2 * j + 2 * KT * r, (n + u) % 2, hi, lo, 2 * u, before(r, 2 * j + u, False))

            mlp_round(0, True)
            with pe.Fori(1, ROUNDS - 1) as r:
                mlp_round(r)
            mlp_round(ROUNDS - 1, ways=1)

            def last_turn(t):
                pe.wait_ge(res[t // (TT // 2)], KT * (ROUNDS + 1))
                if 2 <= t < 6:
                    pe.wait_ge(fin_o, t - 1)
                for k in range(KT):
                    last = nc.tensor.transpose(fin_bank(t)[:, k * P:(k + 1) * P], xT[:, k, t * P:(t + 1) * P], ident[:])
                last.then_inc(fin_t, 1)

            for i in range(HALVES):
                h = i // KT
                pe.wait_ge(w_lo, NL + i + 1)
                if i < 4:
                    pe.wait_ge(relu[i % 2], KT * (ROUNDS - 1) + KT - 1 + i // 2)
                else:
                    pe.wait_ge(res[(i - 4) // KT], KT * ROUNDS + (i - 4) % KT + 1)
                for k in range(KT):
                    if i % KT == 0:
                        pe.wait_ge(hid_lo, 2 * KT * (ROUNDS - 1) + 2 * k + h + 1)
                    last = three(psU[:, i % 4], (NL + i) % 2, k, k, ahi, alo, slice(h * HALF, (h + 1) * HALF), k == 0, k == KT - 1)
                last.then_inc(u_done, 1)
                if FIN_STEP - 1 <= i < FIN_STEP - 1 + TT // 2:
                    last_turn(i - (FIN_STEP - 1))
            for t in range(TT // 2, TT):
                last_turn(t)


_INS = ['x', 'norm1_g', 'w_in', 'cmp_pe', 'cmp_w1', 'cmp_w2', 'w_attn_proj', 'w_pool', 'pool_scale',
        'w_pool_proj', 'w_out', 'norm2_g', 'w_ff1', 'w_ff2', 'final_g']
_OUTS = [((1, 1024, 1024), 'float32')]


def kernel(**inputs):
    import numpy as _np
    import concourse.bacc as _bacc
    from concourse import mybir as _mybir
    from concourse.bass_utils import run_bass_kernel_spmd as _run

    nc = _bacc.Bacc("TRN2", target_bir_lowering=False, num_devices=1, dynamic_dma_scratch_size=1024)
    arrays, args = {}, []
    for name in _INS:
        a = _np.ascontiguousarray(inputs[name])
        arrays[f"in_{name}_dram"] = a
        args.append(nc.dram_tensor(f"in_{name}_dram", a.shape, _mybir.dt.from_np(a.dtype), kind="ExternalInput").ap())
    for i, (shape, dtype) in enumerate(_OUTS):
        dt = _mybir.dt.from_np(_np.dtype(dtype))
        args.append(nc.dram_tensor(f"out_{i}_dram", shape, dt, kind="ExternalOutput").ap())
    hybrid_trunk(nc, *args)
    r = _run(nc, [arrays], core_ids=[0])
    got = tuple(r.results[0][f"out_{i}_dram"] for i in range(len(_OUTS)))
    return got[0]
```
